# Optimizing a Trainium2 kernel written in Bass

```python
import jax, jax.numpy as jnp
from jax import lax
import numpy as np

D_MODEL = 1024
BATCH = 1
SEQ = 256
DEPTH = 1

SC_WIDTH = D_MODEL // 4
SC_GROUPS = 4
SC_KERNEL = 3
SB_HEAD_DIM = 64
SB_HEADS = (D_MODEL // 4) // SB_HEAD_DIM
SB_WIDTH = SB_HEADS * SB_HEAD_DIM
SB_BLOCK = 128
SSM_INNER = D_MODEL // 2
SSM_HEAD_DIM = 64
SSM_HEADS = SSM_INNER // SSM_HEAD_DIM
SSM_GROUPS = 2
SSM_STATE = 64
SSM_CONV = 4
SSM_CHUNK = 256
SSM_CONV_DIM = SSM_INNER + 2 * SSM_GROUPS * SSM_STATE
N_BRANCH = 3
FFN_HIDDEN = -(-8 * D_MODEL // (3 * 256)) * 256
NORM_EPS = 1e-6
N_MOD = 6
PROJ_SIZES = (SC_WIDTH, SC_WIDTH, SC_WIDTH,
              SB_WIDTH, SB_WIDTH, SB_WIDTH,
              SSM_INNER, SSM_CONV_DIM, SSM_HEADS,
              D_MODEL, D_MODEL, D_MODEL)
IN_PROJ = sum(PROJ_SIZES)


def rms_norm(x, g):
    x32 = x.astype(jnp.float32)
    y = x32 * lax.rsqrt(jnp.mean(x32 * x32, axis=-1, keepdims=True) + NORM_EPS)
    return (y * g.astype(jnp.float32)).astype(x.dtype)

def causal_depthwise_conv(x, w):
    k = w.shape[0]
    return lax.conv_general_dilated(
        x, w[:, None, :].astype(x.dtype), window_strides=(1,), padding=[(k - 1, 0)],
        dimension_numbers=("NWC", "WIO", "NWC"), feature_group_count=x.shape[-1])

def split_columns(p):
    offsets = [int(o) for o in np.cumsum(PROJ_SIZES)[:-1]]
    return jnp.split(p, offsets, axis=-1)

def short_conv_mixer(b_gate, c_gate, xa, w_conv):
    return b_gate * causal_depthwise_conv(c_gate * xa, w_conv)

def stick_breaking_attention(q, k, v):
    bsz, seq, heads, dh = q.shape
    n_blk = seq // SB_BLOCK
    scale = dh ** -0.5
    qh = q.transpose(0, 2, 1, 3)
    kh = k.transpose(0, 2, 1, 3)
    vh = v.transpose(0, 2, 1, 3)
    strict = jnp.tril(jnp.ones((SB_BLOCK, SB_BLOCK), jnp.float32), -1)
    outs = []
    for i in range(n_blk):
        start, end = i * SB_BLOCK, (i + 1) * SB_BLOCK
        z = jnp.einsum("bhqd,bhkd->bhqk", qh[:, :, start:end], kh[:, :, :end],
                       preferred_element_type=jnp.float32) * scale
        mask = jnp.arange(end)[None, :] < (start + jnp.arange(SB_BLOCK))[:, None]
        log_keep = jnp.where(mask, jax.nn.log_sigmoid(-z), 0.0)
        lk = log_keep.reshape(bsz, heads, SB_BLOCK, i + 1, SB_BLOCK)
        within = jnp.einsum("bhqcj,js->bhqcs", lk, strict)
        blk_tot = jnp.sum(lk, axis=-1)
        later = lax.cumsum(blk_tot, axis=3, reverse=True) - blk_tot
        log_rest = (within + later[..., None]).reshape(bsz, heads, SB_BLOCK, end)
        att = jnp.exp(jnp.where(mask, z + log_keep + log_rest, -jnp.inf))
        outs.append(jnp.einsum("bhqk,bhkd->bhqd", att.astype(vh.dtype), vh[:, :, :end]))
    out = jnp.concatenate(outs, axis=2)
    return out.transpose(0, 2, 1, 3).reshape(bsz, seq, heads * dh)

def segsum_exp(a_cs):
    l = a_cs.shape[-1]
    mask = jnp.tril(jnp.ones((l, l), dtype=bool))
    diff = a_cs[..., :, None] - a_cs[..., None, :]
    return jnp.exp(jnp.where(mask, diff, -jnp.inf))

def ssd_scan(xh, dt, a_neg, bm, cm):
    bsz, seq, heads, hd = xh.shape
    reps = heads // bm.shape[2]
    bh = jnp.repeat(bm, reps, axis=2)
    ch = jnp.repeat(cm, reps, axis=2)
    xdt = xh * dt[..., None]
    a = dt * a_neg
    pad = (-seq) % SSM_CHUNK
    if pad:
        pw = ((0, 0), (0, pad), (0, 0), (0, 0))
        xdt, bh, ch = jnp.pad(xdt, pw), jnp.pad(bh, pw), jnp.pad(ch, pw)
        a = jnp.pad(a, ((0, 0), (0, pad), (0, 0)))
    n_c = (seq + pad) // SSM_CHUNK
    xc = xdt.reshape(bsz, n_c, SSM_CHUNK, heads, hd)
    bc = bh.reshape(bsz, n_c, SSM_CHUNK, heads, -1)
    cc = ch.reshape(bsz, n_c, SSM_CHUNK, heads, -1)
    a_cs = jnp.cumsum(a.reshape(bsz, n_c, SSM_CHUNK, heads), axis=2)
    decay_in = segsum_exp(a_cs.transpose(0, 1, 3, 2))
    scores = jnp.einsum("bclhn,bcshn->bchls", cc, bc) * decay_in
    y_diag = jnp.einsum("bchls,bcshp->bclhp", scores, xc)
    decay_to_end = jnp.exp(a_cs[:, :, -1:, :] - a_cs)
    chunk_states = jnp.einsum("bclhn,bclhp->bchpn", bc * decay_to_end[..., None], xc)
    chunk_decay = jnp.exp(a_cs[:, :, -1, :])

    def step(state, inp):
        s_c, d_c = inp
        return state * d_c[..., None, None] + s_c, state

    init = jnp.zeros((bsz, heads, hd, bc.shape[-1]), jnp.float32)
    _, prev = lax.scan(step, init, (chunk_states.transpose(1, 0, 2, 3, 4),
                                    chunk_decay.transpose(1, 0, 2)))
    prev = prev.transpose(1, 0, 2, 3, 4)
    y_off = jnp.einsum("bclhn,bchpn->bclhp", cc, prev) * jnp.exp(a_cs)[..., None]
    return (y_diag + y_off).reshape(bsz, seq + pad, heads, hd)[:, :seq]

def mamba2_mixer(z, xbc, dt_raw, conv_w, conv_b, dt_bias, a_log, d_skip, norm_w):
    xbc = jax.nn.silu(causal_depthwise_conv(xbc, conv_w) + conv_b)
    xs, bm, cm = jnp.split(xbc, [SSM_INNER, SSM_INNER + SSM_GROUPS * SSM_STATE], axis=-1)
    bsz, seq, _ = xs.shape
    xh = xs.reshape(bsz, seq, SSM_HEADS, SSM_HEAD_DIM).astype(jnp.float32)
    bm = bm.reshape(bsz, seq, SSM_GROUPS, SSM_STATE).astype(jnp.float32)
    cm = cm.reshape(bsz, seq, SSM_GROUPS, SSM_STATE).astype(jnp.float32)
    dt = jax.nn.softplus(dt_raw.astype(jnp.float32) + dt_bias.astype(jnp.float32))
    a_neg = -jnp.exp(a_log.astype(jnp.float32))
    y = ssd_scan(xh, dt, a_neg, bm, cm) + xh * d_skip.astype(jnp.float32)[:, None]
    y = y.reshape(bsz, seq, SSM_INNER) * jax.nn.silu(z.astype(jnp.float32))
    yg = y.reshape(bsz, seq, SSM_GROUPS, SSM_INNER // SSM_GROUPS)
    yg = yg * lax.rsqrt(jnp.mean(yg * yg, axis=-1, keepdims=True) + NORM_EPS)
    return (yg.reshape(bsz, seq, SSM_INNER) * norm_w.astype(jnp.float32)).astype(z.dtype)

def hybrid_layer(x, c, mod_w, mod_b, g_pre_mix, g_post_mix, g_pre_ffn, g_post_ffn,
                 w_in, sc_conv_w, ssm_conv_w, ssm_conv_b, ssm_dt_bias, ssm_a_log, ssm_d,
                 ssm_norm_w, w_sc_out, w_sb_out, w_ssm_out, w_o, w_ffn_in, w_ffn_out):
    bsz, seq, _ = x.shape
    mod = jax.nn.silu(c) @ mod_w + mod_b
    shift1, scale1, gate1, shift2, scale2, gate2 = [m[:, None, :] for m in jnp.split(mod, N_MOD, axis=-1)]

    h = rms_norm(x, g_pre_mix) * (1 + scale1) + shift1
    (sc_b, sc_c, sc_x, q, k, v, z, xbc, dt_raw,
     gl_a, gl_b, gl_c) = split_columns(h @ w_in)
    y_a = short_conv_mixer(sc_b, sc_c, sc_x, sc_conv_w) @ w_sc_out
    y_b = stick_breaking_attention(
        q.reshape(bsz, seq, SB_HEADS, SB_HEAD_DIM),
        k.reshape(bsz, seq, SB_HEADS, SB_HEAD_DIM),
        v.reshape(bsz, seq, SB_HEADS, SB_HEAD_DIM)) @ w_sb_out
    y_c = mamba2_mixer(z, xbc, dt_raw, ssm_conv_w, ssm_conv_b, ssm_dt_bias, ssm_a_log,
                       ssm_d, ssm_norm_w) @ w_ssm_out
    merged = (jax.nn.sigmoid(gl_a) * y_a + jax.nn.sigmoid(gl_b) * y_b
              + jax.nn.sigmoid(gl_c) * y_c)
    mix_out = merged @ w_o
    x = x + (gate1 * rms_norm(mix_out, g_post_mix)).astype(x.dtype)

    h2 = rms_norm(x, g_pre_ffn) * (1 + scale2) + shift2
    gt, up = jnp.split(h2 @ w_ffn_in, 2, axis=-1)
    f = (jax.nn.silu(gt) * up) @ w_ffn_out
    x = x + (gate2 * rms_norm(f, g_post_ffn)).astype(x.dtype)
    return x

def first_inputs(seed: int = 0) -> dict:
    key = jax.random.key(seed)
    ks = jax.random.split(key, 24)
    f32 = jnp.float32

    def nrm(k, shape, fan_in):
        return jax.random.normal(k, shape, f32) * (fan_in ** -0.5)

    def gain(k, shape):
        return 1.0 + 0.05 * jax.random.normal(k, shape, f32)

    dt0 = jnp.exp(jax.random.uniform(ks[14], (DEPTH, SSM_HEADS), f32,
                                     jnp.log(1e-3), jnp.log(1e-1)))
    return {
        "x": jax.random.normal(ks[0], (BATCH, SEQ, D_MODEL), f32),
        "c": jax.random.normal(ks[1], (BATCH, D_MODEL), f32),
        "mod_w": nrm(ks[2], (DEPTH, D_MODEL, N_MOD * D_MODEL), D_MODEL),
        "mod_b": 0.02 * jax.random.normal(ks[3], (DEPTH, N_MOD * D_MODEL), f32),
        "g_pre_mix": gain(ks[4], (DEPTH, D_MODEL)),
        "g_post_mix": gain(ks[5], (DEPTH, D_MODEL)),
        "g_pre_ffn": gain(ks[6], (DEPTH, D_MODEL)),
        "g_post_ffn": gain(ks[7], (DEPTH, D_MODEL)),
        "w_in": nrm(ks[8], (DEPTH, D_MODEL, IN_PROJ), D_MODEL),
        "sc_conv_w": nrm(ks[9], (DEPTH, SC_KERNEL, SC_WIDTH), SC_KERNEL),
        "ssm_conv_w": nrm(ks[10], (DEPTH, SSM_CONV, SSM_CONV_DIM), SSM_CONV),
        "ssm_conv_b": 0.02 * jax.random.normal(ks[11], (DEPTH, SSM_CONV_DIM), f32),
        "ssm_dt_bias": dt0 + jnp.log(-jnp.expm1(-dt0)),
        "ssm_a_log": jnp.log(jax.random.uniform(ks[12], (DEPTH, SSM_HEADS), f32, 1.0, 16.0)),
        "ssm_d": 1.0 + 0.1 * jax.random.normal(ks[13], (DEPTH, SSM_HEADS), f32),
        "ssm_norm_w": gain(ks[15], (DEPTH, SSM_INNER)),
        "w_sc_out": nrm(ks[16], (DEPTH, SC_WIDTH, D_MODEL), SC_WIDTH),
        "w_sb_out": nrm(ks[17], (DEPTH, SB_WIDTH, D_MODEL), SB_WIDTH),
        "w_ssm_out": nrm(ks[18], (DEPTH, SSM_INNER, D_MODEL), SSM_INNER),
        "w_o": nrm(ks[19], (DEPTH, D_MODEL, D_MODEL), D_MODEL),
        "w_ffn_in": nrm(ks[20], (DEPTH, D_MODEL, 2 * FFN_HIDDEN), D_MODEL),
        "w_ffn_out": nrm(ks[21], (DEPTH, FFN_HIDDEN, D_MODEL), FFN_HIDDEN),
    }

def first_block(x, c, mod_w, mod_b, g_pre_mix, g_post_mix, g_pre_ffn, g_post_ffn, w_in,
              sc_conv_w, ssm_conv_w, ssm_conv_b, ssm_dt_bias, ssm_a_log, ssm_d, ssm_norm_w,
              w_sc_out, w_sb_out, w_ssm_out, w_o, w_ffn_in, w_ffn_out):
    for l in range(DEPTH):
        x = hybrid_layer(x, c, mod_w[l], mod_b[l], g_pre_mix[l], g_post_mix[l],
                         g_pre_ffn[l], g_post_ffn[l], w_in[l], sc_conv_w[l], ssm_conv_w[l],
                         ssm_conv_b[l], ssm_dt_bias[l], ssm_a_log[l], ssm_d[l], ssm_norm_w[l],
                         w_sc_out[l], w_sb_out[l], w_ssm_out[l], w_o[l], w_ffn_in[l],
                         w_ffn_out[l])
    return x


MIX_WIDTH = D_MODEL
ATTN_WIDTH = MIX_WIDTH // 2
POOL_WIDTH = MIX_WIDTH - ATTN_WIDTH
N_HEADS = 8
HEAD_DIM = ATTN_WIDTH // N_HEADS
DILATED_BRANCHES = ((128, 1), (512, 4), (2048, 16))
MAX_SPAN = 2048
Q_BLOCK = 128
POOL_WINDOWS = (2, 4, 8, 16)
POOL_GROUP = POOL_WIDTH // len(POOL_WINDOWS)
PEER_HEADS = 8
PEER_NKEYS = 128
PEER_EXPERTS = PEER_NKEYS * PEER_NKEYS
PEER_QDIM = 256
PEER_TOPK = 16
TOKEN_CHUNK = 128
EPS = 1e-6


def rmsnorm(x, g):
    xf = x.astype(jnp.float32)
    y = xf * lax.rsqrt(jnp.mean(xf * xf, axis=-1, keepdims=True) + EPS)
    return (y * g.astype(jnp.float32)).astype(x.dtype)

def alibi_slopes(n):
    return jnp.asarray([2.0 ** (-8.0 * (h + 1) / n) for h in range(n)], dtype=jnp.float32)

def dilated_attention(q, k, v):
    B, S, H, hd = q.shape
    nblk = S // Q_BLOCK
    pad = ((0, 0), (MAX_SPAN, 0), (0, 0), (0, 0))
    k_pad = jnp.pad(k, pad)
    v_pad = jnp.pad(v, pad)
    slopes = alibi_slopes(H)
    scale = HEAD_DIM ** -0.5
    qi = jnp.arange(Q_BLOCK)
    branches = []
    for w, d in DILATED_BRANCHES:
        j = jnp.arange(w // d + 1)
        gidx = qi[:, None] + MAX_SPAN - j[None, :] * d
        dist = j * d
        branches.append((gidx, dist))

    def block(idx):
        b = idx // nblk
        start = (idx % nblk) * Q_BLOCK
        qb = lax.dynamic_slice(q, (b, start, 0, 0), (1, Q_BLOCK, H, hd))[0].astype(jnp.float32) * scale
        ks = lax.dynamic_slice(k_pad, (b, start, 0, 0), (1, MAX_SPAN + Q_BLOCK, H, hd))[0]
        vs = lax.dynamic_slice(v_pad, (b, start, 0, 0), (1, MAX_SPAN + Q_BLOCK, H, hd))[0]
        pos = start + qi
        lses, outs = [], []
        for gidx, dist in branches:
            kg = jnp.take(ks, gidx, axis=0).astype(jnp.float32)
            vg = jnp.take(vs, gidx, axis=0).astype(jnp.float32)
            distf = dist.astype(jnp.float32)
            s = jnp.einsum('qhd,qjhd->hqj', qb, kg) - slopes[:, None, None] * distf[None, None, :]
            valid = (pos[:, None] - dist[None, :]) >= 0
            s = jnp.where(valid[None], s, -1e30)
            m = jnp.max(s, axis=-1, keepdims=True)
            p = jnp.exp(s - m)
            z = jnp.sum(p, axis=-1, keepdims=True)
            o = jnp.einsum('hqj,qjhd->qhd', p, vg) / jnp.transpose(z, (1, 0, 2))
            lses.append(jnp.transpose((m + jnp.log(z))[..., 0], (1, 0)))
            outs.append(o)
        wts = jax.nn.softmax(jnp.stack(lses, axis=0), axis=0)
        out = jnp.einsum('gqh,gqhd->qhd', wts, jnp.stack(outs, axis=0))
        return out.astype(q.dtype)

    out = lax.map(block, jnp.arange(B * nblk))
    return out.reshape(B, S, H, hd)

def multiscale_pool(u, w_pool, pool_scale):
    B, S, C = u.shape
    uf = u.astype(jnp.float32)
    cs = jnp.pad(jnp.cumsum(uf, axis=1), ((0, 0), (1, 0), (0, 0)))
    pos1 = jnp.arange(1, S + 1, dtype=jnp.float32)
    outs = []
    for g, w in enumerate(POOL_WINDOWS):
        sl = slice(g * POOL_GROUP, (g + 1) * POOL_GROUP)
        cg = cs[:, :, sl]
        upper = cg[:, 1:]
        lower = jnp.pad(cg, ((0, 0), (w - 1, 0), (0, 0)))[:, :S]
        cnt = jnp.minimum(pos1, float(w))[None, :, None]
        mixed = (upper - lower) / cnt - uf[:, :, sl]
        outs.append(jnp.einsum('bsc,ce->bse', mixed, w_pool[g].astype(jnp.float32)))
    y = jnp.concatenate(outs, axis=-1) * pool_scale.astype(jnp.float32)
    return y.astype(u.dtype)

def peer_ffn(h, w_q, sub_keys, expert_u, expert_v):
    B, S, D = h.shape
    T = B * S
    half = PEER_QDIM // 2
    K = PEER_TOPK
    hc = h.reshape(T // TOKEN_CHUNK, TOKEN_CHUNK, D)

    def chunk(xc):
        C = xc.shape[0]
        q = jnp.einsum('cd,de->ce', xc, w_q).astype(jnp.float32).reshape(C, PEER_HEADS, 2, half)
        s = jnp.einsum('chpk,pnk->chpn', q, sub_keys.astype(jnp.float32))
        sv, si = lax.top_k(s, K)
        cand = sv[:, :, 0, :, None] + sv[:, :, 1, None, :]
        cand_id = si[:, :, 0, :, None] * PEER_NKEYS + si[:, :, 1, None, :]
        cand = cand.reshape(C, PEER_HEADS, K * K)
        cand_id = cand_id.reshape(C, PEER_HEADS, K * K)
        top_v, top_pos = lax.top_k(cand, K)
        eid = jnp.take_along_axis(cand_id, top_pos, axis=-1)
        gate = jax.nn.softmax(top_v, axis=-1)
        u = expert_u[eid]
        act = jax.nn.gelu(jnp.einsum('cd,chkd->chk', xc, u).astype(jnp.float32), approximate=False)
        vv = expert_v[eid]
        y = jnp.einsum('chk,chkd->cd', (gate * act).astype(vv.dtype), vv)
        return y.astype(xc.dtype)

    return lax.map(chunk, hc).reshape(B, S, D)

def second_inputs(seed: int = 0) -> dict:
    key = jax.random.key(seed)
    ks = jax.random.split(key, 16)
    D = D_MODEL
    proj_out = 3 * ATTN_WIDTH + POOL_WIDTH
    f32 = jnp.float32
    x = jax.random.normal(ks[0], (BATCH, SEQ, D), f32)
    c = jax.random.normal(ks[1], (BATCH, D), f32)
    w_ada = jax.random.normal(ks[2], (DEPTH, D, N_MOD * D), f32) * (0.5 * D ** -0.5)
    b_ada = jax.random.normal(ks[3], (DEPTH, N_MOD * D), f32) * 0.01
    norm1_g = 1.0 + 0.05 * jax.random.normal(ks[4], (DEPTH, D), f32)
    w_in = jax.random.normal(ks[5], (DEPTH, D, proj_out), f32) * D ** -0.5
    pool_w = jax.random.normal(ks[6], (DEPTH, len(POOL_WINDOWS), POOL_GROUP, POOL_GROUP), f32) * POOL_GROUP ** -0.5
    pool_scale = 1.0 + 0.1 * jax.random.normal(ks[7], (DEPTH, POOL_WIDTH), f32)
    w_out = jax.random.normal(ks[8], (DEPTH, MIX_WIDTH, D), f32) * MIX_WIDTH ** -0.5
    norm2_g = 1.0 + 0.05 * jax.random.normal(ks[9], (DEPTH, D), f32)
    peer_wq = jax.random.normal(ks[10], (DEPTH, D, PEER_HEADS * PEER_QDIM), f32) * D ** -0.5
    peer_subkeys = jax.random.normal(ks[11], (DEPTH, 2, PEER_NKEYS, PEER_QDIM // 2), f32) * (PEER_QDIM // 2) ** -0.5
    peer_u = jax.random.normal(ks[12], (DEPTH, PEER_EXPERTS, D), f32) * D ** -0.5
    peer_v = jax.random.normal(ks[13], (DEPTH, PEER_EXPERTS, D), f32) * 0.5
    final_g = 1.0 + 0.05 * jax.random.normal(ks[14], (D,), f32)
    return {"x": x, "c": c, "w_ada": w_ada, "b_ada": b_ada, "norm1_g": norm1_g,
            "w_in": w_in, "pool_w": pool_w, "pool_scale": pool_scale, "w_out": w_out,
            "norm2_g": norm2_g, "peer_wq": peer_wq, "peer_subkeys": peer_subkeys,
            "peer_u": peer_u, "peer_v": peer_v, "final_g": final_g}

def second_block(x, c, w_ada, b_ada, norm1_g, w_in, pool_w, pool_scale, w_out,
              norm2_g, peer_wq, peer_subkeys, peer_u, peer_v, final_g):
    B, S, D = x.shape
    A = ATTN_WIDTH
    for l in range(DEPTH):
        mod = jnp.einsum('bd,de->be', jax.nn.silu(c), w_ada[l]) + b_ada[l]
        sh1, sc1, g1, sh2, sc2, g2 = jnp.split(mod[:, None, :], N_MOD, axis=-1)
        h = rmsnorm(x, norm1_g[l]) * (1.0 + sc1) + sh1
        proj = jnp.einsum('bsd,de->bse', h, w_in[l])
        q, k, v, u = jnp.split(proj, [A, 2 * A, 3 * A], axis=-1)
        attn = dilated_attention(q.reshape(B, S, N_HEADS, HEAD_DIM),
                                 k.reshape(B, S, N_HEADS, HEAD_DIM),
                                 v.reshape(B, S, N_HEADS, HEAD_DIM)).reshape(B, S, A)
        pool = multiscale_pool(u, pool_w[l], pool_scale[l])
        mixed = jnp.einsum('bse,ed->bsd', jnp.concatenate([attn, pool], axis=-1), w_out[l])
        x = x + g1 * mixed
        h2 = rmsnorm(x, norm2_g[l]) * (1.0 + sc2) + sh2
        x = x + g2 * peer_ffn(h2, peer_wq[l], peer_subkeys[l], peer_u[l], peer_v[l])
    return rmsnorm(x, final_g)


def setup_inputs(seed=0):
    out = dict(first_inputs(seed))
    for name, value in second_inputs(seed + 1).items():
        if name != "x":
            out[name + "_2"] = value
    return out


def reference(
    x, c, mod_w, mod_b, g_pre_mix, g_post_mix, g_pre_ffn, g_post_ffn, w_in, sc_conv_w,
    ssm_conv_w, ssm_conv_b, ssm_dt_bias, ssm_a_log, ssm_d, ssm_norm_w, w_sc_out, w_sb_out,
    w_ssm_out, w_o, w_ffn_in, w_ffn_out, c_2, w_ada_2, b_ada_2, norm1_g_2, w_in_2, pool_w_2,
    pool_scale_2, w_out_2, norm2_g_2, peer_wq_2, peer_subkeys_2, peer_u_2, peer_v_2, final_g_2,
):
    x = first_block(
        x, c, mod_w, mod_b, g_pre_mix, g_post_mix, g_pre_ffn, g_post_ffn, w_in, sc_conv_w,
        ssm_conv_w, ssm_conv_b, ssm_dt_bias, ssm_a_log, ssm_d, ssm_norm_w, w_sc_out, w_sb_out,
        w_ssm_out, w_o, w_ffn_in, w_ffn_out,
    )
    return second_block(
        x, c_2, w_ada_2, b_ada_2, norm1_g_2, w_in_2, pool_w_2, pool_scale_2, w_out_2, norm2_g_2,
        peer_wq_2, peer_subkeys_2, peer_u_2, peer_v_2, final_g_2,
    )


_drawn_inputs = setup_inputs


def setup_inputs(seed=0):
    import zlib

    import numpy as np

    out = dict(_drawn_inputs(seed))
    spreads = {}
    factors = {'ssm_conv_b': 8.0,
     'ssm_d': 6.394,
     'ssm_norm_w': 4.662,
     'b_ada_2': 5.412,
     'norm1_g_2': 5.341,
     'pool_scale_2': 3.599,
     'norm2_g_2': 3.697}
    for name, (base, spread) in spreads.items():
        noise = np.random.default_rng([zlib.crc32(name.encode()), seed]).standard_normal(out[name].shape)
        drawn = base * np.exp(spread * noise) if base else spread * noise
        out[name] = __import__('jax').numpy.asarray(drawn.astype(out[name].dtype))
    for name, factor in factors.items():
        out[name] = (out[name] * factor).astype(out[name].dtype)
    return out
```

```python
from contextlib import ExitStack

import numpy as np

import concourse.bass as bass
from concourse import mybir

ALU = mybir.AluOpType
ACT = mybir.ActivationFunctionType
F32 = mybir.dt.float32
U32 = mybir.dt.uint32
X = mybir.AxisListType.X

P = 128
D = 1024
T = 256
NT = T // P
KC = D // P
UNIT = 2048
RING = 5
FB = 22
PAIRS = FB // 2
HEADS = 8
TOPK = 16
SLOTS = HEADS * TOPK
ROWS = 16
GROUPS = NT * SLOTS // ROWS
EPS = 1e-6
NEG = -1e30

ORDER = [("mv", m) for m in range(8)]
ORDER += [("xbc", j) for j in range(3)] + [("sc", j) for j in range(3)] + [("qk", 0), ("qk", 1), ("v", 0)]
ORDER += [("z", 0), ("z", 1)]
for _j in range(12):
    ORDER += [("gl", _j), ("mv", 8 + _j)]
ORDER += [("sco", 0), ("sbo", 0), ("sso", 0), ("sso", 1)] + [("wo", j) for j in range(4)]
FFN0 = len(ORDER)
ORDER += [("gu", 0), ("gu", 1), ("mv", 20), ("mv", 21)]
for _i in range(1, PAIRS):
    ORDER += [("gu", 2 * _i), ("dn", _i - 1), ("gu", 2 * _i + 1), ("mv", 20 + 2 * _i), ("mv", 21 + 2 * _i)]
ORDER += [("dn", PAIRS - 1)]
for _j in range(4):
    ORDER += [("qk2", _j), ("mv", 42 + _j)]
ORDER += [("v2", 0), ("v2", 1), ("mv", 46), ("u2", 0), ("u2", 1), ("mv", 47)]
ORDER += [("wo2", j) for j in range(4)] + [("wq", j) for j in range(8)]
AT = {name: n for n, name in enumerate(ORDER)}
UNITS = len(ORDER)


MOD_READS = [8, 20, 42, 48]


def DONE(kind, j):
    return AT[kind, j] + 1


SMALL = {}
_at = 0
for _name, _n in (("c", 8), ("c2", 8), ("mod_b", 96), ("g_pre_mix", 8), ("g_pre_ffn", 8), ("g_post_mix", 8),
                  ("g_post_ffn", 8), ("norm1", 8), ("norm2", 8), ("ssm_b", 6), ("ssm_w", 24), ("sc_w", 6),
                  ("ssm_norm", 4), ("pool_scale", 4), ("ssm_d", 4), ("dt_b", 8), ("a_log", 8), ("w_dt", 64),
                  ("pool_w", 512), ("keys", 256), ("ident", P), ("tri", P), ("ones", P), ("suffix", P),
                  ("sb_keep", 384), ("sb_bias", 384), ("ssm_bias", 384), ("dist", 384), ("count", 384),
                  ("iota", TOPK)):
    SMALL[_name] = (_at, _at + _n)
    _at += _n
SMALL_N = _at


def build(nc, stream, small, x, band, final_g, expert_u, expert_v, out):
    with ExitStack() as ctx:
        def sb(name, n, dt=F32):
            return ctx.enter_context(nc.sbuf_tensor(name, [P, n], dt))

        def sem(name):
            return ctx.enter_context(nc.semaphore(name))

        def cut(t, at, *dims):
            n = int(np.prod(dims))
            v = t[:, at:at + n]
            if len(dims) == 2:
                return v.rearrange("p (a b) -> p a b", a=dims[0])
            if len(dims) == 3:
                return v.rearrange("p (a b c) -> p a b c", a=dims[0], b=dims[1])
            return v

        ring = sb("ring", ROWS * D)
        areaA = sb("areaA", 8214)
        areaB = sb("areaB", 9728)
        sm = sb("small", SMALL_N)
        x_sb = sb("x_sb", NT * D)[:, :].rearrange("p (t d) -> p t d", t=NT)
        xn = sb("xn", NT * D)[:, :].rearrange("p (t d) -> p t d", t=NT)
        hT = sb("hT", KC * T)[:, :].rearrange("p (k t) -> p k t", k=KC)
        mT_flat = sb("mT", KC * T)
        mT = mT_flat[:, :].rearrange("p (k t) -> p k t", k=KC)
        diag = sb("diag", D)
        gate_row = sb("gate_row", D)
        scale_row = sb("scale_row", D)
        shift_row = sb("shift_row", D)
        modT = sb("modT", 96)
        cols = sb("cols", 64)
        stat = sb("stat", 64)
        dtb = sb("dtb", 192)

        ps = ctx.enter_context(nc.psum_tensor("ps", [P, 8, 512], F32))
        BM, BX = 2, 7
        B3 = 3

        def c_(name, a=0, b=None):
            lo, hi = SMALL[name]
            return sm[:, lo + a:(hi if b is None else lo + b)]

        slot = [cut(ring, s * UNIT, UNIT) for s in range(RING)]
        gates = cut(ring, RING * UNIT, 24, T)
        row = [cut(ring, r * D, D) for r in range(ROWS)]

        xbc_raw = cut(areaA, 0, 6, T + 3)
        xbc = cut(areaA, 1554, 6, T)
        sc = cut(areaA, 3090, 6, T)
        cx = cut(areaA, 4626, 2, T + 2)
        ya = cut(areaA, 5142, 2, T)
        qk = cut(areaA, 5654, 4, T)
        v1 = cut(areaA, 6678, NT, T)
        zg = cut(areaA, 7190, 4, T)
        sbl = cut(areaB, 0, 4, 384)
        sba = cut(areaB, 1536, 4, 384)
        decay = cut(areaB, 3072, 8, 384)
        a_rep = cut(areaB, 6144, 16, P)
        x_tok = cut(areaB, 8192, NT, 512)
        yb = cut(areaB, 9216, 2, T)
        yc = cut(areaB, 0, 4, T)
        ysq = cut(areaB, 1536, 4, T)
        prod = [cut(areaB, 3072 + 512 * n, 2, T) for n in range(6)]
        sg = cut(areaB, 0, 2, T)
        hid = cut(areaB, 512, 2, T)
        qk2 = cut(areaA, 0, 8, T)
        v2 = cut(areaA, 2048, NT, 512)
        u2 = cut(areaA, 3072, NT, 512)
        band_sb = cut(areaA, 4096, NT, 4, T)
        pooled = cut(areaA, 6144, 4, T)
        pexp = cut(areaB, 0, 4, 384)
        pnrm = cut(areaB, 1536, 4, 384)
        pT = cut(areaB, 3072, 4, 384)
        score = cut(areaA, 0, NT, 16, P)
        rest = cut(areaA, 4096, 16, P)
        qh = cut(areaA, 6144, 2, 512)
        y_acc = [cut(areaA, 6144, D), cut(areaA, 7168, D)]
        y_alt = [cut(areaA, 0, D), cut(areaA, 1024, D)]
        cand = cut(areaB, 0, HEADS, 256)
        cand_rest = cut(areaB, 2048, HEADS, 256)
        onehot = cut(areaB, 4096, SLOTS, TOPK)
        final_row = cut(areaB, 6144, D)
        sv = cut(mT_flat, 0, 16, TOPK)
        si = cut(mT_flat, 256, 16, TOPK).bitcast(U32)
        sif = cut(mT_flat, 512, 16, TOPK)
        tv = cut(mT_flat, 768, HEADS, TOPK)
        ti = cut(mT_flat, 896, SLOTS).bitcast(U32)
        tr = cut(mT_flat, 1024, SLOTS).bitcast(U32)
        pos_f = [cut(mT_flat, 1152, SLOTS), cut(mT_flat, 1280, SLOTS)]
        pick = [cut(mT_flat, 1408, SLOTS), cut(mT_flat, 1536, SLOTS)]
        idx = sb("idx", NT * SLOTS, U32)
        idx_now = sb("idx_now", ROWS, U32)
        gate = sb("gate", NT * SLOTS)
        dots = sb("dots", NT * SLOTS)
        now = sb("now", ROWS)

        small_in, x_in, band_in, final_in = sem("small_in"), sem("x_in"), sem("band_in"), sem("final_in")
        w_in = [sem(f"w_in{s}") for s in range(RING)]
        unit_done = sem("unit_done")
        dve_step, act_step = sem("dve_step"), sem("act_step")
        c_silu = sem("c_silu")
        sq_sum, mean_sq, root = sem("sq_sum"), sem("mean_sq"), sem("root")
        xn_ready, x_T, col_ready, hT_act, hT_dve = (sem("xn_ready"), sem("x_T"), sem("col_ready"), sem("hT_act"),
                                                    sem("hT_dve"))
        evac = sem("evac")
        diag_ready, row_mm, row_ready = sem("diag_ready"), sem("row_mm"), sem("row_ready")
        dt_mm, dt_lin, dt_exp, dt_one, dt_log, a_exp, a_ready = (
            sem("dt_mm"), sem("dt_lin"), sem("dt_exp"), sem("dt_one"), sem("dt_log"), sem("a_exp"), sem("a_ready"))
        conv_done, xbc_ready = sem("conv_done"), sem("xbc_ready")
        sb_z, sb_log, sb_lk, sb_sum, sb_arg, sb_att, sb_out, sb_y = (
            sem("sb_z"), sem("sb_log"), sem("sb_lk"), sem("sb_sum"), sem("sb_arg"), sem("sb_att"), sem("sb_out"),
            sem("sb_y"))
        acs_mm, dec_arg, dec_exp, xs_T, x_tok_ready, bc_mm, w_ready, y_mm = (
            sem("acs_mm"), sem("dec_arg"), sem("dec_exp"), sem("xs_T"), sem("x_tok_ready"), sem("bc_mm"),
            sem("w_ready"), sem("y_mm"))
        ysq_ready, ysum_mm, yms, yroot, yc_ready, ya_ready = (
            sem("ysq_ready"), sem("ysum_mm"), sem("yms"), sem("yroot"), sem("yc_ready"), sem("ya_ready"))
        br_mm, merged = sem("br_mm"), sem("merged")
        res_done = sem("res_done")
        silu_done, hid_ready = sem("silu_done"), sem("hid_ready")
        at_s, at_max, at_exp, at_p, at_T, at_pT, at_pv, at_o = (
            sem("at_s"), sem("at_max"), sem("at_exp"), sem("at_p"), sem("at_T"), sem("at_pT"), sem("at_pv"),
            sem("at_o"))
        at_read = sem("at_read")
        pool_mm, pool_ev, pool_out, pool_y = sem("pool_mm"), sem("pool_ev"), sem("pool_out"), sem("pool_y")
        s_mm, s_ready = sem("s_mm"), sem("s_ready")
        top_v, top_exp, idx_ready = sem("top_v"), sem("top_exp"), sem("idx_ready")
        row_in = [sem(f"row_in{r}") for r in range(ROWS)]
        row_used, idx_copied, pool_go, dots_out, gelu_done, w8_ready = (
            sem("row_used"), sem("idx_copied"), sem("pool_go"), sem("dots_out"), sem("gelu_done"), sem("w8_ready"))
        gate_ready = sem("gate_ready")
        out_ready, out_done = sem("out_ready"), sem("out_done")

        mod_read = sem("mod_read")
        acs_col_mm, acs_read = sem("acs_col_mm"), sem("acs_read")

        class Steps:

            def __init__(self, eng, s):
                self.eng, self.s, self.n = eng, s, 0

            def __call__(self, ins):
                ins.then_inc(self.s, 1)
                self.n += 1

            def wait(self, back=0):
                self.eng.wait_ge(self.s, self.n - back)

        block = ctx.enter_context(nc.Block())

        @block.sync
        def _(sp):
            sp.dma_start(sm[:, :], small).then_inc(small_in, 16)
            sp.dma_start(x_sb, x).then_inc(x_in, 16)
            for s in range(RING):
                sp.dma_start(slot[s], stream[s]).then_inc(w_in[s], 16)
            last = UNITS - (UNITS - RING) % RING
            with sp.Fori(1, last // RING) as i:
                for s in range(RING):
                    sp.wait_ge(unit_done, RING * i + (s - RING + 1))
                    sp.dma_start(slot[s], stream[bass.ds(RING * i + s, 1)].rearrange("o p n -> p (o n)")).then_inc(w_in[s], 16)
            for u in range(last, UNITS):
                sp.wait_ge(unit_done, u - RING + 1)
                sp.dma_start(slot[u % RING], stream[u]).then_inc(w_in[u % RING], 16)
            for t in range(NT):
                sp.wait_ge(out_ready, t + 1)
                sp.dma_start(out[t * P:(t + 1) * P, :], xn[:, t, :]).then_inc(out_done, 16)
            sp.wait_ge(out_done, 16 * NT)

        @block.tensor
        def _(pe):
            mm = nc.tensor.matmul

            def arrived(kind, j):
                u = AT[kind, j]
                pe.wait_ge(w_in[u % RING], 16 * (u // RING + 1))
                return slot[u % RING]

            def matvec(w, vec, columns, k0=0):
                for b in range(2):
                    for k in range(KC):
                        at = (b * KC + k) * P
                        last = mm(columns[b], w[:, at:at + P], vec[:, k:k + 1], start=(k == 0), stop=(k == KC - 1))
                return last

            def mod_unit(m):
                w = arrived("mv", m)
                if m == 0:
                    pe.wait_ge(c_silu, 1)
                if m in MOD_READS:
                    pe.wait_ge(mod_read, MOD_READS.index(m) + 1)
                matvec(w, cols[:, 48 + 8 * (m // 24):56 + 8 * (m // 24)],
                       [ps[:, BM, 2 * m + b:2 * m + b + 1] for b in range(2)]).then_inc(unit_done, 1)

            def gemm_T(w, bank, rhs):
                for b in range(2):
                    for k in range(KC):
                        at = (b * KC + k) * P
                        last = mm(ps[:, bank, b * T:(b + 1) * T], w[:, at:at + P], rhs[:, k, :],
                                  start=(k == 0), stop=(k == KC - 1))
                return last

            evacs = [0]

            def bank_free():
                n = evacs[0]
                evacs[0] += 1
                if n >= 2:
                    pe.wait_ge(evac, n - 1)
                return n % 2

            def proj_T(kind, j):
                w = arrived(kind, j)
                gemm_T(w, bank_free(), hT).then_inc(unit_done, 1)

            def transposes(n):
                for k in range(KC):
                    for t in range(NT):
                        if k == 0:
                            pe.wait_ge(xn_ready, NT * n + t + 1)
                        last = nc.tensor.transpose(ps[:, B3 + k // 2, (k % 2) * T + t * P:(k % 2) * T + (t + 1) * P],
                                                   xn[:, t, k * P:(k + 1) * P], c_("ident"))
                    if k % 2:
                        last.then_inc(x_T, 1)

            def hT_wait(n):
                pe.wait_ge(hT_act, 4 * n + 4)
                pe.wait_ge(hT_dve, 4 * n + 4)

            def broadcast_row(n):
                for h in range(2):
                    pe.wait_ge(diag_ready, n + 1)
                    if 2 * n + h > 0:
                        pe.wait_ge(row_ready, 2 * n + h)
                    mm(ps[:, BX, :], c_("ones"), diag[:, 512 * h:512 * h + 512], start=True, stop=True)\
                        .then_inc(row_mm, 1)

            def wide(kind, j, lhs, n_from_0=None):
                w = arrived(kind, j)
                bank = B3 + 2 * (j // 2)
                for t in range(NT):
                    for k in range(4):
                        kk = 4 * (j % 2) + k
                        last = mm(ps[:, bank + t, :], lhs[:, kk, t * P:(t + 1) * P], w[:, 512 * k:512 * k + 512],
                                  start=(kk == 0), stop=(kk == KC - 1))
                last.then_inc(unit_done, 1)

            pe.wait_ge(small_in, 16)
            for m in range(8):
                mod_unit(m)
            transposes(0)
            hT_wait(0)
            for j in range(3):
                proj_T("xbc", j)
            for t in range(NT):
                for k in range(KC):
                    last = mm(ps[:, BX, 8 * t:8 * t + 8], hT[:, k, t * P:(t + 1) * P],
                              c_("w_dt", 8 * k, 8 * k + 8), start=(k == 0), stop=(k == KC - 1))
            last.then_inc(dt_mm, 1)
            for j in range(3):
                proj_T("sc", j)
            for j in range(2):
                proj_T("qk", j)
            w = arrived("v", 0)
            bank = bank_free()
            for t in range(NT):
                for k in range(KC):
                    last = mm(ps[:, bank, t * T:(t + 1) * T], hT[:, k, t * P:(t + 1) * P], w[:, k * T:(k + 1) * T],
                              start=(k == 0), stop=(k == KC - 1))
            last.then_inc(unit_done, 1)

            def sb_scores(h, part, stop):
                r = slice(64 * (h % 2), 64 * (h % 2) + 64)
                q, k = qk[r, h // 2, :], qk[r, 2 + h // 2, :]
                if part == 0:
                    return mm(ps[:, B3 + h, 0:T], k[:, 0:P], q[:, :], start=True, stop=stop)
                return mm(ps[:, B3 + h, T:T + P], k[:, P:T], q[:, P:T], start=True, stop=stop)

            pe.wait_ge(evac, 8)
            for h in range(4):
                sb_scores(h, 0, True)
                last = sb_scores(h, 1, True)
            last.then_inc(sb_z, 1)
            for j in range(2):
                proj_T("z", j)
            for j in range(12):
                proj_T("gl", j)
                mod_unit(8 + j)
                if j == 2:
                    pe.wait_ge(sb_lk, 1)
                    for h in range(4):
                        sb_scores(h, 0, False)
                        mm(ps[:, B3 + h, P:T], c_("ones"), sbl[:, h, T:T + P], start=False, stop=False)
                        mm(ps[:, B3 + h, 0:T], c_("suffix"), sbl[:, h, 0:T], start=False, stop=True)
                        sb_scores(h, 1, False)
                        last = mm(ps[:, B3 + h, T:T + P], c_("suffix"), sbl[:, h, T:T + P], start=False, stop=True)
                    last.then_inc(sb_sum, 1)
                if j == 4:
                    for t in range(NT):
                        pe.wait_ge(xbc_ready, 6)
                        if t:
                            pe.wait_ge(x_tok_ready, t)
                        for b in range(4):
                            last = nc.tensor.transpose(ps[:, BX, b * P:(b + 1) * P], xbc[:, b, t * P:(t + 1) * P],
                                                       c_("ident"))
                        last.then_inc(xs_T, 1)
                if j == 5:
                    pe.wait_ge(a_ready, 1)
                    pe.wait_ge(x_tok_ready, NT)
                    acs = ps[:, BX, 0:16]
                    mm(acs[:, 0:8], c_("tri"), dtb[:, 16:24], start=True, stop=True)
                    mm(acs[:, 8:16], c_("ones"), dtb[:, 16:24], start=True, stop=False)
                    mm(acs[:, 8:16], c_("tri"), dtb[:, 24:32], start=False, stop=True).then_inc(acs_col_mm, 1)
                if j == 6:
                    pe.wait_ge(acs_read, 1)
                    pe.wait_ge(sb_att, 1)
                    pe.wait_ge(evac, 9)
                    for h in range(4):
                        r = slice(64 * (h % 2), 64 * (h % 2) + 64)
                        o = ps[r, BX, (h // 2) * T:(h // 2) * T + T]
                        mm(o, v1[:, 0, 64 * h:64 * h + 64], sba[:, h, 0:T], start=True, stop=True)
                        last = mm(o[:, P:T], v1[:, 1, 64 * h:64 * h + 64], sba[:, h, T:T + P], start=False, stop=True,
                                  skip_group_check=True)
                    last.then_inc(sb_out, 1)
                    pe.wait_ge(a_ready, 2)
                    lo = SMALL["tri"][0]
                    for h in range(8):
                        o = ps[:, B3 + h // 2, (h % 2) * T:(h % 2) * T + T]
                        mm(o, a_rep[:, h, :], sm[:, lo:lo + T], start=True, stop=True)
                        last = mm(o[:, P:T], a_rep[:, 8 + h, :], c_("tri"), start=False, stop=True,
                                  skip_group_check=True)
                    last.then_inc(acs_mm, 1)
            pe.wait_ge(evac, 23)
            for g in range(2):
                r = slice(64 * g, 64 * g + 64)
                mm(ps[:, g, 0:T], xbc[r, 4, 0:P], xbc[r, 5, :], start=True, stop=True)
                last = mm(ps[:, g, T:T + P], xbc[r, 4, P:T], xbc[r, 5, P:T], start=True, stop=True)
            last.then_inc(bc_mm, 1)
            pe.wait_ge(sb_y, 1)
            broadcast_row(0)
            pe.wait_ge(w_ready, 16)
            for h in range(8):
                r = slice(64 * (h % 2), 64 * (h % 2) + 64)
                b = h // 2
                o = ps[r, B3 + b // 2, (b % 2) * T:(b % 2) * T + T]
                mm(o, x_tok[:, 0, 64 * h:64 * h + 64], decay[:, h, 0:T], start=True, stop=True)
                last = mm(o[:, P:T], x_tok[:, 1, 64 * h:64 * h + 64], decay[:, h, T:T + P], start=False, stop=True,
                          skip_group_check=True)
            last.then_inc(y_mm, 1)
            pe.wait_ge(ysq_ready, 1)
            pe.wait_ge(row_ready, 2)
            for g in range(2):
                for b in range(2):
                    last = mm(ps[:, BX, g * T:(g + 1) * T], c_("ones"), ysq[:, 2 * g + b, :], start=(b == 0),
                              stop=(b == 1))
            last.then_inc(ysum_mm, 1)

            pe.wait_ge(ya_ready, 1)
            pe.wait_ge(yc_ready, 1)
            wa, wb = arrived("sco", 0), arrived("sbo", 0)
            wc = [arrived("sso", 0), arrived("sso", 1)]
            for j in range(4):
                if j >= 2:
                    pe.wait_ge(merged, j - 1)
                banks = (3, 4, 5) if j % 2 == 0 else (6, 7, 0)
                for n, (y, kc) in enumerate(((ya, 2), (yb, 2), (yc, 4))):
                    for b in range(2):
                        for k in range(kc):
                            blk = 2 * j + b
                            if n < 2:
                                at = (blk * 2 + k) * P
                                w = (wa, wb)[n][:, at:at + P]
                            else:
                                at = ((blk % 4) * 4 + k) * P
                                w = wc[blk // 4][:, at:at + P]
                            last = mm(ps[:, banks[n], b * T:(b + 1) * T], w, y[:, k, :], start=(k == 0),
                                      stop=(k == kc - 1))
                last.then_inc(*((unit_done, 4) if j == 3 else (br_mm, 1)))
            pe.wait_ge(merged, 4)
            for j in range(4):
                wide("wo", j, mT)

            transposes(1)
            hT_wait(1)

            def gate_up(j, bank):
                gemm_T(arrived("gu", j), bank, hT).then_inc(unit_done, 1)

            def down(w, first, final):
                for f in range(2):
                    for t in range(NT):
                        for n in range(2):
                            last = mm(ps[:, B3 + 2 * n + t, :], hid[:, f, t * P:(t + 1) * P],
                                      w[:, f * D + 512 * n:f * D + 512 * n + 512],
                                      start=(first and f == 0), stop=(final and f == 1), skip_group_check=True)
                last.then_inc(unit_done, 1)

            gate_up(0, 0)
            gate_up(1, 1)
            mod_unit(20)
            mod_unit(21)
            pe.wait_ge(hid_ready, 1)
            gate_up(2, 0)
            pe.wait_ge(hid_ready, 2)
            down(arrived("dn", 0), True, False)
            gate_up(3, 1)
            mod_unit(22)
            mod_unit(23)
            u0 = AT["gu", 4]
            with pe.Fori(2, PAIRS) as i:
                def slot_of(n):
                    s = (u0 + n) % RING
                    pe.wait_ge(w_in[s], 16 * (i + ((u0 + n) // RING - 1)))
                    return slot[s]

                w = slot_of(0)
                pe.wait_ge(hid_ready, 2 * i - 1)
                gemm_T(w, 0, hT).then_inc(unit_done, 1)
                w = slot_of(1)
                pe.wait_ge(hid_ready, 2 * i)
                down(w, False, False)
                w = slot_of(2)
                gemm_T(w, 1, hT).then_inc(unit_done, 1)
                for n in range(2):
                    w = slot_of(3 + n)
                    matvec(w, cols[:, 56:64], [ps[:, BM, bass.ds(4 * i + (40 + 2 * n + b), 1)] for b in range(2)])\
                        .then_inc(unit_done, 1)
            pe.wait_ge(hid_ready, FB)
            pe.wait_ge(res_done, 1)
            broadcast_row(1)
            down(arrived("dn", PAIRS - 1), False, True)

            transposes(2)
            hT_wait(2)
            evacs[0] = 24
            for j in range(4):
                w = arrived("qk2", j)
                if j >= 2:
                    pe.wait_ge(evac, 23 + j - 1)
                gemm_T(w, j % 2, hT).then_inc(unit_done, 1)
                mod_unit(42 + j)
            for kind, bank in (("v2", B3), ("u2", B3 + 2)):
                for j in range(2):
                    w = arrived(kind, j)
                    for t in range(NT):
                        for k in range(4):
                            kk = 4 * j + k
                            last = mm(ps[:, bank + t, :], hT[:, kk, t * P:(t + 1) * P], w[:, 512 * k:512 * k + 512],
                                      start=(kk == 0), stop=(kk == KC - 1))
                    last.then_inc(unit_done, 1)
                mod_unit(46 if kind == "v2" else 47)

            def att_scores(b):
                pe.wait_ge(evac, 31)
                if b:
                    pe.wait_ge(at_read, b)
                for n in range(4):
                    h = 4 * b + n
                    r = slice(64 * (h % 2), 64 * (h % 2) + 64)
                    q, k = qk2[r, h // 2, :], qk2[r, 4 + h // 2, :]
                    mm(ps[:, B3 + n, 0:P], q[:, 0:P], k[:, 0:P], start=True, stop=True)
                    last = mm(ps[:, B3 + n, P:384], q[:, P:T], k[:, :], start=True, stop=True)
                last.then_inc(at_s, 1)

            flat = ps[:, :, :].rearrange("p b n -> p (b n)")

            def att_transposes(b):
                pe.wait_ge(at_p, b + 1)
                if b == 0:
                    pe.wait_ge(pool_ev, 1)
                    pe.wait_ge(col_ready, 6)
                for n in range(4):
                    for m in range(3):
                        at = 384 * n + P * m
                        last = nc.tensor.transpose(flat[:, at:at + P], pnrm[:, n, P * m:P * m + P], c_("ident"))
                last.then_inc(at_T, 1)

            def att_values(b):
                pe.wait_ge(at_pT, b + 1)
                if b:
                    pe.wait_ge(at_o, b)
                else:
                    pe.wait_ge(row_ready, 6)
                for n in range(4):
                    h = 4 * b + n
                    r = slice(64 * (h % 2), 64 * (h % 2) + 64)
                    o = ps[r, BX, (n // 2) * T:(n // 2) * T + T]
                    mm(o, v2[:, 0, 64 * h:64 * h + 64], pT[:, n, 0:T], start=True, stop=True)
                    last = mm(o[:, P:T], v2[:, 1, 64 * h:64 * h + 64], pT[:, n, T:384], start=False, stop=True,
                              skip_group_check=True)
                last.then_inc(at_pv, 1)

            att_scores(0)
            pe.wait_ge(band_in, 16)
            for g in range(4):
                o = ps[:, g // 2, (g % 2) * T:(g % 2) * T + T]
                mm(o, u2[:, 0, g * P:(g + 1) * P], band_sb[:, 0, g, :], start=True, stop=True)
                last = mm(o[:, P:T], u2[:, 1, g * P:(g + 1) * P], band_sb[:, 1, g, P:T], start=False, stop=True,
                          skip_group_check=True)
            last.then_inc(pool_mm, 1)
            pe.wait_ge(res_done, 2)
            broadcast_row(2)
            att_transposes(0)
            att_scores(1)
            att_values(0)
            att_transposes(1)
            att_values(1)
            pe.wait_ge(at_pT, 2)
            for g in range(4):
                last = mm(ps[:, g // 2, (g % 2) * T:(g % 2) * T + T], c_("pool_w", g * P, (g + 1) * P),
                          pooled[:, g, :], start=True, stop=True)
            last.then_inc(pool_out, 1)
            pe.wait_ge(at_o, 2)
            pe.wait_ge(pool_y, 1)
            for j in range(4):
                wide("wo2", j, mT)
            for n in (3, 4):
                broadcast_row(n)
            transposes(3)
            hT_wait(3)

            def sub_scores(h):
                pe.wait_ge(evac, 31 + h + 1)
                if h >= 4:
                    pe.wait_ge(s_ready, h - 3)
                for t in range(NT):
                    for p in range(2):
                        last = mm(ps[:, B3 + h % 4, (2 * t + p) * P:(2 * t + p + 1) * P],
                                  qh[:, h % 2, p * T + t * P:p * T + (t + 1) * P], c_("keys", p * P, (p + 1) * P),
                                  start=True, stop=True)
                last.then_inc(s_mm, 1)

            for h in range(HEADS):
                w = arrived("wq", h)
                if h >= 2:
                    pe.wait_ge(evac, 31 + h - 1)
                gemm_T(w, h % 2, hT).then_inc(unit_done, 1)
                if h:
                    sub_scores(h - 1)
            sub_scores(HEADS - 1)
            pe.wait_ge(res_done, 3)
            broadcast_row(5)

        @block.scalar
        def _(act):
            step = Steps(act, act_step)
            A = nc.scalar.activation

            def squares(n, source, outs):
                for m, (s, o) in enumerate(zip(source, outs)):
                    A(o, s, ACT.Square, accum_out=stat[:, 8 * (n % 4) + m:8 * (n % 4) + m + 1]).then_inc(sq_sum, 1)

            sq_n = [0]

            def square_root(n, w):
                act.wait_ge(mean_sq, n + 1)
                A(stat[:, 32 + 2 * (n % 8):32 + 2 * (n % 8) + w], stat[:, 48 + 2 * (n % 8):48 + 2 * (n % 8) + w],
                  ACT.Sqrt).then_inc(root, 1)

            def hT_part(n):
                for k in (0, 1, 4, 5):
                    act.wait_ge(x_T, KC // 2 * n + k // 2 + 1)
                    src = ps[:, B3 + k // 2, (k % 2) * T:(k % 2) * T + T]
                    if n < 3:
                        act.wait_ge(col_ready, (1, 3, 4)[n])
                        A(hT[:, k, :], src, ACT.Identity, scale=cols[:, 16 * n + k:16 * n + k + 1],
                          bias=cols[:, 16 * n + 8 + k:16 * n + 9 + k]).then_inc(hT_act, 1)
                    else:
                        A(hT[:, k, :], src, ACT.Identity).then_inc(hT_act, 1)

            def copy_out(kind, j, dst, func=ACT.Identity, scale=1.0, bank=0, w=512):
                act.wait_ge(unit_done, DONE(kind, j))
                src = ps[:, bank, :].rearrange("p (b t) -> p b t", b=2)
                A(dst, src, func, scale=scale).then_inc(evac, 1)

            def row_copy(n, dst):
                for h in range(2):
                    act.wait_ge(row_mm, 2 * n + h + 1)
                    A(dst[:, 512 * h:512 * h + 512], ps[:, BX, :], ACT.Identity).then_inc(row_ready, 1)

            act.wait_ge(small_in, 16)
            A(cols[:, 48:64], c_("c", 0, 16), ACT.Silu).then_inc(c_silu, 1)
            A(dtb[:, 32:40], c_("a_log"), ACT.Exp).then_inc(a_exp, 1)
            act.wait_ge(x_in, 16)
            squares(0, [x_sb[:, t, :] for t in range(NT)], [xn[:, t, :] for t in range(NT)])
            square_root(0, 2)
            hT_part(0)
            n = 0
            for j in range(3):
                copy_out("xbc", j, xbc_raw[:, 2 * j:2 * j + 2, 3:], bank=n % 2)
                n += 1
            for j in range(3):
                copy_out("sc", j, sc[:, 2 * j:2 * j + 2, :], bank=n % 2)
                n += 1
            act.wait_ge(dt_lin, 2)
            A(dtb[:, 64:80], dtb[:, 48:64], ACT.Exp, scale=-1.0).then_inc(dt_exp, 1)
            act.wait_ge(dt_one, 1)
            A(dtb[:, 96:112], dtb[:, 80:96], ACT.Ln).then_inc(dt_log, 1)
            for j in range(2):
                copy_out("qk", j, qk[:, 2 * j:2 * j + 2, :], scale=(0.125 if j == 0 else 1.0), bank=n % 2)
                n += 1
            copy_out("v", 0, v1, bank=n % 2)
            n += 1
            z4 = ps[:, B3:B3 + 4, 0:384]
            act.wait_ge(sb_z, 1)
            step(A(sbl, z4, ACT.Abs))
            step.wait()
            step(A(sbl, sbl, ACT.Exp, scale=-1.0))
            step.wait()
            A(sbl, sbl, ACT.Ln, bias=1.0).then_inc(sb_log, 1)
            for b in range(6):
                act.wait_ge(conv_done, b + 1)
                A(xbc[:, b, :], xbc[:, b, :], ACT.Silu, bias=c_("ssm_b", b, b + 1)).then_inc(xbc_ready, 1)
            for j in range(2):
                copy_out("z", j, zg[:, 2 * j:2 * j + 2, :], func=ACT.Silu, bank=n % 2)
                n += 1
            for j in range(12):
                copy_out("gl", j, gates[:, 2 * j:2 * j + 2, :], func=ACT.Sigmoid, bank=n % 2)
                n += 1
                if j == 4:
                    act.wait_ge(sb_arg, 1)
                    A(sba, sba, ACT.Exp).then_inc(sb_att, 1)
                    for t in range(NT):
                        act.wait_ge(xs_T, t + 1)
                        A(x_tok[:, t, :], ps[:, BX, :], ACT.Identity).then_inc(x_tok_ready, 1)
                if j == 8:
                    act.wait_ge(sb_out, 1)
                    A(yb, ps[:, BX, :].rearrange("p (b t) -> p b t", b=2), ACT.Identity).then_inc(sb_y, 1)
                if j == 10:
                    for hh in range(2):
                        act.wait_ge(dec_arg, 8 * hh + 8)
                        A(decay[:, 4 * hh:4 * hh + 4, :], decay[:, 4 * hh:4 * hh + 4, :], ACT.Exp)\
                            .then_inc(dec_exp, 1)
            row_copy(0, gate_row)
            act.wait_ge(yms, 1)
            A(ysq[:, 0:2, :], ysq[:, 0:2, :], ACT.Sqrt).then_inc(yroot, 1)
            act.wait_ge(unit_done, DONE("wo", 3))
            squares(1, [ps[:, B3 + b, :] for b in range(4)],
                    [xn[:, b % 2, 512 * (b // 2):512 * (b // 2) + 512] for b in range(4)])
            square_root(1, 2)
            act.wait_ge(res_done, 1)
            squares(2, [x_sb[:, t, :] for t in range(NT)], [xn[:, t, :] for t in range(NT)])
            square_root(2, 2)
            hT_part(1)
            for f in range(2):
                act.wait_ge(unit_done, DONE("gu", f))
                A(sg[:, f, :], ps[:, f, 0:T], ACT.Silu).then_inc(silu_done, 1)
            with act.Fori(1, PAIRS) as i:
                for f in range(2):
                    act.wait_ge(unit_done, 5 * i + (AT["gu", 2 + f] - 5 + 1))
                    act.wait_ge(hid_ready, 2 * i + (f - 1))
                    A(sg[:, f, :], ps[:, f, 0:T], ACT.Silu).then_inc(silu_done, 1)
            row_copy(1, gate_row)
            act.wait_ge(unit_done, DONE("dn", PAIRS - 1))
            squares(3, [ps[:, B3 + b, :] for b in range(4)],
                    [xn[:, b % 2, 512 * (b // 2):512 * (b // 2) + 512] for b in range(4)])
            square_root(3, 2)
            act.wait_ge(res_done, 2)
            squares(4, [x_sb[:, t, :] for t in range(NT)], [xn[:, t, :] for t in range(NT)])
            square_root(4, 2)
            hT_part(2)
            for j in range(4):
                copy_out("qk2", j, qk2[:, 2 * j:2 * j + 2, :], bank=j % 2)
            for kind, dst, bank in (("v2", v2, B3), ("u2", u2, B3 + 2)):
                act.wait_ge(unit_done, DONE(kind, 1))
                for t in range(NT):
                    A(dst[:, t, :], ps[:, bank + t, :], ACT.Identity).then_inc(evac, 1)

            def att_exp(b):
                act.wait_ge(at_max, b + 1)
                for n in range(4):
                    for t, (lo, hi) in enumerate(((0, P), (P, 384))):
                        A(pnrm[:, n, lo:hi], pexp[:, n, lo:hi], ACT.Exp, scale=0.125,
                          bias=stat[:, 4 * t + n:4 * t + n + 1]).then_inc(at_exp, 1)

            def pT_copy(b):
                act.wait_ge(at_T, b + 1)
                if b:
                    act.wait_ge(at_pv, b)
                A(pT, flat_ps[:, 0:1536].rearrange("p (a b) -> p a b", a=4), ACT.Identity).then_inc(at_pT, 1)

            def o_copy(b):
                act.wait_ge(at_pv, b + 1)
                A(mT[:, 2 * b:2 * b + 2, :], ps[:, BX, :].rearrange("p (b t) -> p b t", b=2), ACT.Identity)\
                    .then_inc(at_o, 1)

            flat_ps = ps[:, :, :].rearrange("p b n -> p (b n)")
            act.wait_ge(pool_mm, 1)
            A(pooled, flat_ps[:, 0:1024].rearrange("p (a b) -> p a b", a=4), ACT.Identity).then_inc(pool_ev, 1)
            row_copy(2, gate_row)
            att_exp(0)
            pT_copy(0)
            att_exp(1)
            o_copy(0)
            pT_copy(1)
            o_copy(1)
            act.wait_ge(pool_out, 1)
            for g in range(4):
                A(mT[:, 4 + g, :], flat_ps[:, g * T:(g + 1) * T], ACT.Identity,
                  scale=c_("pool_scale", g, g + 1)).then_inc(act_step if g < 3 else pool_y, 1)
            step.n += 3
            row_copy(3, scale_row)
            row_copy(4, shift_row)
            act.wait_ge(res_done, 3)
            squares(5, [x_sb[:, t, :] for t in range(NT)], [xn[:, t, :] for t in range(NT)])
            square_root(5, 2)
            hT_part(3)
            for h in range(HEADS + 1):
                if h < HEADS:
                    act.wait_ge(unit_done, DONE("wq", h))
                    if h >= 2:
                        act.wait_ge(s_mm, h - 1)
                    A(qh[:, h % 2, :], ps[:, h % 2, :], ACT.Identity).then_inc(evac, 1)
                if h:
                    act.wait_ge(s_mm, h)
                    A(score[:, :, 2 * h - 2:2 * h, :],
                      ps[:, B3 + (h - 1) % 4, :].rearrange("p (t s n) -> p t s n", t=NT, s=2), ACT.Identity)\
                        .then_inc(s_ready, 1)
            row_copy(5, gate_row)
            for t in range(NT):
                act.wait_ge(top_v, t + 1)
                g = gate[:, SLOTS * t:SLOTS * (t + 1)]
                A(g, g, ACT.Exp).then_inc(top_exp, 1)
            for t in range(NT):
                act.wait_ge(dots_out, SLOTS // ROWS * (t + 1))
                d = dots[:, SLOTS * t:SLOTS * (t + 1)]
                A(d, d, ACT.Gelu).then_inc(gelu_done, 1)
            act.wait_ge(res_done, 4)
            squares(6, [x_sb[:, t, :] for t in range(NT)], [xn[:, t, :] for t in range(NT)])
            square_root(6, 2)

        @block.gpsimd
        def _(pool):
            pool.wait_ge(res_done, 1)
            pool.dma_start(cut(areaA, 4096, 2048), band).then_inc(band_in, 16)
            pool.wait_ge(res_done, 3)
            pool.dma_start(final_row, final_g).then_inc(final_in, 16)
            pool.wait_ge(idx_ready, NT)
            for table, n_pass in ((expert_u, 0), (expert_v, 1)):
                def gathers(half):
                    for r in range(8 * half, 8 * half + 8):
                        pool.indirect_dma_start(row[r], None, table, bass.IndirectOffsetOnAxis(
                            ap=idx_now[:, r:r + 1], axis=0)).then_inc(row_in[r], 16)

                if n_pass == 0:
                    for half in range(2):
                        nc.gpsimd.tensor_copy(idx_now[:, 8 * half:8 * half + 8], idx[:, 8 * half:8 * half + 8])\
                            .then_inc(idx_copied, 1)
                        pool.wait_ge(idx_copied, half + 1)
                        gathers(half)
                done = n_pass * GROUPS
                with pool.Fori(1 - n_pass, GROUPS) as i:
                    for half in range(2):
                        pool.wait_ge(row_used, ROWS * i + (ROWS * (done - 1) + 8 * half + 8))
                        pool.sem_inc(pool_go, 1)
                        nc.gpsimd.tensor_copy(idx_now[:, 8 * half:8 * half + 8],
                                              idx[:, bass.ds(ROWS * i + 8 * half, 8)]).then_inc(idx_copied, 1)
                        pool.wait_ge(idx_copied, 2 * i + (2 * done + half + 1))
                        pool.sem_inc(pool_go, 1)
                        gathers(half)

        @block.vector
        def _(dve):
            V = nc.vector
            step = Steps(dve, dve_step)

            def rstd(n, pieces):
                need = {0: 2, 1: 6, 2: 8, 3: 12, 4: 14, 5: 16, 6: 18}[n]
                dve.wait_ge(sq_sum, need)
                src = stat[:, 8 * (n % 4):8 * (n % 4) + 2]
                if pieces == 2:
                    step(V.tensor_tensor(stat[:, 8 * (n % 4) + 4:8 * (n % 4) + 6], src,
                                         stat[:, 8 * (n % 4) + 2:8 * (n % 4) + 4], ALU.add))
                    step.wait()
                    src = stat[:, 8 * (n % 4) + 4:8 * (n % 4) + 6]
                V.tensor_scalar(stat[:, 48 + 2 * (n % 8):50 + 2 * (n % 8)], src, 1.0 / D, EPS, ALU.mult, ALU.add)\
                    .then_inc(mean_sq, 1)
                dve.wait_ge(root, n + 1)
                r = stat[:, 32 + 2 * (n % 8):34 + 2 * (n % 8)]
                step(V.reciprocal(r, r))
                step.wait()
                return r

            def normalise(n, r):
                for t in range(NT):
                    V.tensor_scalar(xn[:, t, :], x_sb[:, t, :], r[:, t:t + 1], None, ALU.mult).then_inc(xn_ready, 1)

            def hT_part(n):
                if n < 3:
                    dve.wait_ge(col_ready, (1, 3, 4)[n])
                for k in (2, 3, 6, 7):
                    dve.wait_ge(x_T, KC // 2 * n + k // 2 + 1)
                    src = ps[:, B3 + k // 2, (k % 2) * T:(k % 2) * T + T]
                    if n < 3:
                        V.tensor_scalar(hT[:, k, :], src, cols[:, 16 * n + k:16 * n + k + 1],
                                        cols[:, 16 * n + 8 + k:16 * n + 9 + k], ALU.mult, ALU.add)\
                            .then_inc(hT_dve, 1)
                    else:
                        V.tensor_copy(hT[:, k, :], src).then_inc(hT_dve, 1)

            def modulation(m0, m1):
                dve.wait_ge(unit_done, DONE("mv", m1 - 1))
                V.tensor_tensor(modT[:, 2 * m0:2 * m1], ps[:, BM, 2 * m0:2 * m1], c_("mod_b", 2 * m0, 2 * m1),
                                ALU.add).then_inc(mod_read, 1)
                dve.wait_ge(mod_read, MOD_READS.index(m1) + 1)

            ident8 = c_("ident").unsqueeze(1).to_broadcast([P, 8, P])
            diag3 = diag[:, :].rearrange("p (k n) -> p k n", k=8)

            def spread(n, vec):
                if n:
                    dve.wait_ge(row_mm, 2 * n)
                V.tensor_tensor(diag3, ident8, vec.unsqueeze(2).to_broadcast([P, 8, P]), ALU.mult)\
                    .then_inc(diag_ready, 1)

            def residual(n, r, rows):
                dve.wait_ge(row_ready, rows)
                for b in range(4):
                    t, lo = b % 2, 512 * (b // 2)
                    src = ps[:, B3 + b, :]
                    if r is None:
                        step(V.tensor_tensor(xn[:, t, lo:lo + 512], src, gate_row[:, lo:lo + 512], ALU.mult))
                    else:
                        step(V.scalar_tensor_tensor(out=xn[:, t, lo:lo + 512], in0=src, scalar=r[:, t:t + 1],
                                                    in1=gate_row[:, lo:lo + 512], op0=ALU.mult, op1=ALU.mult))
                step.wait()
                for t in range(NT):
                    ins = V.tensor_tensor(x_sb[:, t, :], x_sb[:, t, :], xn[:, t, :], ALU.add)
                    if t == 0:
                        step(ins)
                step.wait()
                ins.then_inc(res_done, 1)

            step(V.memset(xbc_raw[:, :, 0:3], 0.0))
            step(V.memset(cx[:, :, 0:2], 0.0))
            dve.wait_ge(x_in, 16)
            dve.wait_ge(small_in, 16)
            normalise(0, rstd(0, 1))
            modulation(0, 8)
            step(V.scalar_tensor_tensor(out=cols[:, 0:8], in0=modT[:, 8:16], scalar=1.0, in1=c_("g_pre_mix"),
                                        op0=ALU.add, op1=ALU.mult))
            step.wait()
            V.tensor_copy(cols[:, 8:16], modT[:, 0:8]).then_inc(col_ready, 1)
            dve.wait_ge(col_ready, 1)
            hT_part(0)

            for k in range(4):
                for b in range(6):
                    w = c_("ssm_w", 4 * b + k, 4 * b + k + 1)
                    if k == 0:
                        if b % 2 == 0:
                            dve.wait_ge(evac, b // 2 + 1)
                        step(V.tensor_scalar(xbc[:, b, :], xbc_raw[:, b, 0:T], w, None, ALU.mult))
                    else:
                        step.wait(5)
                        ins = V.scalar_tensor_tensor(out=xbc[:, b, :], in0=xbc_raw[:, b, k:k + T], scalar=w,
                                                     in1=xbc[:, b, :], op0=ALU.mult, op1=ALU.add)
                        if k < 3:
                            step(ins)
                        else:
                            ins.then_inc(conv_done, 1)
                if k == 2:
                    step.wait()
            dt, a, ea = dtb[:, 0:16], dtb[:, 16:32], dtb[:, 32:40]
            mag, e, u, l, lin = dtb[:, 48:64], dtb[:, 64:80], dtb[:, 80:96], dtb[:, 96:112], dtb[:, 112:128]
            dve.wait_ge(dt_mm, 1)
            step(V.tensor_tensor(lin.rearrange("p (t h) -> p t h", t=NT),
                                 ps[:, BX, 0:16].rearrange("p (t h) -> p t h", t=NT),
                                 c_("dt_b").unsqueeze(1).to_broadcast([P, NT, 8]), ALU.add))
            step.wait()
            V.scalar_tensor_tensor(out=mag, in0=lin, scalar=-1.0, in1=lin, op0=ALU.mult, op1=ALU.max)\
                .then_inc(dt_lin, 1)
            V.tensor_scalar(lin, lin, 0.0, None, ALU.max).then_inc(dt_lin, 1)
            dve.wait_ge(dt_exp, 1)
            V.tensor_scalar(u, e, 1.0, None, ALU.add).then_inc(dt_one, 1)
            dve.wait_ge(dt_one, 1)
            step(V.scalar_tensor_tensor(out=dtb[:, 128:144], in0=u, scalar=-1.0, in1=e, op0=ALU.add,
                                        op1=ALU.subtract))
            step(V.reciprocal(dtb[:, 144:160], u))
            step.wait()
            step(V.scalar_tensor_tensor(out=dtb[:, 160:176], in0=dtb[:, 128:144], scalar=-1.0, in1=dtb[:, 144:160],
                                        op0=ALU.mult, op1=ALU.mult))
            dve.wait_ge(dt_log, 1)
            dve.wait_ge(dt_lin, 2)
            step(V.tensor_tensor(lin, lin, l, ALU.add))
            step.wait()
            step(V.tensor_tensor(dt, lin, dtb[:, 160:176], ALU.add))
            step.wait()
            dve.wait_ge(a_exp, 1)
            V.scalar_tensor_tensor(out=a.rearrange("p (t h) -> p t h", t=NT),
                                   in0=dt.rearrange("p (t h) -> p t h", t=NT), scalar=-1.0,
                                   in1=ea.unsqueeze(1).to_broadcast([P, NT, 8]), op0=ALU.mult, op1=ALU.mult)\
                .then_inc(a_ready, 1)
            dve.wait_ge(a_ready, 1)
            V.tensor_copy(a_rep, a.unsqueeze(2).to_broadcast([P, 16, P])).then_inc(a_ready, 1)
            dve.wait_ge(evac, 6)
            step(V.tensor_tensor(cx[:, :, 2:], sc[:, 2:4, :], sc[:, 4:6, :], ALU.mult))
            step.wait()
            for k in range(3):
                for b in range(2):
                    w = c_("sc_w", 3 * b + k, 3 * b + k + 1)
                    if k == 0:
                        step(V.tensor_scalar(ya[:, b, :], cx[:, b, 0:T], w, None, ALU.mult))
                    else:
                        step.wait(1)
                        step(V.scalar_tensor_tensor(out=ya[:, b, :], in0=cx[:, b, k:k + T], scalar=w,
                                                    in1=ya[:, b, :], op0=ALU.mult, op1=ALU.add))
            step.wait()
            V.tensor_tensor(ya, ya, sc[:, 0:2, :], ALU.mult).then_inc(ya_ready, 1)
            z4 = ps[:, B3:B3 + 4, 0:384]
            dve.wait_ge(sb_log, 1)
            for h in range(4):
                step(V.scalar_tensor_tensor(out=sbl[:, h, :], in0=ps[:, B3 + h, 0:384], scalar=0.0,
                                            in1=sbl[:, h, :], op0=ALU.max, op1=ALU.add))
            step.wait()
            V.tensor_tensor(sbl, sbl, c_("sb_keep").unsqueeze(1).to_broadcast([P, 4, 384]), ALU.mult)\
                .then_inc(sb_lk, 1)
            dve.wait_ge(sb_sum, 1)
            V.tensor_tensor(sba, z4, c_("sb_bias").unsqueeze(1).to_broadcast([P, 4, 384]), ALU.add)\
                .then_inc(sb_arg, 1)
            dve.wait_ge(acs_col_mm, 1)
            V.tensor_copy(dtb[:, 176:192], ps[:, BX, 0:16]).then_inc(acs_read, 1)
            modulation(8, 20)
            step(V.tensor_tensor(modT[:, 16:24], modT[:, 16:24], c_("g_post_mix"), ALU.mult))
            step.wait()
            spread(0, modT[:, 16:24])
            dve.wait_ge(acs_mm, 1)
            dve.wait_ge(acs_read, 1)
            for h in range(8):
                col = ps[:, B3 + h // 2, (h % 2) * T:(h % 2) * T + T]
                V.scalar_tensor_tensor(out=decay[:, h, 0:T], in0=col, scalar=dtb[:, 176 + h:177 + h],
                                       in1=c_("ssm_bias", 0, T), op0=ALU.subtract, op1=ALU.add).then_inc(dec_arg, 1)
                V.scalar_tensor_tensor(out=decay[:, h, T:384], in0=col[:, P:T], scalar=dtb[:, 184 + h:185 + h],
                                       in1=c_("ssm_bias", T, 384), op0=ALU.subtract, op1=ALU.add)\
                    .then_inc(dec_arg, 1)
            dve.wait_ge(bc_mm, 1)
            for h in range(8):
                if h % 4 == 0:
                    dve.wait_ge(dec_exp, h // 4 + 1)
                for t, (lo, hi) in enumerate(((0, T), (T, 384))):
                    V.scalar_tensor_tensor(out=decay[:, h, lo:hi], in0=decay[:, h, lo:hi],
                                           scalar=dt[:, 8 * t + h:8 * t + h + 1], in1=ps[:, h // 4, lo:hi],
                                           op0=ALU.mult, op1=ALU.mult).then_inc(w_ready, 1)
            step(V.scalar_tensor_tensor(out=cols[:, 16:24], in0=modT[:, 32:40], scalar=1.0, in1=c_("g_pre_ffn"),
                                        op0=ALU.add, op1=ALU.mult))
            V.tensor_copy(cols[:, 24:32], modT[:, 24:32]).then_inc(col_ready, 2)
            dve.wait_ge(y_mm, 1)
            for b in range(4):
                step(V.scalar_tensor_tensor(out=yc[:, b, :], in0=xbc[:, b, :], scalar=c_("ssm_d", b, b + 1),
                                            in1=ps[:, B3 + b // 2, (b % 2) * T:(b % 2) * T + T],
                                            op0=ALU.mult, op1=ALU.add))
            step.wait()
            step(V.tensor_tensor(yc, yc, zg, ALU.mult))
            step.wait()
            V.tensor_tensor(ysq, yc, yc, ALU.mult).then_inc(ysq_ready, 1)
            dve.wait_ge(ysum_mm, 1)
            V.tensor_scalar(ysq[:, 0:2, :], ps[:, BX, :].rearrange("p (b t) -> p b t", b=2), 1.0 / (2 * P), EPS, ALU.mult,
                            ALU.add).then_inc(yms, 1)
            dve.wait_ge(yroot, 1)
            step(V.reciprocal(ysq[:, 0:2, :], ysq[:, 0:2, :]))
            step.wait()
            for b in range(4):
                ins = V.scalar_tensor_tensor(out=yc[:, b, :], in0=yc[:, b, :], scalar=c_("ssm_norm", b, b + 1),
                                             in1=ysq[:, b // 2, :], op0=ALU.mult, op1=ALU.mult)
                if b < 3:
                    step(ins)
            step.wait()
            ins.then_inc(yc_ready, 1)
            for j in range(4):
                dve.wait_ge(unit_done if j == 3 else br_mm, DONE("sso", 1) if j == 3 else j + 1)
                if j == 0:
                    dve.wait_ge(evac, 23)
                banks = (3, 4, 5) if j % 2 == 0 else (6, 7, 0)
                pr = prod[3 * (j % 2):3 * (j % 2) + 3]
                for n in range(3):
                    step(V.tensor_tensor(pr[n], ps[:, banks[n], :].rearrange("p (b t) -> p b t", b=2),
                                         gates[:, 8 * n + 2 * j:8 * n + 2 * j + 2, :], ALU.mult))
                step.wait()
                step(V.tensor_tensor(pr[0], pr[0], pr[1], ALU.add))
                step.wait()
                V.tensor_tensor(mT[:, 2 * j:2 * j + 2, :], pr[0], pr[2], ALU.add).then_inc(merged, 1)
            residual(0, rstd(1, 2), 2)
            dve.wait_ge(res_done, 1)
            normalise(1, rstd(2, 1))
            hT_part(1)

            for f in range(2):
                dve.wait_ge(silu_done, f + 1)
                V.tensor_tensor(hid[:, f, :], sg[:, f, :], ps[:, f, T:2 * T], ALU.mult).then_inc(hid_ready, 1)
            with dve.Fori(1, PAIRS) as i:
                for f in range(2):
                    dve.wait_ge(silu_done, 2 * i + (f + 1))
                    dve.wait_ge(unit_done, 5 * i + (AT["dn", 0] - 5 + 1))
                    V.tensor_tensor(hid[:, f, :], sg[:, f, :], ps[:, f, T:2 * T], ALU.mult).then_inc(hid_ready, 1)
            modulation(20, 42)
            step(V.tensor_tensor(modT[:, 40:48], modT[:, 40:48], c_("g_post_ffn"), ALU.mult))
            step(V.scalar_tensor_tensor(out=cols[:, 32:40], in0=modT[:, 56:64], scalar=1.0, in1=c_("norm1"),
                                        op0=ALU.add, op1=ALU.mult))
            step.wait()
            V.tensor_copy(cols[:, 40:48], modT[:, 48:56]).then_inc(col_ready, 1)
            spread(1, modT[:, 40:48])
            residual(1, rstd(3, 2), 4)
            dve.wait_ge(res_done, 2)
            normalise(2, rstd(4, 1))
            spread(2, modT[:, 64:72])
            hT_part(2)
            modulation(42, 48)
            V.scalar_tensor_tensor(out=modT[:, 80:88], in0=modT[:, 80:88], scalar=1.0, in1=c_("norm2"),
                                   op0=ALU.add, op1=ALU.mult).then_inc(col_ready, 2)

            for b in range(2):
                dve.wait_ge(at_s, b + 1)
                if b:
                    dve.wait_ge(at_exp, 8)
                for n in range(4):
                    slope = 2.0 ** (-(4 * b + n + 1))
                    ins = V.scalar_tensor_tensor(out=pexp[:, n, :], in0=c_("dist"), scalar=-8.0 * slope,
                                                 in1=ps[:, B3 + n, 0:384], op0=ALU.mult, op1=ALU.add)
                    if n < 3:
                        step(ins)
                ins.then_inc(at_read, 1)
                step.wait()
                dve.wait_ge(at_read, b + 1)
                mx = stat[:, 0:8]
                step(V.tensor_reduce(stat[:, 8:12], pexp[:, :, 0:P], X, ALU.max))
                step(V.tensor_reduce(stat[:, 12:16], pexp[:, :, P:384], X, ALU.max))
                step.wait()
                V.tensor_scalar(mx, stat[:, 8:16], -0.125, None, ALU.mult).then_inc(at_max, 1)
                dve.wait_ge(at_exp, 8 * b + 8)
                if b:
                    dve.wait_ge(at_T, b)
                step(V.tensor_tensor(pnrm, pnrm, c_("count").unsqueeze(1).to_broadcast([P, 4, 384]), ALU.mult))
                step.wait()
                for t, (lo, hi) in enumerate(((0, P), (P, 384))):
                    step(V.tensor_reduce(stat[:, 16 + 4 * t:20 + 4 * t], pnrm[:, :, lo:hi], X, ALU.add))
                step.wait()
                step(V.reciprocal(stat[:, 16:24], stat[:, 16:24]))
                step.wait()
                for t, (lo, hi) in enumerate(((0, P), (P, 384))):
                    ins = V.tensor_tensor(pnrm[:, :, lo:hi], pnrm[:, :, lo:hi],
                                          stat[:, 16 + 4 * t:20 + 4 * t].unsqueeze(2).to_broadcast([P, 4, hi - lo]),
                                          ALU.mult)
                    if t == 0:
                        step(ins)
                step.wait()
                ins.then_inc(at_p, 1)
            dve.wait_ge(col_ready, 6)
            spread(3, modT[:, 80:88])
            spread(4, modT[:, 72:80])
            dve.wait_ge(unit_done, DONE("wo2", 3))
            residual(2, None, 6)
            dve.wait_ge(res_done, 3)
            spread(5, modT[:, 88:96])
            r = rstd(5, 1)
            dve.wait_ge(row_ready, 10)
            for t in range(NT):
                step(V.scalar_tensor_tensor(out=xn[:, t, :], in0=x_sb[:, t, :], scalar=r[:, t:t + 1],
                                            in1=scale_row[:, :], op0=ALU.mult, op1=ALU.mult))
            step.wait()
            for t in range(NT):
                V.tensor_tensor(xn[:, t, :], xn[:, t, :], shift_row[:, :], ALU.add).then_inc(xn_ready, 1)
            hT_part(3)

            def top16(values, spare, out_v, out_i, group=4):
                n = len(values)
                for g in range(0, n, group):
                    some = range(g, min(g + group, n))
                    for q in some:
                        step(V.max(out_v[q][:, 0:8], values[q]))
                    step.wait()
                    for q in some:
                        step(V.max_index(out_i[q][:, 0:8], out_v[q][:, 0:8], values[q]))
                    for q in some:
                        step(V.match_replace(spare[q], out_v[q][:, 0:8], values[q], -3e38))
                    step.wait()
                    for q in some:
                        step(V.max(out_v[q][:, 8:16], spare[q]))
                    step.wait()
                    for q in some:
                        step(V.max_index(out_i[q][:, 8:16], out_v[q][:, 8:16], spare[q]))
                step.wait()

            dve.wait_ge(s_ready, HEADS)
            for t in range(NT):
                top16([score[:, t, q, :] for q in range(16)], [rest[:, q, :] for q in range(16)],
                      [sv[:, q, :] for q in range(16)], [si[:, q, :] for q in range(16)])
                step(V.tensor_copy(sif, si))
                sv4 = sv.rearrange("p (h s) k -> p h s k", s=2)
                step(V.tensor_tensor(cand.rearrange("p h (i j) -> p h i j", i=TOPK),
                                     sv4[:, :, 0, :].unsqueeze(3).to_broadcast([P, HEADS, TOPK, TOPK]),
                                     sv4[:, :, 1, :].unsqueeze(2).to_broadcast([P, HEADS, TOPK, TOPK]), ALU.add))
                step.wait()
                top16([cand[:, h, :] for h in range(HEADS)], [cand_rest[:, h, :] for h in range(HEADS)],
                      [tv[:, h, :] for h in range(HEADS)],
                      [ti[:, TOPK * h:TOPK * (h + 1)] for h in range(HEADS)])
                g3 = gate[:, SLOTS * t:SLOTS * (t + 1)].rearrange("p (h k) -> p h k", h=HEADS)
                V.tensor_tensor(g3, tv, tv[:, :, 0:1].to_broadcast([P, HEADS, TOPK]), ALU.subtract)\
                    .then_inc(top_v, 1)
                for p, (op, by) in enumerate(((ALU.logical_shift_right, 4), (ALU.bitwise_and, 15))):
                    step(V.tensor_scalar(tr, ti, by, None, op))
                    step.wait()
                    step(V.tensor_copy(pos_f[p], tr))
                    step.wait()
                    step(V.tensor_tensor(onehot, pos_f[p].unsqueeze(2).to_broadcast([P, SLOTS, TOPK]),
                                         c_("iota").unsqueeze(1).to_broadcast([P, SLOTS, TOPK]), ALU.is_equal))
                    step.wait()
                    oh4 = onehot.rearrange("p (h k) j -> p h k j", h=HEADS)
                    keys = sif.rearrange("p (h s) k -> p h s k", s=2)[:, :, p, :]
                    step(V.tensor_tensor(oh4, oh4, keys.unsqueeze(2).to_broadcast([P, HEADS, TOPK, TOPK]), ALU.mult))
                    step.wait()
                    step(V.tensor_reduce(pick[p], onehot, X, ALU.add))
                    step.wait()
                V.scalar_tensor_tensor(out=idx[:, SLOTS * t:SLOTS * (t + 1)], in0=pick[0], scalar=float(P),
                                       in1=pick[1], op0=ALU.mult, op1=ALU.add).then_inc(idx_ready, 1)
                dve.wait_ge(top_exp, t + 1)
                z = stat[:, 8 * t:8 * t + 8]
                step(V.tensor_reduce(z, g3, X, ALU.add))
                step.wait()
                step(V.reciprocal(z, z))
                step.wait()
                step(V.tensor_tensor(g3, g3, z.unsqueeze(2).to_broadcast([P, HEADS, TOPK]), ALU.mult))
                step.wait()
                dve.wait_ge(idx_ready, t + 1)

            for t in range(NT):
                g0 = t * SLOTS // ROWS
                with dve.Fori(g0, g0 + SLOTS // ROWS) as i:
                    for r in range(ROWS):
                        dve.wait_ge(row_in[r], 16 * i + 16)
                        V.tensor_tensor_reduce(row[r], row[r], xn[:, t, :], 1.0, 0.0, ALU.mult, ALU.add,
                                               now[:, r:r + 1]).then_inc(row_used, 1)
                    dve.wait_ge(row_used, ROWS * i + ROWS)
                    V.tensor_copy(dots[:, bass.ds(ROWS * i, ROWS)], now[:, :]).then_inc(dots_out, 1)
                    dve.wait_ge(dots_out, i + 1)
            for t in range(NT):
                dve.wait_ge(gelu_done, t + 1)
                g = gate[:, SLOTS * t:SLOTS * (t + 1)]
                step(V.tensor_tensor(g, g, dots[:, SLOTS * t:SLOTS * (t + 1)], ALU.mult))
                step(V.memset(y_acc[t], 0.0))
                step(V.memset(y_alt[t], 0.0))
            step.wait()
            for t in range(NT):
                g0 = t * SLOTS // ROWS
                with dve.Fori(g0, g0 + SLOTS // ROWS) as i:
                    V.tensor_copy(now[:, :], gate[:, bass.ds(ROWS * i, ROWS)]).then_inc(w8_ready, 1)
                    dve.wait_ge(w8_ready, i + 1)
                    for r in range(ROWS):
                        dve.wait_ge(row_in[r], 16 * i + 16 * (GROUPS + 1))
                        dve.wait_ge(row_used, ROWS * i + (ROWS * GROUPS + r - 1))
                        y = (y_acc, y_alt)[r % 2][t]
                        V.scalar_tensor_tensor(out=y, in0=row[r], scalar=now[:, r:r + 1], in1=y, op0=ALU.mult,
                                               op1=ALU.add).then_inc(row_used, 1)
                    dve.wait_ge(row_used, ROWS * i + ROWS * (GROUPS + 1))
            dve.wait_ge(row_ready, 12)
            for t in range(NT):
                step(V.tensor_tensor(y_acc[t], y_acc[t], y_alt[t], ALU.add))
            step.wait()
            for t in range(NT):
                step(V.tensor_tensor(y_acc[t], y_acc[t], gate_row[:, :], ALU.mult))
            step.wait()
            for t in range(NT):
                ins = V.tensor_tensor(x_sb[:, t, :], x_sb[:, t, :], y_acc[t], ALU.add)
                if t == 0:
                    step(ins)
            step.wait()
            ins.then_inc(res_done, 1)
            r = rstd(6, 1)
            dve.wait_ge(final_in, 16)
            dve.wait_ge(res_done, 4)
            for t in range(NT):
                V.scalar_tensor_tensor(out=xn[:, t, :], in0=x_sb[:, t, :], scalar=r[:, t:t + 1], in1=final_row,
                                       op0=ALU.mult, op1=ALU.mult).then_inc(out_ready, 1)


def _cols(v):
    return np.asarray(v).reshape(-1, P).T


def _t_units(w):
    w = w.reshape(KC, P, -1, 2, P).transpose(2, 1, 3, 0, 4)
    return w.reshape(w.shape[0], P, UNIT)


def _m_units(w):
    n = w.shape[1] // 512
    return w.reshape(2, 4, P, n, 512).transpose(3, 0, 2, 1, 4).reshape(2 * n, P, UNIT)


def _out_units(w):
    k = w.shape[0] // P
    per = UNIT // (k * P)
    return w.reshape(k, P, KC // per, per, P).transpose(2, 1, 3, 0, 4).reshape(KC // per, P, UNIT)


def _constants():
    p, c = np.arange(P)[:, None], np.arange(P)[None, :]
    key, wide = np.arange(P)[:, None], np.arange(T)[None, :]
    strict = np.concatenate([key < wide, key < np.arange(P)[None, :]], 1)
    loose = np.concatenate([key <= wide, key <= np.arange(P)[None, :]], 1)
    dist = np.concatenate([p - c, P + p - wide], 1)
    count = np.zeros(dist.shape)
    for w, d in ((128, 1), (512, 4), (2048, 16)):
        count += (dist >= 0) & (dist <= w) & (dist % d == 0)
    band = np.zeros((P, NT, 4, T))
    t = np.arange(T)
    for g, w in enumerate((2, 4, 8, 16)):
        for n in range(NT):
            s = n * P + np.arange(P)[:, None]
            band[:, n, g, :] = ((s <= t) & (s > t - w)) / np.minimum(t + 1.0, w) - (s == t)
    return {
        "ident": p == c, "tri": p <= c, "ones": np.ones((P, P)), "suffix": p >= c,
        "sb_keep": np.where(strict, -1.0, 0.0), "sb_bias": np.where(strict, 0.0, NEG),
        "ssm_bias": np.where(loose, 0.0, NEG), "dist": np.where(dist >= 0, dist, -NEG), "count": count,
        "iota": np.broadcast_to(np.arange(TOPK), (P, TOPK)),
    }, band.reshape(P, -1)


def kernel(**inputs):
    import concourse.bacc as bacc
    from concourse.bass_utils import run_bass_kernel_spmd

    f = {k: np.asarray(v) for k, v in inputs.items()}
    for name in ("mod_w", "mod_b", "g_pre_mix", "g_post_mix", "g_pre_ffn", "g_post_ffn", "w_in", "sc_conv_w",
                 "ssm_conv_w", "ssm_conv_b", "ssm_dt_bias", "ssm_a_log", "ssm_d", "ssm_norm_w", "w_sc_out",
                 "w_sb_out", "w_ssm_out", "w_o", "w_ffn_in", "w_ffn_out", "w_ada_2", "b_ada_2", "norm1_g_2",
                 "w_in_2", "pool_w_2", "pool_scale_2", "w_out_2", "norm2_g_2", "peer_wq_2", "peer_subkeys_2",
                 "peer_u_2", "peer_v_2"):
        f[name] = f[name][0]
    w_in = f["w_in"]
    at = np.cumsum([0, 768, 256, 256, 256, 512, 768, 8, 3072])
    part = {n: w_in[:, at[i]:at[i + 1]] for i, n in enumerate(("sc", "q", "k", "v", "z", "xbc", "dt", "gl"))}
    hidden = FB * P
    gu = f["w_ffn_in"].reshape(KC, P, 2, FB, P).transpose(3, 1, 2, 0, 4).reshape(FB, P, UNIT)
    w2 = f["w_in_2"]
    kinds = {
        "mv": np.concatenate([_t_units(f["mod_w"]), _t_units(f["w_ada_2"])]),
        "xbc": _t_units(part["xbc"]), "sc": _t_units(part["sc"]),
        "qk": np.concatenate([_t_units(part["q"]), _t_units(part["k"])]),
        "v": part["v"].reshape(KC, P, T).transpose(1, 0, 2).reshape(1, P, UNIT),
        "z": _t_units(part["z"]), "gl": _t_units(part["gl"]),
        "sco": _out_units(f["w_sc_out"]), "sbo": _out_units(f["w_sb_out"]), "sso": _out_units(f["w_ssm_out"]),
        "wo": _m_units(f["w_o"]), "gu": gu,
        "dn": f["w_ffn_out"].reshape(PAIRS, 2, P, D).transpose(0, 2, 1, 3).reshape(PAIRS, P, UNIT),
        "qk2": _t_units(w2[:, 0:1024]), "v2": _m_units(w2[:, 1024:1536]), "u2": _m_units(w2[:, 1536:2048]),
        "wo2": _m_units(f["w_out_2"]), "wq": _t_units(f["peer_wq_2"]),
    }
    assert hidden == f["w_ffn_out"].shape[0]
    stream = np.stack([kinds[kind][j] for kind, j in ORDER])
    consts, band = _constants()
    pieces = {
        "c": _cols(f["c"]), "c2": _cols(f["c_2"]),
        "mod_b": np.concatenate([_cols(f["mod_b"]), _cols(f["b_ada_2"])], 1),
        "g_pre_mix": _cols(f["g_pre_mix"]), "g_pre_ffn": _cols(f["g_pre_ffn"]),
        "g_post_mix": _cols(f["g_post_mix"]), "g_post_ffn": _cols(f["g_post_ffn"]),
        "norm1": _cols(f["norm1_g_2"]), "norm2": _cols(f["norm2_g_2"]), "ssm_b": _cols(f["ssm_conv_b"]),
        "ssm_w": f["ssm_conv_w"].reshape(4, 6, P).transpose(2, 1, 0).reshape(P, 24),
        "sc_w": f["sc_conv_w"].reshape(3, 2, P).transpose(2, 1, 0).reshape(P, 6),
        "ssm_norm": _cols(f["ssm_norm_w"]), "pool_scale": _cols(f["pool_scale_2"]),
        "ssm_d": _cols(np.repeat(f["ssm_d"], 64)),
        "dt_b": np.broadcast_to(f["ssm_dt_bias"], (P, 8)), "a_log": np.broadcast_to(f["ssm_a_log"], (P, 8)),
        "w_dt": part["dt"].reshape(KC, P, 8).transpose(1, 0, 2).reshape(P, 64),
        "pool_w": f["pool_w_2"].transpose(1, 0, 2).reshape(P, 512),
        "keys": f["peer_subkeys_2"].transpose(2, 0, 1).reshape(P, 256),
        **consts,
    }
    small = np.concatenate([np.asarray(pieces[n], dtype=np.float32) for n in SMALL], 1)
    arrays = {
        "stream": stream, "small": small,
        "x": np.ascontiguousarray(f["x"].reshape(NT, P, D).transpose(1, 0, 2)),
        "band": band.astype(np.float32), "final_g": np.ascontiguousarray(np.broadcast_to(f["final_g_2"], (P, D))),
        "expert_u": f["peer_u_2"], "expert_v": f["peer_v_2"],
    }
    nc = bacc.Bacc("TRN2", target_bir_lowering=False, num_devices=1)
    args = [nc.dram_tensor(f"in_{n}", a.shape, mybir.dt.from_np(a.dtype), kind="ExternalInput").ap()
            for n, a in arrays.items()]
    out = nc.dram_tensor("out", (T, D), F32, kind="ExternalOutput").ap()
    build(nc, *args, out)
    r = run_bass_kernel_spmd(nc, [{f"in_{n}": a for n, a in arrays.items()}], core_ids=[0])
    return r.results[0]["out"].reshape(1, T, D)
```

```python
from contextlib import ExitStack

import numpy as np

import concourse.bass as bass
from concourse import mybir

ALU = mybir.AluOpType
ACT = mybir.ActivationFunctionType
F32 = mybir.dt.float32
U32 = mybir.dt.uint32
X = mybir.AxisListType.X

P = 128
D = 1024
T = 256
NT = T // P
KC = D // P
UNIT = 2048
RING = 3
FB = 22
PAIRS = FB // 2
HEADS = 8
TOPK = 16
SLOTS = HEADS * TOPK
ROWS = 16
GROUPS = NT * SLOTS // ROWS
EPS = 1e-6
NEG = -1e30

ORDER = [("xbc", j) for j in range(3)] + [("sc", j) for j in range(3)] + [("qk", 0), ("qk", 1), ("v", 0)]
ORDER += [("z", 0), ("z", 1)] + [("gl", j) for j in range(12)]
ORDER += [("br", j) for j in range(4)] + [("wo", j) for j in range(4)]
ORDER += [("gu", 0), ("gu", 1)]
for _i in range(1, PAIRS):
    ORDER += [("gu", 2 * _i), ("dn", _i - 1), ("gu", 2 * _i + 1)]
ORDER += [("dn", PAIRS - 1)]
ORDER += [("qk2", j) for j in range(4)] + [("v2", 0), ("v2", 1), ("u2", 0), ("u2", 1)]
ORDER += [("wo2", j) for j in range(4)] + [("wq", j) for j in range(8)]
AT = {name: n for n, name in enumerate(ORDER)}
UNITS = len(ORDER)


ROUTE_STEPS = 5 * 4 + 1 + 5 * NT + 5 * 2
MODS = 48
MOD_READS = [8, 20, 48]


def DONE(kind, j):
    return AT[kind, j] + 1


SMALL = {}
_at = 0
for _name, _n in (("c", 8), ("c2", 8), ("mod_b", 96), ("g_pre_mix", 8), ("g_pre_ffn", 8), ("g_post_mix", 8),
                  ("g_post_ffn", 8), ("norm1", 8), ("norm2", 8), ("ssm_b", 6), ("ssm_w", 24), ("sc_w", 6),
                  ("ssm_norm", 4), ("pool_scale", 4), ("ssm_d", 4), ("dt_b", 8), ("a_log", 8), ("w_dt", 64),
                  ("pool_w", 512), ("keys", 256), ("ident", P), ("tri", P), ("ones", P), ("suffix", P),
                  ("sb_keep", 384), ("sb_bias", 384), ("ssm_bias", 384), ("dist", 384), ("count", 384),
                  ("iota", TOPK)):
    SMALL[_name] = (_at, _at + _n)
    _at += _n
SMALL_N = _at


def build(nc, stream, mod_w, small, x, band, final_g, expert_u, expert_v, out):
    with ExitStack() as ctx:
        def sb(name, n, dt=F32):
            return ctx.enter_context(nc.sbuf_tensor(name, [P, n], dt))

        def sem(name):
            return ctx.enter_context(nc.semaphore(name))

        def cut(t, at, *dims):
            n = int(np.prod(dims))
            v = t[:, at:at + n]
            if len(dims) == 2:
                return v.rearrange("p (a b) -> p a b", a=dims[0])
            if len(dims) == 3:
                return v.rearrange("p (a b c) -> p a b c", a=dims[0], b=dims[1])
            return v

        ring = sb("ring", RING * UNIT)
        mod_ring = sb("mod_ring", 2 * UNIT)
        gate_area = sb("gate_area", 24 * T)
        mod_sum = sb("mod_sum", 2 * T)
        areaA = sb("areaA", 8214)
        areaB = sb("areaB", 9728)
        sm = sb("small", SMALL_N)
        x_sb = sb("x_sb", NT * D)[:, :].rearrange("p (t d) -> p t d", t=NT)
        xn = sb("xn", NT * D)[:, :].rearrange("p (t d) -> p t d", t=NT)
        hT = sb("hT", KC * T)[:, :].rearrange("p (k t) -> p k t", k=KC)
        mT_flat = sb("mT", KC * T)
        mT = mT_flat[:, :].rearrange("p (k t) -> p k t", k=KC)
        diag = sb("diag", D)
        gate_row = sb("gate_row", D)
        scale_row = areaB[:, 6144:7168]
        shift_row = areaB[:, 7168:8192]
        modT = sb("modT", 96)
        cols = sb("cols", 64)
        stat = sb("stat", 64)
        dtb = sb("dtb", 192)

        ps = ctx.enter_context(nc.psum_tensor("ps", [P, 8, 512], F32))
        BM, BX = 2, 7
        B3 = 3

        def c_(name, a=0, b=None):
            lo, hi = SMALL[name]
            return sm[:, lo + a:(hi if b is None else lo + b)]

        slot = [cut(ring, s * UNIT, UNIT) for s in range(RING)]
        gates = cut(gate_area, 0, 24, T)
        row = ([cut(gate_area, r * D, D) for r in range(6)] + [cut(mod_ring, r * D, D) for r in range(4)]
               + [cut(areaB, r * D, D) for r in range(6)])

        xbc_raw = cut(areaA, 0, 6, T + 3)
        xbc = cut(areaA, 1554, 6, T)
        sc = cut(areaA, 3090, 6, T)
        cx = cut(areaA, 4626, 2, T + 2)
        ya = cut(areaA, 5142, 2, T)
        qk = cut(areaA, 5654, 4, T)
        v1 = cut(areaA, 6678, NT, T)
        zg = cut(areaA, 7190, 4, T)
        sbl = cut(areaB, 0, 4, 384)
        sba = cut(areaB, 1536, 4, 384)
        decay = cut(areaB, 3072, 8, 384)
        a_rep = cut(areaB, 6144, 16, P)
        x_tok = cut(areaB, 8192, NT, 512)
        yb = cut(areaB, 9216, 2, T)
        yc = cut(areaB, 0, 4, T)
        ysq = cut(areaB, 1536, 4, T)
        prod = [cut(areaB, 3072 + 512 * n, 2, T) for n in range(6)]
        sg = cut(areaB, 0, 2, T)
        hid = cut(areaB, 512, 2, T)
        qk2 = cut(areaA, 0, 8, T)
        v2 = cut(areaA, 2048, NT, 512)
        u2 = cut(areaA, 3072, NT, 512)
        band_sb = cut(areaA, 4096, NT, 4, T)
        pooled = cut(areaA, 6144, 4, T)
        pexp = cut(areaB, 0, 4, 384)
        pnrm = cut(areaB, 1536, 4, 384)
        pT = cut(areaB, 3072, 4, 384)
        score = cut(areaA, 0, 512)
        rest = cut(areaA, 1024, 4, P)
        cand = cut(areaA, 1536, NT, 256)
        cand_rest = cut(areaA, 2048, NT, 256)
        onehot = [cut(areaA, 512, NT * TOPK, TOPK), cut(areaA, 2560, NT * TOPK, TOPK)]
        qh = cut(areaA, 3072, 2, 512)
        y_acc = [cut(areaA, 4096, D), cut(areaA, 5120, D)]
        y_alt = [cut(areaA, 6144, D), cut(areaA, 7168, D)]
        final_row = diag[:, :]
        sv = cut(mT_flat, 0, 4, TOPK)
        si = cut(mT_flat, 64, 4, TOPK).bitcast(U32)
        sif = cut(mT_flat, 128, 4, TOPK)
        tv = cut(mT_flat, 192, NT, TOPK)
        ti = cut(mT_flat, 224, NT * TOPK).bitcast(U32)
        tr = [cut(mT_flat, 256, NT * TOPK).bitcast(U32), cut(mT_flat, 416, NT * TOPK).bitcast(U32)]
        pos_f = [cut(mT_flat, 288, NT * TOPK), cut(mT_flat, 320, NT * TOPK)]
        pick = [cut(mT_flat, 352, NT * TOPK), cut(mT_flat, 384, NT * TOPK)]
        idx = sb("idx", NT * SLOTS, U32)
        idx_now = sb("idx_now", ROWS, U32)
        gate = sb("gate", NT * SLOTS)
        dots = sb("dots", NT * SLOTS)
        now = sb("now", NT * ROWS)[:, :].rearrange("p (t r) -> p t r", t=NT)

        small_in, x_in, band_in, final_in = sem("small_in"), sem("x_in"), sem("band_in"), sem("final_in")
        w_in = [sem(f"w_in{s}") for s in range(RING)]
        unit_done = sem("unit_done")
        dve_step, act_step = sem("dve_step"), sem("act_step")
        c_silu = sem("c_silu")
        sq_sum, mean_sq, root = sem("sq_sum"), sem("mean_sq"), sem("root")
        xn_ready, x_T, col_ready, hT_act, hT_dve = (sem("xn_ready"), sem("x_T"), sem("col_ready"), sem("hT_act"),
                                                    sem("hT_dve"))
        evac = sem("evac")
        diag_ready, row_mm, row_ready = sem("diag_ready"), sem("row_mm"), sem("row_ready")
        dt_mm, dt_lin, dt_exp, dt_one, dt_log, a_exp, a_ready = (
            sem("dt_mm"), sem("dt_lin"), sem("dt_exp"), sem("dt_one"), sem("dt_log"), sem("a_exp"), sem("a_ready"))
        conv_done, xbc_ready = sem("conv_done"), sem("xbc_ready")
        sb_z, sb_log, sb_lk, sb_sum, sb_arg, sb_att, sb_out, sb_y = (
            sem("sb_z"), sem("sb_log"), sem("sb_lk"), sem("sb_sum"), sem("sb_arg"), sem("sb_att"), sem("sb_out"),
            sem("sb_y"))
        acs_mm, dec_arg, dec_exp, xs_T, x_tok_ready, bc_mm, w_ready, y_mm = (
            sem("acs_mm"), sem("dec_arg"), sem("dec_exp"), sem("xs_T"), sem("x_tok_ready"), sem("bc_mm"),
            sem("w_ready"), sem("y_mm"))
        ysq_ready, ysum_mm, yms, yroot, yc_ready, ya_ready = (
            sem("ysq_ready"), sem("ysum_mm"), sem("yms"), sem("yroot"), sem("yc_ready"), sem("ya_ready"))
        merged = sem("merged")
        res_done = sem("res_done")
        silu_done, hid_ready = sem("silu_done"), sem("hid_ready")
        at_s, at_max, at_exp, at_p, at_T, at_pT, at_pv, at_o = (
            sem("at_s"), sem("at_max"), sem("at_exp"), sem("at_p"), sem("at_T"), sem("at_pT"), sem("at_pv"),
            sem("at_o"))
        at_read = sem("at_read")
        pool_mm, pool_ev, pool_out, pool_y = sem("pool_mm"), sem("pool_ev"), sem("pool_out"), sem("pool_y")
        s_mm, s_ready = sem("s_mm"), sem("s_ready")
        top_v, top_exp, idx_ready = sem("top_v"), sem("top_exp"), sem("idx_ready")
        row_in = [sem(f"row_in{r}") for r in range(ROWS)]
        row_used, idx_copied, pool_go, dots_out, gelu_done, w8_ready = (
            sem("row_used"), sem("idx_copied"), sem("pool_go"), sem("dots_out"), sem("gelu_done"), sem("w8_ready"))
        gate_ready = sem("gate_ready")
        out_ready, out_done = sem("out_ready"), sem("out_done")

        mod_in = [sem("mod_in0"), sem("mod_in1")]
        mod_summed, mod_used, mod_read = sem("mod_summed"), sem("mod_used"), sem("mod_read")
        mod_step = sem("mod_step")
        top_done = sem("top_done")
        dve_go = sem("dve_go")
        route_step = sem("route_step")
        acs_col_mm, acs_read = sem("acs_col_mm"), sem("acs_read")

        class Steps:

            def __init__(self, eng, s):
                self.eng, self.s, self.n = eng, s, 0

            def __call__(self, ins):
                ins.then_inc(self.s, 1)
                self.n += 1

            def wait(self, back=0):
                self.eng.wait_ge(self.s, self.n - back)

        block = ctx.enter_context(nc.Block())

        @block.sync
        def _(sp):
            sp.dma_start(sm[:, :], small).then_inc(small_in, 16)
            sp.dma_start(x_sb, x).then_inc(x_in, 16)
            sp.wait_ge(mod_summed, 4)
            for s in range(RING):
                sp.dma_start(slot[s], stream[s]).then_inc(w_in[s], 16)
            with sp.Fori(1, UNITS // RING) as i:
                for s in range(RING):
                    sp.wait_ge(unit_done, RING * i + (s - RING + 1))
                    sp.dma_start(slot[s], stream[bass.ds(RING * i + s, 1)].rearrange("o p n -> p (o n)"))\
                        .then_inc(w_in[s], 16)
            for t in range(NT):
                sp.wait_ge(out_ready, t + 1)
                sp.dma_start(out[t * P:(t + 1) * P, :], xn[:, t, :]).then_inc(out_done, 16)
            sp.wait_ge(out_done, 16 * NT)

        @block.tensor
        def _(pe):
            mm = nc.tensor.matmul

            def arrived(kind, j):
                u = AT[kind, j]
                pe.wait_ge(w_in[u % RING], 16 * (u // RING + 1))
                return slot[u % RING]

            def mod_sum_over_partitions(m, columns=None):
                for b in range(2):
                    o = columns[b] if columns else ps[:, BM, 2 * m + b:2 * m + b + 1]
                    last = mm(o, mod_sum[:, T * (m % 2) + b * P:T * (m % 2) + (b + 1) * P], c_("ones", 0, 1),
                              start=True, stop=True)
                last.then_inc(mod_used, 1)

            def mod_units(*ms):
                for m in ms:
                    pe.wait_ge(mod_summed, m + 1)
                    if m in MOD_READS:
                        pe.wait_ge(mod_read, MOD_READS.index(m) + 1)
                    mod_sum_over_partitions(m)

            def gemm_T(w, bank, rhs):
                for b in range(2):
                    for k in range(KC):
                        at = (b * KC + k) * P
                        last = mm(ps[:, bank, b * T:(b + 1) * T], w[:, at:at + P], rhs[:, k, :],
                                  start=(k == 0), stop=(k == KC - 1))
                return last

            evacs = [0]

            def bank_free():
                n = evacs[0]
                evacs[0] += 1
                if n >= 2:
                    pe.wait_ge(evac, n - 1)
                return n % 2

            def proj_T(kind, j):
                w = arrived(kind, j)
                gemm_T(w, bank_free(), hT).then_inc(unit_done, 1)

            def transposes(n):
                for k in range(KC):
                    for t in range(NT):
                        if k == 0:
                            pe.wait_ge(xn_ready, NT * n + t + 1)
                        last = nc.tensor.transpose(ps[:, B3 + k // 2, (k % 2) * T + t * P:(k % 2) * T + (t + 1) * P],
                                                   xn[:, t, k * P:(k + 1) * P], c_("ident"))
                    if k % 2:
                        last.then_inc(x_T, 1)

            def hT_wait(n):
                pe.wait_ge(hT_act, 4 * n + 4)
                pe.wait_ge(hT_dve, 4 * n + 4)

            def broadcast_row(n):
                for h in range(2):
                    pe.wait_ge(diag_ready, n + 1)
                    if 2 * n + h > 0:
                        pe.wait_ge(row_ready, 2 * n + h)
                    mm(ps[:, BX, :], c_("ones"), diag[:, 512 * h:512 * h + 512], start=True, stop=True)\
                        .then_inc(row_mm, 1)

            def wide(kind, j, lhs, n_from_0=None):
                w = arrived(kind, j)
                bank = B3 + 2 * (j // 2)
                for t in range(NT):
                    for k in range(4):
                        kk = 4 * (j % 2) + k
                        last = mm(ps[:, bank + t, :], lhs[:, kk, t * P:(t + 1) * P], w[:, 512 * k:512 * k + 512],
                                  start=(kk == 0), stop=(kk == KC - 1))
                last.then_inc(unit_done, 1)

            pe.wait_ge(small_in, 16)
            mod_units(*range(8))
            transposes(0)
            hT_wait(0)
            for j in range(3):
                proj_T("xbc", j)
            for t in range(NT):
                for k in range(KC):
                    last = mm(ps[:, BX, 8 * t:8 * t + 8], hT[:, k, t * P:(t + 1) * P],
                              c_("w_dt", 8 * k, 8 * k + 8), start=(k == 0), stop=(k == KC - 1))
            last.then_inc(dt_mm, 1)
            for j in range(3):
                proj_T("sc", j)
            for j in range(2):
                proj_T("qk", j)
            w = arrived("v", 0)
            bank = bank_free()
            for t in range(NT):
                for k in range(KC):
                    last = mm(ps[:, bank, t * T:(t + 1) * T], hT[:, k, t * P:(t + 1) * P], w[:, k * T:(k + 1) * T],
                              start=(k == 0), stop=(k == KC - 1))
            last.then_inc(unit_done, 1)

            def sb_scores(h, part, stop):
                r = slice(64 * (h % 2), 64 * (h % 2) + 64)
                q, k = qk[r, h // 2, :], qk[r, 2 + h // 2, :]
                if part == 0:
                    return mm(ps[:, B3 + h, 0:T], k[:, 0:P], q[:, :], start=True, stop=stop)
                return mm(ps[:, B3 + h, T:T + P], k[:, P:T], q[:, P:T], start=True, stop=stop)

            mod_units(8, 9)
            pe.wait_ge(evac, 8)
            for h in range(4):
                sb_scores(h, 0, True)
                last = sb_scores(h, 1, True)
            last.then_inc(sb_z, 1)
            for j in range(2):
                proj_T("z", j)
            mod_units(10, 11)
            for j in range(12):
                proj_T("gl", j)
                if j in (3, 7, 8, 9):
                    m = 12 + 2 * (3, 7, 8, 9).index(j)
                    mod_units(m, m + 1)
                if j == 2:
                    pe.wait_ge(sb_lk, 1)
                    for h in range(4):
                        sb_scores(h, 0, False)
                        mm(ps[:, B3 + h, P:T], c_("ones"), sbl[:, h, T:T + P], start=False, stop=False)
                        mm(ps[:, B3 + h, 0:T], c_("suffix"), sbl[:, h, 0:T], start=False, stop=True)
                        sb_scores(h, 1, False)
                        last = mm(ps[:, B3 + h, T:T + P], c_("suffix"), sbl[:, h, T:T + P], start=False, stop=True)
                    last.then_inc(sb_sum, 1)
                if j == 4:
                    for t in range(NT):
                        pe.wait_ge(xbc_ready, 6)
                        if t:
                            pe.wait_ge(x_tok_ready, t)
                        for b in range(4):
                            last = nc.tensor.transpose(ps[:, BX, b * P:(b + 1) * P], xbc[:, b, t * P:(t + 1) * P],
                                                       c_("ident"))
                        last.then_inc(xs_T, 1)
                if j == 5:
                    pe.wait_ge(a_ready, 1)
                    pe.wait_ge(x_tok_ready, NT)
                    acs = ps[:, BX, 0:16]
                    mm(acs[:, 0:8], c_("tri"), dtb[:, 16:24], start=True, stop=True)
                    mm(acs[:, 8:16], c_("ones"), dtb[:, 16:24], start=True, stop=False)
                    mm(acs[:, 8:16], c_("tri"), dtb[:, 24:32], start=False, stop=True).then_inc(acs_col_mm, 1)
                if j == 6:
                    pe.wait_ge(acs_read, 1)
                    pe.wait_ge(sb_att, 1)
                    pe.wait_ge(evac, 9)
                    for h in range(4):
                        r = slice(64 * (h % 2), 64 * (h % 2) + 64)
                        o = ps[r, BX, (h // 2) * T:(h // 2) * T + T]
                        mm(o, v1[:, 0, 64 * h:64 * h + 64], sba[:, h, 0:T], start=True, stop=True)
                        last = mm(o[:, P:T], v1[:, 1, 64 * h:64 * h + 64], sba[:, h, T:T + P], start=False, stop=True,
                                  skip_group_check=True)
                    last.then_inc(sb_out, 1)
                    pe.wait_ge(a_ready, 2)
                    lo = SMALL["tri"][0]
                    for h in range(8):
                        o = ps[:, B3 + h // 2, (h % 2) * T:(h % 2) * T + T]
                        mm(o, a_rep[:, h, :], sm[:, lo:lo + T], start=True, stop=True)
                        last = mm(o[:, P:T], a_rep[:, 8 + h, :], c_("tri"), start=False, stop=True,
                                  skip_group_check=True)
                    last.then_inc(acs_mm, 1)
            pe.wait_ge(evac, 23)
            for g in range(2):
                r = slice(64 * g, 64 * g + 64)
                mm(ps[:, g, 0:T], xbc[r, 4, 0:P], xbc[r, 5, :], start=True, stop=True)
                last = mm(ps[:, g, T:T + P], xbc[r, 4, P:T], xbc[r, 5, P:T], start=True, stop=True)
            last.then_inc(bc_mm, 1)
            pe.wait_ge(sb_y, 1)
            broadcast_row(0)
            pe.wait_ge(w_ready, 16)
            for h in range(8):
                r = slice(64 * (h % 2), 64 * (h % 2) + 64)
                b = h // 2
                o = ps[r, B3 + b // 2, (b % 2) * T:(b % 2) * T + T]
                mm(o, x_tok[:, 0, 64 * h:64 * h + 64], decay[:, h, 0:T], start=True, stop=True)
                last = mm(o[:, P:T], x_tok[:, 1, 64 * h:64 * h + 64], decay[:, h, T:T + P], start=False, stop=True,
                          skip_group_check=True)
            last.then_inc(y_mm, 1)
            pe.wait_ge(ysq_ready, 1)
            pe.wait_ge(row_ready, 2)
            for g in range(2):
                for b in range(2):
                    last = mm(ps[:, BX, g * T:(g + 1) * T], c_("ones"), ysq[:, 2 * g + b, :], start=(b == 0),
                              stop=(b == 1))
            last.then_inc(ysum_mm, 1)

            pe.wait_ge(ya_ready, 1)
            pe.wait_ge(yc_ready, 1)
            for j in range(4):
                if j >= 2:
                    pe.wait_ge(merged, j - 1)
                w = arrived("br", j)
                banks = (3, 4, 5) if j % 2 == 0 else (6, 7, 0)
                at = 0
                for n, (y, kc) in enumerate(((ya, 2), (yb, 2), (yc, 4))):
                    for b in range(2):
                        for k in range(kc):
                            last = mm(ps[:, banks[n], b * T:(b + 1) * T], w[:, at:at + P], y[:, k, :],
                                      start=(k == 0), stop=(k == kc - 1))
                            at += P
                last.then_inc(unit_done, 1)
            mod_units(20, 21)
            pe.wait_ge(merged, 4)
            for j in range(4):
                wide("wo", j, mT)
            mod_units(22, 23)

            transposes(1)
            hT_wait(1)

            def gate_up(j, bank):
                gemm_T(arrived("gu", j), bank, hT).then_inc(unit_done, 1)

            def down(w, first, final):
                for f in range(2):
                    for t in range(NT):
                        for n in range(2):
                            last = mm(ps[:, B3 + 2 * n + t, :], hid[:, f, t * P:(t + 1) * P],
                                      w[:, f * D + 512 * n:f * D + 512 * n + 512],
                                      start=(first and f == 0), stop=(final and f == 1), skip_group_check=True)
                last.then_inc(unit_done, 1)

            gate_up(0, 0)
            gate_up(1, 1)
            mod_units(24, 25)
            pe.wait_ge(hid_ready, 1)
            gate_up(2, 0)
            pe.wait_ge(hid_ready, 2)
            down(arrived("dn", 0), True, False)
            mod_units(26, 27)
            gate_up(3, 1)
            u0 = AT["gu", 4]
            with pe.Fori(2, PAIRS) as i:
                def slot_of(n):
                    s = (u0 + n) % RING
                    pe.wait_ge(w_in[s], 16 * (i + ((u0 + n) // RING - 1)))
                    return slot[s]

                w = slot_of(0)
                pe.wait_ge(hid_ready, 2 * i - 1)
                gemm_T(w, 0, hT).then_inc(unit_done, 1)
                for n in range(2):
                    pe.wait_ge(mod_summed, 2 * i + (25 + n))
                    mod_sum_over_partitions(n, [ps[:, BM, bass.ds(4 * i + (48 + 2 * n + b), 1)] for b in range(2)])
                w = slot_of(1)
                pe.wait_ge(hid_ready, 2 * i)
                down(w, False, False)
                w = slot_of(2)
                gemm_T(w, 1, hT).then_inc(unit_done, 1)
            mod_units(46, 47)
            pe.wait_ge(hid_ready, FB)
            pe.wait_ge(res_done, 1)
            broadcast_row(1)
            down(arrived("dn", PAIRS - 1), False, True)

            transposes(2)
            hT_wait(2)
            evacs[0] = 24
            for j in range(4):
                w = arrived("qk2", j)
                if j >= 2:
                    pe.wait_ge(evac, 23 + j - 1)
                gemm_T(w, j % 2, hT).then_inc(unit_done, 1)
            for kind, bank in (("v2", B3), ("u2", B3 + 2)):
                for j in range(2):
                    w = arrived(kind, j)
                    for t in range(NT):
                        for k in range(4):
                            kk = 4 * j + k
                            last = mm(ps[:, bank + t, :], hT[:, kk, t * P:(t + 1) * P], w[:, 512 * k:512 * k + 512],
                                      start=(kk == 0), stop=(kk == KC - 1))
                    last.then_inc(unit_done, 1)

            def att_scores(b):
                pe.wait_ge(evac, 31)
                if b:
                    pe.wait_ge(at_read, b)
                for n in range(4):
                    h = 4 * b + n
                    r = slice(64 * (h % 2), 64 * (h % 2) + 64)
                    q, k = qk2[r, h // 2, :], qk2[r, 4 + h // 2, :]
                    mm(ps[:, B3 + n, 0:P], q[:, 0:P], k[:, 0:P], start=True, stop=True)
                    last = mm(ps[:, B3 + n, P:384], q[:, P:T], k[:, :], start=True, stop=True)
                last.then_inc(at_s, 1)

            flat = ps[:, :, :].rearrange("p b n -> p (b n)")

            def att_transposes(b):
                pe.wait_ge(at_p, b + 1)
                if b == 0:
                    pe.wait_ge(pool_ev, 1)
                    pe.wait_ge(mod_read, 3)
                for n in range(4):
                    for m in range(3):
                        at = 384 * n + P * m
                        last = nc.tensor.transpose(flat[:, at:at + P], pnrm[:, n, P * m:P * m + P], c_("ident"))
                last.then_inc(at_T, 1)

            def att_values(b):
                pe.wait_ge(at_pT, b + 1)
                if b:
                    pe.wait_ge(at_o, b)
                else:
                    pe.wait_ge(row_ready, 6)
                for n in range(4):
                    h = 4 * b + n
                    r = slice(64 * (h % 2), 64 * (h % 2) + 64)
                    o = ps[r, BX, (n // 2) * T:(n // 2) * T + T]
                    mm(o, v2[:, 0, 64 * h:64 * h + 64], pT[:, n, 0:T], start=True, stop=True)
                    last = mm(o[:, P:T], v2[:, 1, 64 * h:64 * h + 64], pT[:, n, T:384], start=False, stop=True,
                              skip_group_check=True)
                last.then_inc(at_pv, 1)

            att_scores(0)
            pe.wait_ge(band_in, 16)
            for g in range(4):
                o = ps[:, g // 2, (g % 2) * T:(g % 2) * T + T]
                mm(o, u2[:, 0, g * P:(g + 1) * P], band_sb[:, 0, g, :], start=True, stop=True)
                last = mm(o[:, P:T], u2[:, 1, g * P:(g + 1) * P], band_sb[:, 1, g, P:T], start=False, stop=True,
                          skip_group_check=True)
            last.then_inc(pool_mm, 1)
            pe.wait_ge(res_done, 2)
            broadcast_row(2)
            att_transposes(0)
            att_scores(1)
            att_values(0)
            att_transposes(1)
            att_values(1)
            pe.wait_ge(at_pT, 2)
            for g in range(4):
                last = mm(ps[:, g // 2, (g % 2) * T:(g % 2) * T + T], c_("pool_w", g * P, (g + 1) * P),
                          pooled[:, g, :], start=True, stop=True)
            last.then_inc(pool_out, 1)
            pe.wait_ge(at_o, 2)
            pe.wait_ge(pool_y, 1)
            for j in range(4):
                wide("wo2", j, mT)
            for n in (3, 4):
                broadcast_row(n)
            transposes(3)
            hT_wait(3)

            def sub_scores(h):
                pe.wait_ge(evac, 31 + h + 1)
                if h >= 4:
                    pe.wait_ge(s_ready, h - 3)
                for t in range(NT):
                    for p in range(2):
                        last = mm(ps[:, B3 + h % 4, (2 * t + p) * P:(2 * t + p + 1) * P],
                                  qh[:, h % 2, p * T + t * P:p * T + (t + 1) * P], c_("keys", p * P, (p + 1) * P),
                                  start=True, stop=True)
                last.then_inc(s_mm, 1)

            for h in range(HEADS):
                w = arrived("wq", h)
                if h >= 2:
                    pe.wait_ge(evac, 31 + h - 1)
                gemm_T(w, h % 2, hT).then_inc(unit_done, 1)
                if h:
                    sub_scores(h - 1)
                else:
                    broadcast_row(5)
            sub_scores(HEADS - 1)

        @block.scalar
        def _(act):
            step = Steps(act, act_step)
            A = nc.scalar.activation

            def squares(n, source, outs):
                for m, (s, o) in enumerate(zip(source, outs)):
                    A(o, s, ACT.Square, accum_out=stat[:, 8 * (n % 4) + m:8 * (n % 4) + m + 1]).then_inc(sq_sum, 1)

            sq_n = [0]

            def square_root(n, w):
                act.wait_ge(mean_sq, n + 1)
                A(stat[:, 32 + 2 * (n % 8):32 + 2 * (n % 8) + w], stat[:, 48 + 2 * (n % 8):48 + 2 * (n % 8) + w],
                  ACT.Sqrt).then_inc(root, 1)

            def hT_part(n):
                for k in (0, 1, 4, 5):
                    act.wait_ge(x_T, KC // 2 * n + k // 2 + 1)
                    src = ps[:, B3 + k // 2, (k % 2) * T:(k % 2) * T + T]
                    if n < 3:
                        act.wait_ge(col_ready, (1, 3, 4)[n])
                        A(hT[:, k, :], src, ACT.Identity, scale=cols[:, 16 * n + k:16 * n + k + 1],
                          bias=cols[:, 16 * n + 8 + k:16 * n + 9 + k]).then_inc(hT_act, 1)
                    else:
                        A(hT[:, k, :], src, ACT.Identity).then_inc(hT_act, 1)

            def copy_out(kind, j, dst, func=ACT.Identity, scale=1.0, bank=0, w=512):
                act.wait_ge(unit_done, DONE(kind, j))
                src = ps[:, bank, :].rearrange("p (b t) -> p b t", b=2)
                A(dst, src, func, scale=scale).then_inc(evac, 1)

            def row_copy(n, dst):
                for h in range(2):
                    act.wait_ge(row_mm, 2 * n + h + 1)
                    A(dst[:, 512 * h:512 * h + 512], ps[:, BX, :], ACT.Identity).then_inc(row_ready, 1)

            act.wait_ge(small_in, 16)
            A(cols[:, 48:64], c_("c", 0, 16), ACT.Silu).then_inc(c_silu, 1)
            A(dtb[:, 32:40], c_("a_log"), ACT.Exp).then_inc(a_exp, 1)
            act.wait_ge(x_in, 16)
            squares(0, [x_sb[:, t, :] for t in range(NT)], [xn[:, t, :] for t in range(NT)])
            square_root(0, 2)
            hT_part(0)
            n = 0
            for j in range(3):
                copy_out("xbc", j, xbc_raw[:, 2 * j:2 * j + 2, 3:], bank=n % 2)
                n += 1
            for j in range(3):
                copy_out("sc", j, sc[:, 2 * j:2 * j + 2, :], bank=n % 2)
                n += 1
            act.wait_ge(dt_lin, 2)
            A(dtb[:, 64:80], dtb[:, 48:64], ACT.Exp, scale=-1.0).then_inc(dt_exp, 1)
            act.wait_ge(dt_one, 1)
            A(dtb[:, 96:112], dtb[:, 80:96], ACT.Ln).then_inc(dt_log, 1)
            for j in range(2):
                copy_out("qk", j, qk[:, 2 * j:2 * j + 2, :], scale=(0.125 if j == 0 else 1.0), bank=n % 2)
                n += 1
            copy_out("v", 0, v1, bank=n % 2)
            n += 1
            z4 = ps[:, B3:B3 + 4, 0:384]
            act.wait_ge(sb_z, 1)
            step(A(sbl, z4, ACT.Abs))
            step.wait()
            step(A(sbl, sbl, ACT.Exp, scale=-1.0))
            step.wait()
            A(sbl, sbl, ACT.Ln, bias=1.0).then_inc(sb_log, 1)
            for b in range(6):
                act.wait_ge(conv_done, b + 1)
                A(xbc[:, b, :], xbc[:, b, :], ACT.Silu, bias=c_("ssm_b", b, b + 1)).then_inc(xbc_ready, 1)
            for j in range(2):
                copy_out("z", j, zg[:, 2 * j:2 * j + 2, :], func=ACT.Silu, bank=n % 2)
                n += 1
            for j in range(12):
                copy_out("gl", j, gates[:, 2 * j:2 * j + 2, :], func=ACT.Sigmoid, bank=n % 2)
                n += 1
                if j == 4:
                    act.wait_ge(sb_arg, 1)
                    A(sba, sba, ACT.Exp).then_inc(sb_att, 1)
                    for t in range(NT):
                        act.wait_ge(xs_T, t + 1)
                        A(x_tok[:, t, :], ps[:, BX, :], ACT.Identity).then_inc(x_tok_ready, 1)
                if j == 8:
                    act.wait_ge(sb_out, 1)
                    A(yb, ps[:, BX, :].rearrange("p (b t) -> p b t", b=2), ACT.Identity).then_inc(sb_y, 1)
                if j == 10:
                    for hh in range(2):
                        act.wait_ge(dec_arg, 8 * hh + 8)
                        A(decay[:, 4 * hh:4 * hh + 4, :], decay[:, 4 * hh:4 * hh + 4, :], ACT.Exp)\
                            .then_inc(dec_exp, 1)
            row_copy(0, gate_row)
            act.wait_ge(yms, 1)
            A(ysq[:, 0:2, :], ysq[:, 0:2, :], ACT.Sqrt).then_inc(yroot, 1)
            act.wait_ge(unit_done, DONE("wo", 3))
            squares(1, [ps[:, B3 + b, :] for b in range(4)],
                    [xn[:, b % 2, 512 * (b // 2):512 * (b // 2) + 512] for b in range(4)])
            square_root(1, 2)
            act.wait_ge(res_done, 1)
            squares(2, [x_sb[:, t, :] for t in range(NT)], [xn[:, t, :] for t in range(NT)])
            square_root(2, 2)
            hT_part(1)
            for f in range(2):
                act.wait_ge(unit_done, DONE("gu", f))
                A(sg[:, f, :], ps[:, f, 0:T], ACT.Silu).then_inc(silu_done, 1)
            with act.Fori(1, PAIRS) as i:
                for f in range(2):
                    act.wait_ge(unit_done, 3 * i + (AT["gu", 2 + f] - 3 + 1))
                    act.wait_ge(hid_ready, 2 * i + (f - 1))
                    A(sg[:, f, :], ps[:, f, 0:T], ACT.Silu).then_inc(silu_done, 1)
            row_copy(1, gate_row)
            act.wait_ge(unit_done, DONE("dn", PAIRS - 1))
            squares(3, [ps[:, B3 + b, :] for b in range(4)],
                    [xn[:, b % 2, 512 * (b // 2):512 * (b // 2) + 512] for b in range(4)])
            square_root(3, 2)
            act.wait_ge(res_done, 2)
            squares(4, [x_sb[:, t, :] for t in range(NT)], [xn[:, t, :] for t in range(NT)])
            square_root(4, 2)
            hT_part(2)
            for j in range(4):
                copy_out("qk2", j, qk2[:, 2 * j:2 * j + 2, :], bank=j % 2)
            for kind, dst, bank in (("v2", v2, B3), ("u2", u2, B3 + 2)):
                act.wait_ge(unit_done, DONE(kind, 1))
                for t in range(NT):
                    A(dst[:, t, :], ps[:, bank + t, :], ACT.Identity).then_inc(evac, 1)

            def att_exp(b):
                act.wait_ge(at_max, b + 1)
                for n in range(4):
                    for t, (lo, hi) in enumerate(((0, P), (P, 384))):
                        A(pnrm[:, n, lo:hi], pexp[:, n, lo:hi], ACT.Exp, scale=0.125,
                          bias=stat[:, 4 * t + n:4 * t + n + 1]).then_inc(at_exp, 1)

            def pT_copy(b):
                act.wait_ge(at_T, b + 1)
                if b:
                    act.wait_ge(at_pv, b)
                A(pT, flat_ps[:, 0:1536].rearrange("p (a b) -> p a b", a=4), ACT.Identity).then_inc(at_pT, 1)

            def o_copy(b):
                act.wait_ge(at_pv, b + 1)
                A(mT[:, 2 * b:2 * b + 2, :], ps[:, BX, :].rearrange("p (b t) -> p b t", b=2), ACT.Identity)\
                    .then_inc(at_o, 1)

            flat_ps = ps[:, :, :].rearrange("p b n -> p (b n)")
            act.wait_ge(pool_mm, 1)
            A(pooled, flat_ps[:, 0:1024].rearrange("p (a b) -> p a b", a=4), ACT.Identity).then_inc(pool_ev, 1)
            row_copy(2, gate_row)
            att_exp(0)
            pT_copy(0)
            att_exp(1)
            o_copy(0)
            pT_copy(1)
            o_copy(1)
            act.wait_ge(pool_out, 1)
            for g in range(4):
                A(mT[:, 4 + g, :], flat_ps[:, g * T:(g + 1) * T], ACT.Identity,
                  scale=c_("pool_scale", g, g + 1)).then_inc(act_step if g < 3 else pool_y, 1)
            step.n += 3
            row_copy(3, scale_row)
            row_copy(4, shift_row)
            act.wait_ge(res_done, 3)
            squares(5, [x_sb[:, t, :] for t in range(NT)], [xn[:, t, :] for t in range(NT)])
            square_root(5, 2)
            hT_part(3)

            for h in range(HEADS + 1):
                if h < HEADS:
                    act.wait_ge(unit_done, DONE("wq", h))
                    if h >= 2:
                        act.wait_ge(s_mm, h - 1)
                    A(qh[:, h % 2, :], ps[:, h % 2, :], ACT.Identity).then_inc(evac, 1)
                if h == 0:
                    row_copy(5, gate_row)
                else:
                    act.wait_ge(s_mm, h)
                    if h >= 2:
                        act.wait_ge(top_done, h - 1)
                    A(score, ps[:, B3 + (h - 1) % 4, :], ACT.Identity).then_inc(s_ready, 1)
            act.wait_ge(top_v, HEADS)
            A(gate[:, :], gate[:, :], ACT.Exp).then_inc(top_exp, 1)
            act.wait_ge(dots_out, GROUPS)
            A(dots[:, :], dots[:, :], ACT.Gelu).then_inc(gelu_done, 1)
            act.wait_ge(res_done, 4)
            squares(6, [x_sb[:, t, :] for t in range(NT)], [xn[:, t, :] for t in range(NT)])
            square_root(6, 2)

        @block.gpsimd
        def _(pool):
            for n in range(2):
                pool.dma_start(cut(mod_ring, n * UNIT, UNIT), mod_w[n]).then_inc(mod_in[n], 16)

            def load_mods(m0, m1):
                with pool.Fori(m0 // 2, m1 // 2) as i:
                    for n in range(2):
                        pool.wait_ge(mod_summed, 2 * i + (n - 1))
                        pool.sem_inc(pool_go, 1)
                        pool.dma_start(cut(mod_ring, n * UNIT, UNIT),
                                       mod_w[bass.ds(2 * i + n, 1)].rearrange("o p n -> p (o n)"))\
                            .then_inc(mod_in[n], 16)

            load_mods(2, 24)
            pool.wait_ge(res_done, 1)
            pool.dma_start(cut(areaA, 4096, 2048), band).then_inc(band_in, 16)
            load_mods(24, MODS)
            pool.wait_ge(row_mm, 12)
            pool.dma_start(final_row[:, :], final_g).then_inc(final_in, 16)

            for table, n_pass in ((expert_u, 0), (expert_v, 1)):
                def gathers(half):
                    for r in range(8 * half, 8 * half + 8):
                        pool.indirect_dma_start(row[r], None, table, bass.IndirectOffsetOnAxis(
                            ap=idx_now[:, r:r + 1], axis=0)).then_inc(row_in[r], 16)

                if n_pass == 0:
                    pool.wait_ge(idx_ready, NT)
                    for half in range(2):
                        nc.gpsimd.tensor_copy(idx_now[:, 8 * half:8 * half + 8], idx[:, 8 * half:8 * half + 8])\
                            .then_inc(idx_copied, 1)
                        pool.wait_ge(idx_copied, half + 1)
                        gathers(half)
                done = n_pass * GROUPS
                with pool.Fori(1 - n_pass, GROUPS) as i:
                    if n_pass == 0:
                        pool.wait_ge(idx_ready, i + 1)
                        pool.sem_inc(pool_go, 1)
                    for half in range(2):
                        pool.wait_ge(row_used, ROWS * i + (ROWS * (done - 1) + 8 * half + 8))
                        pool.sem_inc(pool_go, 1)
                        nc.gpsimd.tensor_copy(idx_now[:, 8 * half:8 * half + 8],
                                              idx[:, bass.ds(ROWS * i + 8 * half, 8)]).then_inc(idx_copied, 1)
                        pool.wait_ge(idx_copied, 2 * i + (2 * done + half + 1))
                        pool.sem_inc(pool_go, 1)
                        gathers(half)

        @block.vector
        def _(dve):
            V = nc.vector
            step = Steps(dve, dve_step)

            def rstd(n, pieces):
                need = {0: 2, 1: 6, 2: 8, 3: 12, 4: 14, 5: 16, 6: 18}[n]
                dve.wait_ge(sq_sum, need)
                src = stat[:, 8 * (n % 4):8 * (n % 4) + 2]
                if pieces == 2:
                    step(V.tensor_tensor(stat[:, 8 * (n % 4) + 4:8 * (n % 4) + 6], src,
                                         stat[:, 8 * (n % 4) + 2:8 * (n % 4) + 4], ALU.add))
                    step.wait()
                    src = stat[:, 8 * (n % 4) + 4:8 * (n % 4) + 6]
                V.tensor_scalar(stat[:, 48 + 2 * (n % 8):50 + 2 * (n % 8)], src, 1.0 / D, EPS, ALU.mult, ALU.add)\
                    .then_inc(mean_sq, 1)
                dve.wait_ge(root, n + 1)
                r = stat[:, 32 + 2 * (n % 8):34 + 2 * (n % 8)]
                step(V.reciprocal(r, r))
                step.wait()
                return r

            def normalise(n, r):
                for t in range(NT):
                    V.tensor_scalar(xn[:, t, :], x_sb[:, t, :], r[:, t:t + 1], None, ALU.mult).then_inc(xn_ready, 1)

            def hT_part(n):
                if n < 3:
                    dve.wait_ge(col_ready, (1, 3, 4)[n])
                for k in (2, 3, 6, 7):
                    dve.wait_ge(x_T, KC // 2 * n + k // 2 + 1)
                    src = ps[:, B3 + k // 2, (k % 2) * T:(k % 2) * T + T]
                    if n < 3:
                        V.tensor_scalar(hT[:, k, :], src, cols[:, 16 * n + k:16 * n + k + 1],
                                        cols[:, 16 * n + 8 + k:16 * n + 9 + k], ALU.mult, ALU.add)\
                            .then_inc(hT_dve, 1)
                    else:
                        V.tensor_copy(hT[:, k, :], src).then_inc(hT_dve, 1)

            def mod_product(n, vec, arrived):
                dve.wait_ge(mod_in[n], arrived)
                w = cut(mod_ring, n * UNIT, KC, T)
                o = mod_sum[:, n * T:(n + 1) * T]
                for k in range(KC):
                    if k == 0:
                        ins = V.tensor_scalar(o, w[:, k, :], vec[:, k:k + 1], None, ALU.mult)
                    else:
                        ins = V.scalar_tensor_tensor(out=o, in0=w[:, k, :], scalar=vec[:, k:k + 1], in1=o,
                                                     op0=ALU.mult, op1=ALU.add)
                    if k < KC - 1:
                        yield ins
                ins.then_inc(mod_summed, 1)

            def mod_units(*ms):
                for m in ms:
                    if m == 0:
                        dve.wait_ge(c_silu, 1)
                    if m >= 2:
                        dve.wait_ge(mod_used, m - 1)
                    vec = cols[:, 48 + 8 * (m // 24):56 + 8 * (m // 24)]
                    for ins in mod_product(m % 2, vec, 16 * (m // 2 + 1)):
                        step(ins)
                        step.wait()

            def modulation(m0, m1):
                dve.wait_ge(mod_used, m1)
                V.tensor_tensor(modT[:, 2 * m0:2 * m1], ps[:, BM, 2 * m0:2 * m1], c_("mod_b", 2 * m0, 2 * m1),
                                ALU.add).then_inc(mod_read, 1)
                dve.wait_ge(mod_read, MOD_READS.index(m1) + 1)

            ident8 = c_("ident").unsqueeze(1).to_broadcast([P, 8, P])
            diag3 = diag[:, :].rearrange("p (k n) -> p k n", k=8)

            def spread(n, vec):
                if n:
                    dve.wait_ge(row_mm, 2 * n)
                V.tensor_tensor(diag3, ident8, vec.unsqueeze(2).to_broadcast([P, 8, P]), ALU.mult)\
                    .then_inc(diag_ready, 1)

            def residual(n, r, rows):
                dve.wait_ge(row_ready, rows)
                for b in range(4):
                    t, lo = b % 2, 512 * (b // 2)
                    src = ps[:, B3 + b, :]
                    if r is None:
                        step(V.tensor_tensor(xn[:, t, lo:lo + 512], src, gate_row[:, lo:lo + 512], ALU.mult))
                    else:
                        step(V.scalar_tensor_tensor(out=xn[:, t, lo:lo + 512], in0=src, scalar=r[:, t:t + 1],
                                                    in1=gate_row[:, lo:lo + 512], op0=ALU.mult, op1=ALU.mult))
                step.wait()
                for t in range(NT):
                    ins = V.tensor_tensor(x_sb[:, t, :], x_sb[:, t, :], xn[:, t, :], ALU.add)
                    if t == 0:
                        step(ins)
                step.wait()
                ins.then_inc(res_done, 1)

            step(V.memset(xbc_raw[:, :, 0:3], 0.0))
            step(V.memset(cx[:, :, 0:2], 0.0))
            dve.wait_ge(x_in, 16)
            dve.wait_ge(small_in, 16)
            mod_units(0, 1)
            normalise(0, rstd(0, 1))
            mod_units(*range(2, 8))
            modulation(0, 8)
            step(V.scalar_tensor_tensor(out=cols[:, 0:8], in0=modT[:, 8:16], scalar=1.0, in1=c_("g_pre_mix"),
                                        op0=ALU.add, op1=ALU.mult))
            step.wait()
            V.tensor_copy(cols[:, 8:16], modT[:, 0:8]).then_inc(col_ready, 1)
            dve.wait_ge(col_ready, 1)
            hT_part(0)

            for k in range(4):
                for b in range(6):
                    w = c_("ssm_w", 4 * b + k, 4 * b + k + 1)
                    if k == 0:
                        if b % 2 == 0:
                            dve.wait_ge(evac, b // 2 + 1)
                        step(V.tensor_scalar(xbc[:, b, :], xbc_raw[:, b, 0:T], w, None, ALU.mult))
                    else:
                        step.wait(5)
                        ins = V.scalar_tensor_tensor(out=xbc[:, b, :], in0=xbc_raw[:, b, k:k + T], scalar=w,
                                                     in1=xbc[:, b, :], op0=ALU.mult, op1=ALU.add)
                        if k < 3:
                            step(ins)
                        else:
                            ins.then_inc(conv_done, 1)
                if k == 2:
                    step.wait()
            dt, a, ea = dtb[:, 0:16], dtb[:, 16:32], dtb[:, 32:40]
            mag, e, u, l, lin = dtb[:, 48:64], dtb[:, 64:80], dtb[:, 80:96], dtb[:, 96:112], dtb[:, 112:128]
            dve.wait_ge(dt_mm, 1)
            step(V.tensor_tensor(lin.rearrange("p (t h) -> p t h", t=NT),
                                 ps[:, BX, 0:16].rearrange("p (t h) -> p t h", t=NT),
                                 c_("dt_b").unsqueeze(1).to_broadcast([P, NT, 8]), ALU.add))
            step.wait()
            V.scalar_tensor_tensor(out=mag, in0=lin, scalar=-1.0, in1=lin, op0=ALU.mult, op1=ALU.max)\
                .then_inc(dt_lin, 1)
            V.tensor_scalar(lin, lin, 0.0, None, ALU.max).then_inc(dt_lin, 1)
            dve.wait_ge(dt_exp, 1)
            V.tensor_scalar(u, e, 1.0, None, ALU.add).then_inc(dt_one, 1)
            dve.wait_ge(dt_one, 1)
            step(V.scalar_tensor_tensor(out=dtb[:, 128:144], in0=u, scalar=-1.0, in1=e, op0=ALU.add,
                                        op1=ALU.subtract))
            step(V.reciprocal(dtb[:, 144:160], u))
            step.wait()
            step(V.scalar_tensor_tensor(out=dtb[:, 160:176], in0=dtb[:, 128:144], scalar=-1.0, in1=dtb[:, 144:160],
                                        op0=ALU.mult, op1=ALU.mult))
            dve.wait_ge(dt_log, 1)
            dve.wait_ge(dt_lin, 2)
            step(V.tensor_tensor(lin, lin, l, ALU.add))
            step.wait()
            step(V.tensor_tensor(dt, lin, dtb[:, 160:176], ALU.add))
            step.wait()
            dve.wait_ge(a_exp, 1)
            V.scalar_tensor_tensor(out=a.rearrange("p (t h) -> p t h", t=NT),
                                   in0=dt.rearrange("p (t h) -> p t h", t=NT), scalar=-1.0,
                                   in1=ea.unsqueeze(1).to_broadcast([P, NT, 8]), op0=ALU.mult, op1=ALU.mult)\
                .then_inc(a_ready, 1)
            dve.wait_ge(a_ready, 1)
            V.tensor_copy(a_rep, a.unsqueeze(2).to_broadcast([P, 16, P])).then_inc(a_ready, 1)
            dve.wait_ge(evac, 6)
            step(V.tensor_tensor(cx[:, :, 2:], sc[:, 2:4, :], sc[:, 4:6, :], ALU.mult))
            step.wait()
            for k in range(3):
                for b in range(2):
                    w = c_("sc_w", 3 * b + k, 3 * b + k + 1)
                    if k == 0:
                        step(V.tensor_scalar(ya[:, b, :], cx[:, b, 0:T], w, None, ALU.mult))
                    else:
                        step.wait(1)
                        step(V.scalar_tensor_tensor(out=ya[:, b, :], in0=cx[:, b, k:k + T], scalar=w,
                                                    in1=ya[:, b, :], op0=ALU.mult, op1=ALU.add))
            step.wait()
            V.tensor_tensor(ya, ya, sc[:, 0:2, :], ALU.mult).then_inc(ya_ready, 1)
            mod_units(8, 9, 10, 11)
            z4 = ps[:, B3:B3 + 4, 0:384]
            dve.wait_ge(sb_log, 1)
            for h in range(4):
                step(V.scalar_tensor_tensor(out=sbl[:, h, :], in0=ps[:, B3 + h, 0:384], scalar=0.0,
                                            in1=sbl[:, h, :], op0=ALU.max, op1=ALU.add))
            step.wait()
            V.tensor_tensor(sbl, sbl, c_("sb_keep").unsqueeze(1).to_broadcast([P, 4, 384]), ALU.mult)\
                .then_inc(sb_lk, 1)
            mod_units(12, 13)
            dve.wait_ge(sb_sum, 1)
            V.tensor_tensor(sba, z4, c_("sb_bias").unsqueeze(1).to_broadcast([P, 4, 384]), ALU.add)\
                .then_inc(sb_arg, 1)
            dve.wait_ge(acs_col_mm, 1)
            V.tensor_copy(dtb[:, 176:192], ps[:, BX, 0:16]).then_inc(acs_read, 1)
            mod_units(14, 15)
            dve.wait_ge(acs_mm, 1)
            dve.wait_ge(acs_read, 1)
            for h in range(8):
                col = ps[:, B3 + h // 2, (h % 2) * T:(h % 2) * T + T]
                V.scalar_tensor_tensor(out=decay[:, h, 0:T], in0=col, scalar=dtb[:, 176 + h:177 + h],
                                       in1=c_("ssm_bias", 0, T), op0=ALU.subtract, op1=ALU.add).then_inc(dec_arg, 1)
                V.scalar_tensor_tensor(out=decay[:, h, T:384], in0=col[:, P:T], scalar=dtb[:, 184 + h:185 + h],
                                       in1=c_("ssm_bias", T, 384), op0=ALU.subtract, op1=ALU.add)\
                    .then_inc(dec_arg, 1)
            mod_units(16, 17, 18, 19)
            modulation(8, 20)
            step(V.tensor_tensor(modT[:, 16:24], modT[:, 16:24], c_("g_post_mix"), ALU.mult))
            step.wait()
            spread(0, modT[:, 16:24])
            step(V.scalar_tensor_tensor(out=cols[:, 16:24], in0=modT[:, 32:40], scalar=1.0, in1=c_("g_pre_ffn"),
                                        op0=ALU.add, op1=ALU.mult))
            V.tensor_copy(cols[:, 24:32], modT[:, 24:32]).then_inc(col_ready, 2)
            dve.wait_ge(bc_mm, 1)
            for h in range(8):
                if h % 4 == 0:
                    dve.wait_ge(dec_exp, h // 4 + 1)
                for t, (lo, hi) in enumerate(((0, T), (T, 384))):
                    V.scalar_tensor_tensor(out=decay[:, h, lo:hi], in0=decay[:, h, lo:hi],
                                           scalar=dt[:, 8 * t + h:8 * t + h + 1], in1=ps[:, h // 4, lo:hi],
                                           op0=ALU.mult, op1=ALU.mult).then_inc(w_ready, 1)
            dve.wait_ge(y_mm, 1)
            for b in range(4):
                step(V.scalar_tensor_tensor(out=yc[:, b, :], in0=xbc[:, b, :], scalar=c_("ssm_d", b, b + 1),
                                            in1=ps[:, B3 + b // 2, (b % 2) * T:(b % 2) * T + T],
                                            op0=ALU.mult, op1=ALU.add))
            step.wait()
            step(V.tensor_tensor(yc, yc, zg, ALU.mult))
            step.wait()
            V.tensor_tensor(ysq, yc, yc, ALU.mult).then_inc(ysq_ready, 1)
            dve.wait_ge(ysum_mm, 1)
            V.tensor_scalar(ysq[:, 0:2, :], ps[:, BX, :].rearrange("p (b t) -> p b t", b=2), 1.0 / (2 * P), EPS, ALU.mult,
                            ALU.add).then_inc(yms, 1)
            dve.wait_ge(yroot, 1)
            step(V.reciprocal(ysq[:, 0:2, :], ysq[:, 0:2, :]))
            step.wait()
            for b in range(4):
                ins = V.scalar_tensor_tensor(out=yc[:, b, :], in0=yc[:, b, :], scalar=c_("ssm_norm", b, b + 1),
                                             in1=ysq[:, b // 2, :], op0=ALU.mult, op1=ALU.mult)
                if b < 3:
                    step(ins)
            step.wait()
            ins.then_inc(yc_ready, 1)
            for j in range(4):
                dve.wait_ge(unit_done, DONE("br", j))
                if j == 0:
                    dve.wait_ge(evac, 23)
                banks = (3, 4, 5) if j % 2 == 0 else (6, 7, 0)
                pr = prod[3 * (j % 2):3 * (j % 2) + 3]
                for n in range(3):
                    step(V.tensor_tensor(pr[n], ps[:, banks[n], :].rearrange("p (b t) -> p b t", b=2),
                                         gates[:, 8 * n + 2 * j:8 * n + 2 * j + 2, :], ALU.mult))
                step.wait()
                step(V.tensor_tensor(pr[0], pr[0], pr[1], ALU.add))
                step.wait()
                V.tensor_tensor(mT[:, 2 * j:2 * j + 2, :], pr[0], pr[2], ALU.add).then_inc(merged, 1)
            mod_units(20, 21, 22, 23)
            residual(0, rstd(1, 2), 2)
            dve.wait_ge(res_done, 1)
            normalise(1, rstd(2, 1))
            hT_part(1)

            for f in range(2):
                dve.wait_ge(silu_done, f + 1)
                V.tensor_tensor(hid[:, f, :], sg[:, f, :], ps[:, f, T:2 * T], ALU.mult).then_inc(hid_ready, 1)
                mod_units(24 + f)
            mod_units(26, 27)
            with dve.Fori(1, PAIRS) as i:
                for f in range(2):
                    dve.wait_ge(silu_done, 2 * i + (f + 1))
                    dve.wait_ge(unit_done, 3 * i + (AT["dn", 0] - 3 + 1))
                    V.tensor_tensor(hid[:, f, :], sg[:, f, :], ps[:, f, T:2 * T], ALU.mult).then_inc(hid_ready, 1)
                    dve.wait_ge(mod_used, 2 * i + (25 + f))
                    own = 0
                    for ins in mod_product(f, cols[:, 56:64], 16 * i + 16 * 14):
                        ins.then_inc(mod_step, 1)
                        own += 1
                        dve.wait_ge(mod_step, 14 * i + (7 * f + own - 14))
            modulation(20, 48)
            step(V.tensor_tensor(modT[:, 40:48], modT[:, 40:48], c_("g_post_ffn"), ALU.mult))
            step(V.scalar_tensor_tensor(out=cols[:, 32:40], in0=modT[:, 56:64], scalar=1.0, in1=c_("norm1"),
                                        op0=ALU.add, op1=ALU.mult))
            step.wait()
            V.tensor_copy(cols[:, 40:48], modT[:, 48:56]).then_inc(col_ready, 1)
            spread(1, modT[:, 40:48])
            residual(1, rstd(3, 2), 4)
            dve.wait_ge(res_done, 2)
            normalise(2, rstd(4, 1))
            spread(2, modT[:, 64:72])
            hT_part(2)
            V.scalar_tensor_tensor(out=modT[:, 80:88], in0=modT[:, 80:88], scalar=1.0, in1=c_("norm2"),
                                   op0=ALU.add, op1=ALU.mult).then_inc(col_ready, 2)

            for b in range(2):
                dve.wait_ge(at_s, b + 1)
                if b:
                    dve.wait_ge(at_exp, 8)
                for n in range(4):
                    slope = 2.0 ** (-(4 * b + n + 1))
                    ins = V.scalar_tensor_tensor(out=pexp[:, n, :], in0=c_("dist"), scalar=-8.0 * slope,
                                                 in1=ps[:, B3 + n, 0:384], op0=ALU.mult, op1=ALU.add)
                    if n < 3:
                        step(ins)
                ins.then_inc(at_read, 1)
                step.wait()
                dve.wait_ge(at_read, b + 1)
                mx = stat[:, 0:8]
                step(V.tensor_reduce(stat[:, 8:12], pexp[:, :, 0:P], X, ALU.max))
                step(V.tensor_reduce(stat[:, 12:16], pexp[:, :, P:384], X, ALU.max))
                step.wait()
                V.tensor_scalar(mx, stat[:, 8:16], -0.125, None, ALU.mult).then_inc(at_max, 1)
                dve.wait_ge(at_exp, 8 * b + 8)
                if b:
                    dve.wait_ge(at_T, b)
                step(V.tensor_tensor(pnrm, pnrm, c_("count").unsqueeze(1).to_broadcast([P, 4, 384]), ALU.mult))
                step.wait()
                for t, (lo, hi) in enumerate(((0, P), (P, 384))):
                    step(V.tensor_reduce(stat[:, 16 + 4 * t:20 + 4 * t], pnrm[:, :, lo:hi], X, ALU.add))
                step.wait()
                step(V.reciprocal(stat[:, 16:24], stat[:, 16:24]))
                step.wait()
                for t, (lo, hi) in enumerate(((0, P), (P, 384))):
                    ins = V.tensor_tensor(pnrm[:, :, lo:hi], pnrm[:, :, lo:hi],
                                          stat[:, 16 + 4 * t:20 + 4 * t].unsqueeze(2).to_broadcast([P, 4, hi - lo]),
                                          ALU.mult)
                    if t == 0:
                        step(ins)
                step.wait()
                ins.then_inc(at_p, 1)
            dve.wait_ge(col_ready, 6)
            spread(3, modT[:, 80:88])
            spread(4, modT[:, 72:80])
            dve.wait_ge(unit_done, DONE("wo2", 3))
            residual(2, None, 6)
            dve.wait_ge(res_done, 3)
            spread(5, modT[:, 88:96])
            r = rstd(5, 1)
            dve.wait_ge(row_ready, 10)
            for t in range(NT):
                step(V.scalar_tensor_tensor(out=xn[:, t, :], in0=x_sb[:, t, :], scalar=r[:, t:t + 1],
                                            in1=scale_row[:, :], op0=ALU.mult, op1=ALU.mult))
            step.wait()
            for t in range(NT):
                V.tensor_tensor(xn[:, t, :], xn[:, t, :], shift_row[:, :], ALU.add).then_inc(xn_ready, 1)
            hT_part(3)

            n_step = [0]

            def own(ins):
                ins.then_inc(route_step, 1)
                n_step[0] += 1

            def top16(h, values, spare, out_v, out_i):
                lists = range(len(values))
                for q in lists:
                    own(V.max(out_v[q][:, 0:8], values[q]))
                settled(h)
                carry()
                for q in lists:
                    own(V.max_index(out_i[q][:, 0:8], out_v[q][:, 0:8], values[q]))
                for q in lists:
                    own(V.match_replace(spare[q], out_v[q][:, 0:8], values[q], -3e38))
                settled(h)
                carry()
                for q in lists:
                    own(V.max(out_v[q][:, 8:16], spare[q]))
                settled(h)
                carry()
                for q in lists:
                    own(V.max_index(out_i[q][:, 8:16], out_v[q][:, 8:16], spare[q]))
                settled(h)

            def settled(h):
                dve.wait_ge(route_step, h * ROUTE_STEPS + n_step[0])

            def carry():
                dve.sem_inc(dve_go, 1)

            def route(h):
                n_step[0] = 0
                dve.wait_ge(s_ready, h + 1)
                carry()
                sc4 = score.rearrange("p (q n) -> p q n", q=4)
                top16(h, [sc4[:, q, :] for q in range(4)], [rest[:, q, :] for q in range(4)],
                      [sv[:, q, :] for q in range(4)], [si[:, q, :] for q in range(4)])
                V.tensor_copy(sif, si).then_inc(top_done, 1)
                sv4 = sv.rearrange("p (t s) k -> p t s k", s=2)
                own(V.tensor_tensor(cand.rearrange("p t (i j) -> p t i j", i=TOPK),
                                    sv4[:, :, 0, :].unsqueeze(3).to_broadcast([P, NT, TOPK, TOPK]),
                                    sv4[:, :, 1, :].unsqueeze(2).to_broadcast([P, NT, TOPK, TOPK]), ALU.add))
                settled(h)
                carry()
                top16(h, [cand[:, t, :] for t in range(NT)], [cand_rest[:, t, :] for t in range(NT)],
                      [tv[:, t, :] for t in range(NT)], [ti[:, TOPK * t:TOPK * (t + 1)] for t in range(NT)])
                halves = ((ALU.logical_shift_right, 4), (ALU.bitwise_and, 15))
                for p, (op, by) in enumerate(halves):
                    own(V.tensor_scalar(tr[p], ti, by, None, op))
                settled(h)
                for p in range(2):
                    own(V.tensor_copy(pos_f[p], tr[p]))
                settled(h)
                for p in range(2):
                    own(V.tensor_tensor(onehot[p], pos_f[p].unsqueeze(2).to_broadcast([P, NT * TOPK, TOPK]),
                                        c_("iota").unsqueeze(1).to_broadcast([P, NT * TOPK, TOPK]), ALU.is_equal))
                settled(h)
                for p in range(2):
                    oh4 = onehot[p].rearrange("p (t k) j -> p t k j", t=NT)
                    keys = sif.rearrange("p (t s) k -> p t s k", s=2)[:, :, p, :]
                    own(V.tensor_tensor(oh4, oh4, keys.unsqueeze(2).to_broadcast([P, NT, TOPK, TOPK]), ALU.mult))
                settled(h)
                for p in range(2):
                    own(V.tensor_reduce(pick[p], onehot[p], X, ALU.add))
                settled(h)
                at = bass.ds(NT * TOPK * h, NT * TOPK)
                V.scalar_tensor_tensor(out=idx[:, at], in0=pick[0], scalar=float(P), in1=pick[1], op0=ALU.mult,
                                       op1=ALU.add).then_inc(idx_ready, NT)
                V.tensor_tensor(gate[:, at].rearrange("p (t k) -> p t k", t=NT), tv,
                                tv[:, :, 0:1].to_broadcast([P, NT, TOPK]), ALU.subtract).then_inc(top_v, 1)
                dve.wait_ge(top_v, h + 1)
                assert n_step[0] == ROUTE_STEPS

            def dot_products(h):
                for t in range(NT):
                    used = h * (NT * ROWS) + t * ROWS
                    for r in range(ROWS):
                        dve.wait_ge(row_in[r], h * (16 * NT) + 16 * (t + 1))
                        V.tensor_tensor_reduce(row[r], row[r], xn[:, t, :], 1.0, 0.0, ALU.mult, ALU.add,
                                               now[:, t, r:r + 1]).then_inc(row_used, 1)
                    dve.wait_ge(row_used, used + ROWS)
                    V.tensor_copy(dots[:, bass.ds(used, ROWS)], now[:, t, :]).then_inc(dots_out, 1)
                dve.wait_ge(dots_out, h * NT + NT)

            route(0)
            with dve.Fori(1, HEADS) as i:
                route(i)
                dot_products(i - 1)
            dot_products(HEADS - 1)

            g3 = gate[:, :].rearrange("p (g k) -> p g k", k=TOPK)
            z = stat[:, 0:NT * HEADS]
            dve.wait_ge(top_exp, 1)
            step(V.tensor_reduce(z, g3, X, ALU.add))
            step.wait()
            step(V.reciprocal(z, z))
            step.wait()
            step(V.tensor_tensor(g3, g3, z.unsqueeze(2).to_broadcast([P, NT * HEADS, TOPK]), ALU.mult))
            for y in y_acc + y_alt:
                step(V.memset(y, 0.0))
            step.wait()
            dve.wait_ge(gelu_done, 1)
            step(V.tensor_tensor(gate[:, :], gate[:, :], dots[:, :], ALU.mult))
            step.wait()
            with dve.Fori(0, HEADS) as i:
                for t in range(NT):
                    V.tensor_copy(now[:, t, :], gate[:, bass.ds(i * (NT * ROWS) + t * ROWS, ROWS)])\
                        .then_inc(w8_ready, 1)
                dve.wait_ge(w8_ready, i * NT + NT)
                for t in range(NT):
                    for r in range(ROWS):
                        dve.wait_ge(row_in[r], i * (16 * NT) + 16 * (GROUPS + t + 1))
                        dve.wait_ge(row_used, i * (NT * ROWS) + (ROWS * (GROUPS + t) + r - 1))
                        y = (y_acc, y_alt)[r % 2][t]
                        V.scalar_tensor_tensor(out=y, in0=row[r], scalar=now[:, t, r:r + 1], in1=y, op0=ALU.mult,
                                               op1=ALU.add).then_inc(row_used, 1)
                dve.wait_ge(row_used, i * (NT * ROWS) + ROWS * (GROUPS + NT))
            dve.wait_ge(row_ready, 12)
            for t in range(NT):
                step(V.tensor_tensor(y_acc[t], y_acc[t], y_alt[t], ALU.add))
            step.wait()
            for t in range(NT):
                step(V.tensor_tensor(y_acc[t], y_acc[t], gate_row[:, :], ALU.mult))
            step.wait()
            for t in range(NT):
                ins = V.tensor_tensor(x_sb[:, t, :], x_sb[:, t, :], y_acc[t], ALU.add)
                if t == 0:
                    step(ins)
            step.wait()
            ins.then_inc(res_done, 1)
            r = rstd(6, 1)
            dve.wait_ge(final_in, 16)
            dve.wait_ge(res_done, 4)
            for t in range(NT):
                V.scalar_tensor_tensor(out=xn[:, t, :], in0=x_sb[:, t, :], scalar=r[:, t:t + 1], in1=final_row,
                                       op0=ALU.mult, op1=ALU.mult).then_inc(out_ready, 1)


def _cols(v):
    return np.asarray(v).reshape(-1, P).T


def _t_units(w):
    w = w.reshape(KC, P, -1, 2, P).transpose(2, 1, 3, 0, 4)
    return w.reshape(w.shape[0], P, UNIT)


def _m_units(w):
    n = w.shape[1] // 512
    return w.reshape(2, 4, P, n, 512).transpose(3, 0, 2, 1, 4).reshape(2 * n, P, UNIT)


def _pair_blocks(w):
    k = w.shape[0] // P
    return w.reshape(k, P, KC // 2, 2, P).transpose(2, 1, 3, 0, 4).reshape(KC // 2, P, -1)


def _mod_units(w):
    return w.reshape(KC, P, -1, T).transpose(2, 1, 0, 3).reshape(-1, P, UNIT)


def _constants():
    p, c = np.arange(P)[:, None], np.arange(P)[None, :]
    key, wide = np.arange(P)[:, None], np.arange(T)[None, :]
    strict = np.concatenate([key < wide, key < np.arange(P)[None, :]], 1)
    loose = np.concatenate([key <= wide, key <= np.arange(P)[None, :]], 1)
    dist = np.concatenate([p - c, P + p - wide], 1)
    count = np.zeros(dist.shape)
    for w, d in ((128, 1), (512, 4), (2048, 16)):
        count += (dist >= 0) & (dist <= w) & (dist % d == 0)
    band = np.zeros((P, NT, 4, T))
    t = np.arange(T)
    for g, w in enumerate((2, 4, 8, 16)):
        for n in range(NT):
            s = n * P + np.arange(P)[:, None]
            band[:, n, g, :] = ((s <= t) & (s > t - w)) / np.minimum(t + 1.0, w) - (s == t)
    return {
        "ident": p == c, "tri": p <= c, "ones": np.ones((P, P)), "suffix": p >= c,
        "sb_keep": np.where(strict, -1.0, 0.0), "sb_bias": np.where(strict, 0.0, NEG),
        "ssm_bias": np.where(loose, 0.0, NEG), "dist": np.where(dist >= 0, dist, -NEG), "count": count,
        "iota": np.broadcast_to(np.arange(TOPK), (P, TOPK)),
    }, band.reshape(P, -1)


def kernel(**inputs):
    import concourse.bacc as bacc
    from concourse.bass_utils import run_bass_kernel_spmd

    f = {k: np.asarray(v) for k, v in inputs.items()}
    for name in ("mod_w", "mod_b", "g_pre_mix", "g_post_mix", "g_pre_ffn", "g_post_ffn", "w_in", "sc_conv_w",
                 "ssm_conv_w", "ssm_conv_b", "ssm_dt_bias", "ssm_a_log", "ssm_d", "ssm_norm_w", "w_sc_out",
                 "w_sb_out", "w_ssm_out", "w_o", "w_ffn_in", "w_ffn_out", "w_ada_2", "b_ada_2", "norm1_g_2",
                 "w_in_2", "pool_w_2", "pool_scale_2", "w_out_2", "norm2_g_2", "peer_wq_2", "peer_subkeys_2",
                 "peer_u_2", "peer_v_2"):
        f[name] = f[name][0]
    w_in = f["w_in"]
    at = np.cumsum([0, 768, 256, 256, 256, 512, 768, 8, 3072])
    part = {n: w_in[:, at[i]:at[i + 1]] for i, n in enumerate(("sc", "q", "k", "v", "z", "xbc", "dt", "gl"))}
    hidden = FB * P
    gu = f["w_ffn_in"].reshape(KC, P, 2, FB, P).transpose(3, 1, 2, 0, 4).reshape(FB, P, UNIT)
    w2 = f["w_in_2"]
    kinds = {
        "xbc": _t_units(part["xbc"]), "sc": _t_units(part["sc"]),
        "qk": np.concatenate([_t_units(part["q"]), _t_units(part["k"])]),
        "v": part["v"].reshape(KC, P, T).transpose(1, 0, 2).reshape(1, P, UNIT),
        "z": _t_units(part["z"]), "gl": _t_units(part["gl"]),
        "br": np.concatenate([_pair_blocks(f[n]) for n in ("w_sc_out", "w_sb_out", "w_ssm_out")], 2),
        "wo": _m_units(f["w_o"]), "gu": gu,
        "dn": f["w_ffn_out"].reshape(PAIRS, 2, P, D).transpose(0, 2, 1, 3).reshape(PAIRS, P, UNIT),
        "qk2": _t_units(w2[:, 0:1024]), "v2": _m_units(w2[:, 1024:1536]), "u2": _m_units(w2[:, 1536:2048]),
        "wo2": _m_units(f["w_out_2"]), "wq": _t_units(f["peer_wq_2"]),
    }
    assert hidden == f["w_ffn_out"].shape[0]
    stream = np.stack([kinds[kind][j] for kind, j in ORDER])
    consts, band = _constants()
    pieces = {
        "c": _cols(f["c"]), "c2": _cols(f["c_2"]),
        "mod_b": np.concatenate([_cols(f["mod_b"]), _cols(f["b_ada_2"])], 1),
        "g_pre_mix": _cols(f["g_pre_mix"]), "g_pre_ffn": _cols(f["g_pre_ffn"]),
        "g_post_mix": _cols(f["g_post_mix"]), "g_post_ffn": _cols(f["g_post_ffn"]),
        "norm1": _cols(f["norm1_g_2"]), "norm2": _cols(f["norm2_g_2"]), "ssm_b": _cols(f["ssm_conv_b"]),
        "ssm_w": f["ssm_conv_w"].reshape(4, 6, P).transpose(2, 1, 0).reshape(P, 24),
        "sc_w": f["sc_conv_w"].reshape(3, 2, P).transpose(2, 1, 0).reshape(P, 6),
        "ssm_norm": _cols(f["ssm_norm_w"]), "pool_scale": _cols(f["pool_scale_2"]),
        "ssm_d": _cols(np.repeat(f["ssm_d"], 64)),
        "dt_b": np.broadcast_to(f["ssm_dt_bias"], (P, 8)), "a_log": np.broadcast_to(f["ssm_a_log"], (P, 8)),
        "w_dt": part["dt"].reshape(KC, P, 8).transpose(1, 0, 2).reshape(P, 64),
        "pool_w": f["pool_w_2"].transpose(1, 0, 2).reshape(P, 512),
        "keys": f["peer_subkeys_2"].transpose(2, 0, 1).reshape(P, 256),
        **consts,
    }
    small = np.concatenate([np.asarray(pieces[n], dtype=np.float32) for n in SMALL], 1)
    arrays = {
        "stream": stream, "mod_w": np.concatenate([_mod_units(f["mod_w"]), _mod_units(f["w_ada_2"])]),
        "small": small,
        "x": np.ascontiguousarray(f["x"].reshape(NT, P, D).transpose(1, 0, 2)),
        "band": band.astype(np.float32), "final_g": np.ascontiguousarray(np.broadcast_to(f["final_g_2"], (P, D))),
        "expert_u": f["peer_u_2"], "expert_v": f["peer_v_2"],
    }
    nc = bacc.Bacc("TRN2", target_bir_lowering=False, num_devices=1)
    args = [nc.dram_tensor(f"in_{n}", a.shape, mybir.dt.from_np(a.dtype), kind="ExternalInput").ap()
            for n, a in arrays.items()]
    out = nc.dram_tensor("out", (T, D), F32, kind="ExternalOutput").ap()
    build(nc, *args, out)
    r = run_bass_kernel_spmd(nc, [{f"in_{n}": a for n, a in arrays.items()}], core_ids=[0])
    return r.results[0]["out"].reshape(1, T, D)
```

```python
from contextlib import ExitStack

import numpy as np

import concourse.bass as bass
from concourse import mybir

ALU = mybir.AluOpType
ACT = mybir.ActivationFunctionType
F32 = mybir.dt.float32
F32R = mybir.dt.float32r
U32 = mybir.dt.uint32
X = mybir.AxisListType.X

P = 128
D = 1024
T = 256
NT = T // P
KC = D // P
UNIT = 2048
RING = 3
FB = 22
PAIRS = FB // 2
HEADS = 8
TOPK = 16
SLOTS = HEADS * TOPK
ROWS = 16
FEW = 4
EPS = 1e-6
NEG = -1e30

ORDER = [("xbc", j) for j in range(3)] + [("sc", j) for j in range(3)] + [("qk", 0), ("qk", 1), ("v", 0)]
ORDER += [("z", 0), ("z", 1)] + [("gl", j) for j in range(12)]
ORDER += [("br", j) for j in range(4)] + [("wo", j) for j in range(4)]
ORDER += [("gu", 0), ("gu", 1)]
for _i in range(1, PAIRS):
    ORDER += [("gu", 2 * _i), ("dn", _i - 1), ("gu", 2 * _i + 1)]
ORDER += [("dn", PAIRS - 1)]
ORDER += [("qk2", j) for j in range(4)] + [("v2", 0), ("v2", 1), ("u2", 0), ("u2", 1)]
ORDER += [("wo2", j) for j in (1, 3, 0, 2)] + [("wq", j) for j in range(8)]
AT = {name: n for n, name in enumerate(ORDER)}
UNITS = len(ORDER)

ROUTE_STEPS = 5 * 4 + 1 + 5 * NT + 5 * 2
ROUTE_STEPS_0 = 5 * 4 + 2 * NT - 1 + 5 * NT + 5 * 2 * NT

SPLIT0 = AT["gu", 0]
SPLITS = AT["wo2", 1] - SPLIT0
HALF = 3 * UNIT // 4

MODS = 48
MOD_EARLY = 8
MOD_READS = [8, 20, 48]


def DONE(kind, j):
    return AT[kind, j] + 1


SMALL = {}
_at = 0
for _name, _n in (("c", 8), ("c2", 8), ("mod_b", 96), ("g_pre_mix", 8), ("g_pre_ffn", 8), ("g_post_mix", 8),
                  ("g_post_ffn", 8), ("norm1", 8), ("norm2", 8), ("ssm_b", 6), ("ssm_w", 24), ("sc_w", 6),
                  ("ssm_norm", 4), ("pool_scale", 4), ("ssm_d", 4), ("dt_b", 8), ("a_log", 8), ("w_dt", 64),
                  ("ident", P), ("tri", P), ("ones", P), ("suffix", P),
                  ("pool_w", 512), ("keys", 256), ("sb_keep", 384), ("sb_bias", 384), ("ssm_bias", 384),
                  ("dist", 384), ("count", 384),
                  ("iota", TOPK)):
    SMALL[_name] = (_at, _at + _n)
    _at += _n
SMALL_N = _at


def build(nc, stream, mod_w, small, x, band, final_g, expert_u, expert_v, out):
    with ExitStack() as ctx:
        start = {}

        def sb(name, n, dt=F32):
            start[name] = nc.sbuf_base
            return ctx.enter_context(nc.sbuf_tensor(name, [P, n], dt))

        def sem(name):
            return ctx.enter_context(nc.semaphore(name))

        def rounded(name, host, at, *dims):
            t = nc.alloc_sbuf_tensor_at(name, [P, int(np.prod(dims))], F32R, offset=start[host] + 4 * at)
            return cut(t, 0, *dims)

        def cut(t, at, *dims):
            n = int(np.prod(dims))
            v = t[:, at:at + n]
            if len(dims) == 2:
                return v.rearrange("p (a b) -> p a b", a=dims[0])
            if len(dims) == 3:
                return v.rearrange("p (a b c) -> p a b c", a=dims[0], b=dims[1])
            return v

        ring = sb("ring", RING * UNIT)
        mod_ring = sb("mod_ring", 2 * UNIT)
        gate_area = sb("gate_area", 24 * T)
        mod_sum = sb("mod_sum", 4 * T)
        areaA = sb("areaA", 8216)
        areaB = sb("areaB", 9728)
        sm = sb("small", SMALL_N)
        x_sb = sb("x_sb", NT * D)[:, :].rearrange("p (t d) -> p t d", t=NT)
        xn = sb("xn", NT * D)[:, :].rearrange("p (t d) -> p t d", t=NT)
        hT = sb("hT", KC * T)[:, :].rearrange("p (k t) -> p k t", k=KC)
        mT_flat = sb("mT", KC * T)
        mT = mT_flat[:, :].rearrange("p (k t) -> p k t", k=KC)
        diag = sb("diag", D)
        gate_row = sb("gate_row", D)
        scale_row = areaB[:, 6144:7168]
        shift_row = areaB[:, 7168:8192]
        modT = sb("modT", 96)
        cols = sb("cols", 64)
        stat = sb("stat", 64)
        dtb = sb("dtb", 192)

        ps = ctx.enter_context(nc.psum_tensor("ps", [P, 8, 512], F32))
        BM, BX = 2, 7
        B3 = 3

        def c_(name, a=0, b=None):
            lo, hi = SMALL[name]
            return sm[:, lo + a:(hi if b is None else lo + b)]

        slot = [cut(ring, s * UNIT, UNIT) for s in range(RING)]
        gates = cut(gate_area, 0, 24, T)
        row = ([cut(gate_area, r * D, D) for r in range(6)] + [cut(mod_ring, r * D, D) for r in range(4)]
               + [cut(areaB, r * D, D) for r in range(6)])

        def mod_place(m):
            if 2 <= m < 5:
                return cut(gate_area, (m - 2) * UNIT, UNIT)
            if 5 <= m < MOD_EARLY:
                return cut(areaB, (m - 5) * UNIT, UNIT)
            return cut(mod_ring, (m % 2) * UNIT, UNIT)

        def sum_place(m):
            return m % 4 if m < 24 else m % 2

        def mod_arrived(m):
            if m < MOD_EARLY:
                return mod_early_in[m], 16
            return mod_in[m % 2], 16 * ((m - MOD_EARLY) // 2 + 1)

        xbc_raw = cut(areaA, 0, 6, T + 3)
        xbc = cut(areaA, 1554, 6, T)
        sc = cut(areaA, 3090, 6, T)
        cx = cut(areaA, 4626, 2, T + 2)
        ya = cut(areaA, 5142, 2, T)
        qk = cut(areaA, 5654, 4, T)
        v1 = cut(areaA, 6678, NT, T)
        zg = cut(areaA, 7190, 4, T)
        sbl = cut(areaB, 0, 4, 384)
        sba = cut(areaB, 1536, 4, 384)
        decay = cut(areaB, 3072, 8, 384)
        a_rep = cut(areaB, 6144, 16, P)
        x_tok = cut(areaB, 8192, NT, 512)
        yb = cut(areaB, 9216, 2, T)
        yc = cut(areaB, 0, 4, T)
        ysq = cut(areaB, 1536, 4, T)
        prod = [cut(areaB, 3072 + 512 * n, 2, T) for n in range(6)]
        sg = cut(areaA, 0, 2, T)
        hid = cut(areaA, 512, 2, T)
        hid_h, hid_l = rounded("hid_h", "areaA", 1024, 2, T), rounded("hid_l", "areaA", 512, 2, T)
        w_hi = [rounded(f"w_hi{s}", "gate_area", s * UNIT, UNIT) for s in range(RING)]
        w_lo = [rounded(f"w_lo{s}", "areaB", s * UNIT, UNIT) for s in range(RING)]
        hT_h, hT_l = rounded("hT_h", "mT", 0, KC, T), rounded("hT_l", "hT", 0, KC, T)
        qk2 = cut(areaA, 0, 8, T)
        v2 = cut(areaA, 2048, NT, 512)
        u2 = cut(areaA, 3072, NT, 512)
        band_sb = cut(areaA, 4096, NT, 4, T)
        pooled = cut(areaA, 6144, 4, T)
        pexp = cut(areaB, 6144, 4, 384)
        pnrm = cut(areaB, 8192, 4, 384)
        pT = cut(areaB, 3072, 4, 384)
        score = cut(areaA, 0, 512)
        rest = cut(areaA, 1024, 4, P)
        cand = cut(areaA, 1536, NT, 256)
        cand_rest = cut(areaA, 2048, NT, 256)
        onehot = [cut(areaA, 512, NT * TOPK, TOPK), cut(areaA, 2560, NT * TOPK, TOPK)]
        qh = cut(areaA, 3072, 2, 512)
        y_acc = [cut(areaA, 4096, D), cut(areaA, 5120, D)]
        y_alt = [cut(areaA, 6144, D), cut(areaA, 7168, D)]
        final_row = diag[:, :]
        sv = cut(mT_flat, 0, 4, TOPK)
        si = cut(mT_flat, 64, 4, TOPK).bitcast(U32)
        sif = cut(mT_flat, 128, 4, TOPK)
        tv = cut(mT_flat, 192, NT, TOPK)
        ti = cut(mT_flat, 224, NT * TOPK).bitcast(U32)
        tr = [cut(mT_flat, 256, NT * TOPK).bitcast(U32), cut(mT_flat, 416, NT * TOPK).bitcast(U32)]
        pos_f = [cut(mT_flat, 288, NT * TOPK), cut(mT_flat, 320, NT * TOPK)]
        pick = [cut(mT_flat, 352, NT * TOPK), cut(mT_flat, 384, NT * TOPK)]
        idx = sb("idx", NT * SLOTS, U32)
        idx_now = sb("idx_now", ROWS, U32)
        gate_h = sb("gate_h", NT * ROWS)[:, :].rearrange("p (t r) -> p t r", t=NT)
        now = sb("now", NT * ROWS)[:, :].rearrange("p (t r) -> p t r", t=NT)
        weight = sb("weight", NT * ROWS)[:, :].rearrange("p (t r) -> p t r", t=NT)

        c_in, small_in, late_in, x_in, band_in, final_in = (sem("c_in"), sem("small_in"), sem("late_in"), sem("x_in"),
                                                            sem("band_in"), sem("final_in"))
        w_in = [sem(f"w_in{s}") for s in range(RING)]
        unit_done = sem("unit_done")
        dve_step, act_step = sem("dve_step"), sem("act_step")
        c_silu = sem("c_silu")
        sq_sum, mean_sq, root = sem("sq_sum"), sem("mean_sq"), sem("root")
        xn_ready, x_T, col_ready, hT_act, hT_dve = (sem("xn_ready"), sem("x_T"), sem("col_ready"), sem("hT_act"),
                                                    sem("hT_dve"))
        evac = sem("evac")
        diag_ready, row_mm, row_ready = sem("diag_ready"), sem("row_mm"), sem("row_ready")
        dt_mm, dt_lin, dt_exp, dt_one, dt_log, a_exp, a_ready = (
            sem("dt_mm"), sem("dt_lin"), sem("dt_exp"), sem("dt_one"), sem("dt_log"), sem("a_exp"), sem("a_ready"))
        conv_done, xbc_ready = sem("conv_done"), sem("xbc_ready")
        sb_z, sb_log, sb_lk, sb_sum, sb_arg, sb_att, sb_out, sb_y = (
            sem("sb_z"), sem("sb_log"), sem("sb_lk"), sem("sb_sum"), sem("sb_arg"), sem("sb_att"), sem("sb_out"),
            sem("sb_y"))
        acs_mm, dec_arg, dec_exp, xs_T, x_tok_ready, bc_mm, w_ready, y_mm = (
            sem("acs_mm"), sem("dec_arg"), sem("dec_exp"), sem("xs_T"), sem("x_tok_ready"), sem("bc_mm"),
            sem("w_ready"), sem("y_mm"))
        ysq_ready, ysum_mm, yms, yroot, yc_ready, ya_ready = (
            sem("ysq_ready"), sem("ysum_mm"), sem("yms"), sem("yroot"), sem("yc_ready"), sem("ya_ready"))
        merged = sem("merged")
        res_done = sem("res_done")
        silu_done, hid_ready, hid_step = sem("silu_done"), sem("hid_ready"), sem("hid_step")
        hi_ready = sem("hi_ready")
        lo_dve, lo_pool = sem("lo_dve"), sem("lo_pool")
        hTh_act, hT_lo = sem("hTh_act"), sem("hT_lo")
        at_s, at_max, at_exp, at_p, at_T, at_pT, at_pv, at_o = (
            sem("at_s"), sem("at_max"), sem("at_exp"), sem("at_p"), sem("at_T"), sem("at_pT"), sem("at_pv"),
            sem("at_o"))
        at_read = sem("at_read")
        pool_mm, pool_ev, pool_out, pool_y = sem("pool_mm"), sem("pool_ev"), sem("pool_out"), sem("pool_y")
        s_mm, s_ready = sem("s_mm"), sem("s_ready")
        top_v, top_exp, idx_ready = sem("top_v"), sem("top_exp"), sem("idx_ready")
        row_in = [sem(f"row_in{r}") for r in range(ROWS)]
        row_used, idx_copied, pool_go, gelu_done, weight_ready, weigh_step = (
            sem("row_used"), sem("idx_copied"), sem("pool_go"), sem("gelu_done"), sem("weight_ready"),
            sem("weigh_step"))
        out_ready, out_done = sem("out_ready"), sem("out_done")

        mod_in = [sem("mod_in0"), sem("mod_in1")]
        mod_early_in = [sem(f"mod_early_in{n}") for n in range(MOD_EARLY)]
        mod_summed, mod_used, mod_read = sem("mod_summed"), sem("mod_used"), sem("mod_read")
        mod_step = sem("mod_step")
        top_done = sem("top_done")
        dve_go = sem("dve_go")
        route_step = sem("route_step")
        acs_col_mm, acs_read = sem("acs_col_mm"), sem("acs_read")

        class Steps:

            def __init__(self, eng, s):
                self.eng, self.s, self.n = eng, s, 0

            def __call__(self, ins):
                ins.then_inc(self.s, 1)
                self.n += 1

            def wait(self, back=0):
                self.eng.wait_ge(self.s, self.n - back)

        block = ctx.enter_context(nc.Block())

        @block.sync
        def _(sp):
            n_c, n_late = SMALL["c2"][1], SMALL["pool_w"][0]
            sp.dma_start(sm[:, 0:n_c], small[:, 0:n_c]).then_inc(c_in, 16)
            for m in range(MOD_EARLY):
                sp.dma_start(mod_place(m), mod_w[m]).then_inc(mod_arrived(m)[0], 16)
                if m == 1:
                    sp.dma_start(x_sb, x).then_inc(x_in, 16)
                if m == 3:
                    sp.dma_start(sm[:, n_c:n_late], small[:, n_c:n_late]).then_inc(small_in, 16)
            for s in range(RING):
                sp.dma_start(slot[s], stream[s]).then_inc(w_in[s], 16)
            sp.dma_start(sm[:, n_late:], small[:, n_late:]).then_inc(late_in, 16)

            def load(i, s, split):
                if split:
                    sp.wait_ge(lo_dve, RING * i + (s - RING + 1 - SPLIT0))
                    sp.wait_ge(lo_pool, RING * i + (s - RING + 1 - SPLIT0))
                else:
                    sp.wait_ge(unit_done, RING * i + (s - RING + 1))
                sp.dma_start(slot[s], stream[bass.ds(RING * i + s, 1)].rearrange("o p n -> p (o n)"))\
                    .then_inc(w_in[s], 16)

            edge, edge2 = (SPLIT0 + RING) // RING, (SPLIT0 + SPLITS + RING) // RING
            with sp.Fori(1, edge) as i:
                for s in range(RING):
                    load(i, s, False)
            for s in range(RING):
                load(edge, s, RING * edge + s >= SPLIT0 + RING)
            with sp.Fori(edge + 1, edge2) as i:
                for s in range(RING):
                    load(i, s, True)
            assert RING * edge2 == SPLIT0 + SPLITS + RING
            with sp.Fori(edge2, UNITS // RING) as i:
                for s in range(RING):
                    load(i, s, False)
            for t in range(NT):
                sp.wait_ge(out_ready, t + 1)
                sp.dma_start(out[t * P:(t + 1) * P, :], xn[:, t, :]).then_inc(out_done, 16)
            sp.wait_ge(out_done, 16 * NT)

        @block.tensor
        def _(pe):
            mm = nc.tensor.matmul

            def arrived(kind, j):
                u = AT[kind, j]
                pe.wait_ge(w_in[u % RING], 16 * (u // RING + 1))
                return slot[u % RING]

            def mod_sum_over_partitions(m, columns=None):
                for b in range(2):
                    o = columns[b] if columns else ps[:, BM, 2 * m + b:2 * m + b + 1]
                    at = T * sum_place(m) + b * P
                    last = mm(o, mod_sum[:, at:at + P], c_("ones", 0, 1),
                              start=True, stop=True)
                last.then_inc(mod_used, 1)

            def mod_units(*ms):
                for m in ms:
                    pe.wait_ge(mod_summed, m + 1)
                    if m in MOD_READS:
                        pe.wait_ge(mod_read, MOD_READS.index(m) + 1)
                    mod_sum_over_partitions(m)

            def gemm_T(w, bank, rhs, new=None):
                for b in range(2):
                    for k in range(KC):
                        if new is not None and b == 0:
                            hT_chunk(new, k)
                        at = (b * KC + k) * P
                        last = mm(ps[:, bank, b * T:(b + 1) * T], w[:, at:at + P], rhs[:, k, :],
                                  start=(k == 0), stop=(k == KC - 1))
                return last

            def parts(kind, j):
                u = AT[kind, j]
                pe.wait_ge(lo_dve, u - SPLIT0 + 1)
                pe.wait_ge(lo_pool, u - SPLIT0 + 1)
                return w_hi[u % RING], w_lo[u % RING]

            def mm3(o, lhs, rhs, start, stop, **kw):
                mm(o, lhs[1], rhs[0], start=start, stop=False, **kw)
                mm(o, lhs[0], rhs[1], start=False, stop=False, **kw)
                return mm(o, lhs[0], rhs[0], start=False, stop=stop, **kw)

            hT_parts = (hT_h, hT_l)

            def gemm3_T(w, bank, new=None):
                for b in range(2):
                    for k in range(KC):
                        if new is not None and b == 0:
                            hT_chunk(new, k)
                        at = (b * KC + k) * P
                        last = mm3(ps[:, bank, b * T:(b + 1) * T], [v[:, at:at + P] for v in w],
                                   [v[:, k, :] for v in hT_parts], k == 0, k == KC - 1)
                return last

            evacs = [0]

            def bank_free():
                n = evacs[0]
                evacs[0] += 1
                if n >= 2:
                    pe.wait_ge(evac, n - 1)
                return n % 2

            def proj_T(kind, j):
                w = arrived(kind, j)
                gemm_T(w, bank_free(), hT, 0 if (kind, j) == ("xbc", 0) else None).then_inc(unit_done, 1)

            def transposes(n):
                for t in range(NT):
                    pe.wait_ge(xn_ready, NT * n + t + 1)
                    for k in range(KC):
                        last = nc.tensor.transpose(ps[:, B3 + k // 2, (k % 2) * T + t * P:(k % 2) * T + (t + 1) * P],
                                                   xn[:, t, k * P:(k + 1) * P], c_("ident"))
                        if t == NT - 1 and k % 2:
                            last.then_inc(x_T, 1)

            def hT_chunk(n, k):
                m = 2 * (k // 4) + k % 2 + 1
                if k // 2 % 2:
                    pe.wait_ge(hT_dve, 4 * n + m)
                elif n in (1, 2):
                    pe.wait_ge(hT_lo, 4 * (n - 1) + m)
                else:
                    pe.wait_ge(hT_act, 4 * n + m)

            def broadcast_row(n):
                for h in range(2):
                    pe.wait_ge(diag_ready, n + 1)
                    if 2 * n + h > 0:
                        pe.wait_ge(row_ready, 2 * n + h)
                    mm(ps[:, BX, :], c_("ones"), diag[:, 512 * h:512 * h + 512], start=True, stop=True)\
                        .then_inc(row_mm, 1)

            def wide(kind, j, lhs, late_first=False):
                w = arrived(kind, j)
                bank = B3 + 2 * (j // 2)
                for t in range(NT):
                    for k in range(4):
                        kk = 4 * (j % 2) + k
                        last = mm(ps[:, bank + t, :], lhs[:, kk, t * P:(t + 1) * P], w[:, 512 * k:512 * k + 512],
                                  start=(kk == (4 if late_first else 0)), stop=(kk == (3 if late_first else KC - 1)),
                                  skip_group_check=late_first)
                last.then_inc(unit_done, 1)

            pe.wait_ge(small_in, 16)
            mod_units(0, 1)
            transposes(0)
            mod_units(*range(2, 8))
            for j in range(3):
                proj_T("xbc", j)
            for t in range(NT):
                for k in range(KC):
                    last = mm(ps[:, BX, 8 * t:8 * t + 8], hT[:, k, t * P:(t + 1) * P],
                              c_("w_dt", 8 * k, 8 * k + 8), start=(k == 0), stop=(k == KC - 1))
            last.then_inc(dt_mm, 1)
            for j in range(3):
                proj_T("sc", j)
            for j in range(2):
                proj_T("qk", j)
            w = arrived("v", 0)
            bank = bank_free()
            for t in range(NT):
                for k in range(KC):
                    last = mm(ps[:, bank, t * T:(t + 1) * T], hT[:, k, t * P:(t + 1) * P], w[:, k * T:(k + 1) * T],
                              start=(k == 0), stop=(k == KC - 1))
            last.then_inc(unit_done, 1)

            def sb_scores(h, part, stop):
                r = slice(64 * (h % 2), 64 * (h % 2) + 64)
                q, k = qk[r, h // 2, :], qk[r, 2 + h // 2, :]
                if part == 0:
                    return mm(ps[:, B3 + h, 0:T], k[:, 0:P], q[:, :], start=True, stop=stop)
                return mm(ps[:, B3 + h, T:T + P], k[:, P:T], q[:, P:T], start=True, stop=stop)

            mod_units(8, 9)
            pe.wait_ge(evac, 8)
            for h in range(4):
                sb_scores(h, 0, True)
                last = sb_scores(h, 1, True)
            last.then_inc(sb_z, 1)
            for j in range(2):
                proj_T("z", j)
            mod_units(10, 11)
            for j in range(12):
                proj_T("gl", j)
                if j == 3:
                    mod_units(12, 13)
                if j == 2:
                    pe.wait_ge(sb_lk, 1)
                    for h in range(4):
                        sb_scores(h, 0, False)
                        mm(ps[:, B3 + h, P:T], c_("ones"), sbl[:, h, T:T + P], start=False, stop=False)
                        mm(ps[:, B3 + h, 0:T], c_("suffix"), sbl[:, h, 0:T], start=False, stop=True)
                        sb_scores(h, 1, False)
                        last = mm(ps[:, B3 + h, T:T + P], c_("suffix"), sbl[:, h, T:T + P], start=False, stop=True)
                    last.then_inc(sb_sum, 1)
                if j == 4:
                    for t in range(NT):
                        pe.wait_ge(xbc_ready, 6)
                        if t:
                            pe.wait_ge(x_tok_ready, t)
                        for b in range(4):
                            last = nc.tensor.transpose(ps[:, BX, b * P:(b + 1) * P], xbc[:, b, t * P:(t + 1) * P],
                                                       c_("ident"))
                        last.then_inc(xs_T, 1)
                if j == 5:
                    pe.wait_ge(a_ready, 1)
                    pe.wait_ge(x_tok_ready, NT)
                    acs = ps[:, BX, 0:16]
                    mm(acs[:, 0:8], c_("tri"), dtb[:, 16:24], start=True, stop=True)
                    mm(acs[:, 8:16], c_("ones"), dtb[:, 16:24], start=True, stop=False)
                    mm(acs[:, 8:16], c_("tri"), dtb[:, 24:32], start=False, stop=True).then_inc(acs_col_mm, 1)
                if j == 6:
                    pe.wait_ge(acs_read, 1)
                    pe.wait_ge(sb_att, 1)
                    pe.wait_ge(evac, 9)
                    for h in range(4):
                        r = slice(64 * (h % 2), 64 * (h % 2) + 64)
                        o = ps[r, BX, (h // 2) * T:(h // 2) * T + T]
                        mm(o, v1[:, 0, 64 * h:64 * h + 64], sba[:, h, 0:T], start=True, stop=True)
                        last = mm(o[:, P:T], v1[:, 1, 64 * h:64 * h + 64], sba[:, h, T:T + P], start=False, stop=True,
                                  skip_group_check=True)
                    last.then_inc(sb_out, 1)
                    pe.wait_ge(a_ready, 2)
                    lo = SMALL["tri"][0]
                    for h in range(8):
                        o = ps[:, B3 + h // 2, (h % 2) * T:(h % 2) * T + T]
                        mm(o, a_rep[:, h, :], sm[:, lo:lo + T], start=True, stop=True)
                        last = mm(o[:, P:T], a_rep[:, 8 + h, :], c_("tri"), start=False, stop=True,
                                  skip_group_check=True)
                    last.then_inc(acs_mm, 1)
                    mod_units(14, 15)
                if j == 7:
                    pe.wait_ge(dec_arg, 16)
                    for g in range(2):
                        r = slice(64 * g, 64 * g + 64)
                        mm(ps[:, B3 + g, 0:T], xbc[r, 4, 0:P], xbc[r, 5, :], start=True, stop=True)
                        last = mm(ps[:, B3 + g, T:T + P], xbc[r, 4, P:T], xbc[r, 5, P:T], start=True, stop=True)
                    last.then_inc(bc_mm, 1)
                if j == 8:
                    pe.wait_ge(w_ready, 16)
                    for h in range(8):
                        r = slice(64 * (h % 2), 64 * (h % 2) + 64)
                        b = h // 2
                        o = ps[r, B3 + 2 + b // 2, (b % 2) * T:(b % 2) * T + T]
                        mm(o, x_tok[:, 0, 64 * h:64 * h + 64], decay[:, h, 0:T], start=True, stop=True)
                        last = mm(o[:, P:T], x_tok[:, 1, 64 * h:64 * h + 64], decay[:, h, T:T + P], start=False, stop=True,
                                  skip_group_check=True)
                    last.then_inc(y_mm, 1)
                    mod_units(16, 17)
                if j == 9:
                    pe.wait_ge(ysq_ready, 1)
                    pe.wait_ge(sb_y, 1)
                    for g in range(2):
                        for b in range(2):
                            last = mm(ps[:, BX, g * T:(g + 1) * T], c_("ones"), ysq[:, 2 * g + b, :], start=(b == 0),
                                      stop=(b == 1))
                    last.then_inc(ysum_mm, 1)

                    mod_units(18, 19)
            pe.wait_ge(yms, 1)
            broadcast_row(0)
            pe.wait_ge(ya_ready, 1)
            pe.wait_ge(yc_ready, 1)
            for j in range(4):
                if j == 1:
                    pe.wait_ge(row_ready, 2)
                if j >= 2:
                    pe.wait_ge(merged, j - 1)
                w = arrived("br", j)
                banks = (3, 4, 5) if j % 2 == 0 else (6, 7, 0)
                at = 0
                for n, (y, kc) in enumerate(((ya, 2), (yb, 2), (yc, 4))):
                    for b in range(2):
                        for k in range(kc):
                            last = mm(ps[:, banks[n], b * T:(b + 1) * T], w[:, at:at + P], y[:, k, :],
                                      start=(k == 0), stop=(k == kc - 1))
                            at += P
                last.then_inc(unit_done, 1)
            pe.wait_ge(merged, 4)
            for j in range(4):
                wide("wo", j, mT)
                if j in (0, 2):
                    mod_units(20 + j, 21 + j)

            transposes(1)

            def gate_up(j, bank):
                gemm3_T(parts("gu", j), bank, 1 if j == 0 else None).then_inc(unit_done, 1)

            def down(w, first, final):
                for f in range(2):
                    for t in range(NT):
                        for n in range(2):
                            cols_f = slice(f * D + 512 * n, f * D + 512 * n + 512)
                            last = mm3(ps[:, B3 + 2 * n + t, :],
                                       [v[:, f, t * P:(t + 1) * P] for v in (hid_h, hid_l)],
                                       [v[:, cols_f] for v in w], first and f == 0, final and f == 1,
                                       skip_group_check=True)
                last.then_inc(unit_done, 1)

            gate_up(0, 0)
            gate_up(1, 1)
            pe.wait_ge(hid_ready, 1)
            gate_up(2, 0)
            mod_units(24, 25)
            pe.wait_ge(hid_ready, 2)
            down(parts("dn", 0), True, False)
            gate_up(3, 1)
            mod_units(26, 27)
            with pe.Fori(2, PAIRS) as i:
                def parts_of(n):
                    u0 = AT["gu", 4] + n
                    pe.wait_ge(lo_dve, 3 * i + (u0 - SPLIT0 + 1 - 6))
                    pe.wait_ge(lo_pool, 3 * i + (u0 - SPLIT0 + 1 - 6))
                    return w_hi[u0 % RING], w_lo[u0 % RING]

                w = parts_of(0)
                pe.wait_ge(hid_ready, 2 * i - 1)
                gemm3_T(w, 0).then_inc(unit_done, 1)
                for n in range(2):
                    pe.wait_ge(mod_summed, 2 * i + (25 + n))
                    mod_sum_over_partitions(n, [ps[:, BM, bass.ds(4 * i + (48 + 2 * n + b), 1)] for b in range(2)])
                w = parts_of(1)
                pe.wait_ge(hid_ready, 2 * i)
                down(w, False, False)
                gemm3_T(parts_of(2), 1).then_inc(unit_done, 1)
            mod_units(46, 47)
            pe.wait_ge(hid_ready, FB)
            down(parts("dn", PAIRS - 1), False, True)
            pe.wait_ge(res_done, 2)
            broadcast_row(1)

            transposes(2)
            evacs[0] = 24
            for j in range(4):
                w = parts("qk2", j)
                if j >= 2:
                    pe.wait_ge(evac, 23 + j - 1)
                gemm3_T(w, j % 2, 2 if j == 0 else None).then_inc(unit_done, 1)

            def token_major(kind, bank):
                for j in range(2):
                    w = parts(kind, j)
                    for t in range(NT):
                        for k in range(4):
                            kk = 4 * j + k
                            last = mm3(ps[:, bank + t, :], [v[:, kk, t * P:(t + 1) * P] for v in hT_parts],
                                       [v[:, 512 * k:512 * k + 512] for v in w], kk == 0, kk == KC - 1)
                    last.then_inc(unit_done, 1)

            token_major("v2", B3)

            def att_scores(b):
                pe.wait_ge(evac, 29)
                if b:
                    pe.wait_ge(at_read, b)
                for n in range(4):
                    h = 4 * b + n
                    r = slice(64 * (h % 2), 64 * (h % 2) + 64)
                    q, k = qk2[r, h // 2, :], qk2[r, 4 + h // 2, :]
                    mm(ps[:, B3 + n, 0:P], q[:, 0:P], k[:, 0:P], start=True, stop=True)
                    last = mm(ps[:, B3 + n, P:384], q[:, P:T], k[:, :], start=True, stop=True)
                last.then_inc(at_s, 1)

            flat = ps[:, :, :].rearrange("p b n -> p (b n)")

            def att_transposes(b):
                pe.wait_ge(at_p, b + 1)
                if b == 0:
                    pe.wait_ge(evac, 31)
                    pe.wait_ge(mod_read, 3)
                else:
                    pe.wait_ge(pool_y, 1)
                for n in range(4):
                    for m in range(3):
                        at = 384 * n + P * m
                        last = nc.tensor.transpose(flat[:, at:at + P], pnrm[:, n, P * m:P * m + P], c_("ident"))
                last.then_inc(at_T, 1)

            def att_values(b):
                pe.wait_ge(at_pT, b + 1)
                if b:
                    pe.wait_ge(at_o, b)
                else:
                    pe.wait_ge(row_ready, 6)
                for n in range(4):
                    h = 4 * b + n
                    r = slice(64 * (h % 2), 64 * (h % 2) + 64)
                    o = ps[r, BX, (n // 2) * T:(n // 2) * T + T]
                    mm(o, v2[:, 0, 64 * h:64 * h + 64], pT[:, n, 0:T], start=True, stop=True)
                    last = mm(o[:, P:T], v2[:, 1, 64 * h:64 * h + 64], pT[:, n, T:384], start=False, stop=True,
                              skip_group_check=True)
                last.then_inc(at_pv, 1)

            att_scores(0)
            pe.wait_ge(res_done, 4)
            broadcast_row(2)
            token_major("u2", 0)
            att_transposes(0)
            att_scores(1)
            att_values(0)
            pe.wait_ge(band_in, 16)
            for g in range(4):
                o = ps[:, g // 2, (g % 2) * T:(g % 2) * T + T]
                mm(o, u2[:, 0, g * P:(g + 1) * P], band_sb[:, 0, g, :], start=True, stop=True)
                last = mm(o[:, P:T], u2[:, 1, g * P:(g + 1) * P], band_sb[:, 1, g, P:T], start=False, stop=True,
                          skip_group_check=True)
            last.then_inc(pool_mm, 1)
            pe.wait_ge(pool_ev, 1)
            for g in range(4):
                last = mm(ps[:, g // 2, (g % 2) * T:(g % 2) * T + T], c_("pool_w", g * P, (g + 1) * P),
                          pooled[:, g, :], start=True, stop=True)
            last.then_inc(pool_out, 1)
            att_transposes(1)
            pe.wait_ge(pool_y, 1)
            pe.wait_ge(at_read, 2)
            wide("wo2", 1, mT, True)
            pe.wait_ge(at_o, 1)
            broadcast_row(3)
            wide("wo2", 3, mT, True)
            pe.wait_ge(row_ready, 8)
            att_values(1)
            pe.wait_ge(at_o, 2)
            wide("wo2", 0, mT, True)
            broadcast_row(4)
            wide("wo2", 2, mT, True)
            transposes(3)

            def sub_scores(h):
                pe.wait_ge(evac, 31 + h + 1)
                if h >= 4:
                    pe.wait_ge(s_ready, h - 3)
                for t in range(NT):
                    for p in range(2):
                        last = mm(ps[:, B3 + h % 4, (2 * t + p) * P:(2 * t + p + 1) * P],
                                  qh[:, h % 2, p * T + t * P:p * T + (t + 1) * P], c_("keys", p * P, (p + 1) * P),
                                  start=True, stop=True)
                last.then_inc(s_mm, 1)

            for h in range(HEADS):
                w = arrived("wq", h)
                if h >= 2:
                    pe.wait_ge(evac, 31 + h - 1)
                gemm_T(w, h % 2, hT, 3 if h == 0 else None).then_inc(unit_done, 1)
                if h == 0:
                    sub_scores(0)
                    broadcast_row(5)
                if h >= 2:
                    sub_scores(h - 1)
            sub_scores(HEADS - 1)

        @block.scalar
        def _(act):
            step = Steps(act, act_step)
            A = nc.scalar.activation

            def squares(n, source, outs):
                for m, (s, o) in enumerate(zip(source, outs)):
                    A(o, s, ACT.Square, accum_out=stat[:, 8 * (n % 4) + m:8 * (n % 4) + m + 1]).then_inc(sq_sum, 1)

            def residual_squares(n, m):
                for t in range(NT):
                    act.wait_ge(res_done, NT * (n - 1) + t + 1)
                    A(xn[:, t, :], x_sb[:, t, :], ACT.Square, accum_out=stat[:, 8 * (m % 4) + t:8 * (m % 4) + t + 1])\
                        .then_inc(sq_sum, 1)


            def square_root(n, w):
                act.wait_ge(mean_sq, n + 1)
                A(stat[:, 32 + 2 * (n % 8):32 + 2 * (n % 8) + w], stat[:, 48 + 2 * (n % 8):48 + 2 * (n % 8) + w],
                  ACT.Sqrt).then_inc(root, 1)

            def hT_part(n):
                for k in (0, 1, 4, 5):
                    act.wait_ge(x_T, KC // 2 * n + k // 2 + 1)
                    src = ps[:, B3 + k // 2, (k % 2) * T:(k % 2) * T + T]
                    act.wait_ge(col_ready, (1, 3, 4, 8)[n])
                    scale, bias = (cols[:, c + k:c + k + 1] for c in (16 * n, 16 * n + 8))
                    A(hT[:, k, :], src, ACT.Identity, scale=scale, bias=bias).then_inc(hT_act, 1)
                    if n in (1, 2):
                        A(hT_h[:, k, :], src, ACT.Identity, scale=scale, bias=bias).then_inc(hTh_act, 1)

            def copy_out(kind, j, dst, func=ACT.Identity, scale=1.0, bank=0, w=512):
                act.wait_ge(unit_done, DONE(kind, j))
                src = ps[:, bank, :].rearrange("p (b t) -> p b t", b=2)
                A(dst, src, func, scale=scale).then_inc(evac, 1)

            def split_hi(u, i=0):
                act.wait_ge(w_in[u % RING], i * 16 + 16 * (u // RING + 1))
                if u >= SPLIT0 + RING:
                    act.wait_ge(unit_done, i * RING + (u - RING + 1))
                A(w_hi[u % RING], slot[u % RING], ACT.Identity).then_inc(hi_ready, 1)

            def row_copy(n, dst):
                for h in range(2):
                    act.wait_ge(row_mm, 2 * n + h + 1)
                    A(dst[:, 512 * h:512 * h + 512], ps[:, BX, :], ACT.Identity).then_inc(row_ready, 1)

            act.wait_ge(c_in, 16)
            A(cols[:, 48:64], c_("c", 0, 16), ACT.Silu).then_inc(c_silu, 1)
            act.wait_ge(x_in, 16)
            squares(0, [x_sb[:, t, :] for t in range(NT)], [xn[:, t, :] for t in range(NT)])
            square_root(0, 2)
            act.wait_ge(small_in, 16)
            A(dtb[:, 32:40], c_("a_log"), ACT.Exp).then_inc(a_exp, 1)
            hT_part(0)
            n = 0
            for j in range(3):
                copy_out("xbc", j, xbc_raw[:, 2 * j:2 * j + 2, 3:], bank=n % 2)
                n += 1
            for j in range(3):
                copy_out("sc", j, sc[:, 2 * j:2 * j + 2, :], bank=n % 2)
                n += 1
            act.wait_ge(dt_lin, 2)
            A(dtb[:, 64:80], dtb[:, 48:64], ACT.Exp, scale=-1.0).then_inc(dt_exp, 1)
            act.wait_ge(dt_one, 1)
            A(dtb[:, 96:112], dtb[:, 80:96], ACT.Ln).then_inc(dt_log, 1)
            for j in range(2):
                copy_out("qk", j, qk[:, 2 * j:2 * j + 2, :], scale=(0.125 if j == 0 else 1.0), bank=n % 2)
                n += 1
            copy_out("v", 0, v1, bank=n % 2)
            n += 1
            z4 = ps[:, B3:B3 + 4, 0:384]
            act.wait_ge(sb_z, 1)
            step(A(sbl, z4, ACT.Abs))
            step.wait()
            step(A(sbl, sbl, ACT.Exp, scale=-1.0))
            step.wait()
            A(sbl, sbl, ACT.Ln, bias=1.0).then_inc(sb_log, 1)
            for b in range(6):
                act.wait_ge(conv_done, b + 1)
                A(xbc[:, b, :], xbc[:, b, :], ACT.Silu, bias=c_("ssm_b", b, b + 1)).then_inc(xbc_ready, 1)
            for j in range(2):
                copy_out("z", j, zg[:, 2 * j:2 * j + 2, :], func=ACT.Silu, bank=n % 2)
                n += 1
            for j in range(12):
                copy_out("gl", j, gates[:, 2 * j:2 * j + 2, :], func=ACT.Sigmoid, bank=n % 2)
                n += 1
                if j == 4:
                    act.wait_ge(sb_arg, 1)
                    A(sba, sba, ACT.Exp).then_inc(sb_att, 1)
                    for t in range(NT):
                        act.wait_ge(xs_T, t + 1)
                        A(x_tok[:, t, :], ps[:, BX, :], ACT.Identity).then_inc(x_tok_ready, 1)
                if j == 6:
                    act.wait_ge(sb_out, 1)
                    A(yb, ps[:, BX, :].rearrange("p (b t) -> p b t", b=2), ACT.Identity).then_inc(sb_y, 1)
                if j == 6:
                    for hh in range(2):
                        act.wait_ge(dec_arg, 8 * hh + 8)
                        A(decay[:, 4 * hh:4 * hh + 4, :], decay[:, 4 * hh:4 * hh + 4, :], ACT.Exp)\
                            .then_inc(dec_exp, 1)
                if j == 9:
                    act.wait_ge(yms, 1)
                    A(ysq[:, 0:2, :], ysq[:, 0:2, :], ACT.Sqrt).then_inc(yroot, 1)
            row_copy(0, gate_row)
            act.wait_ge(merged, 4)
            split_hi(SPLIT0)
            split_hi(SPLIT0 + 1)
            act.wait_ge(unit_done, DONE("wo", 3))
            squares(1, [ps[:, B3 + b, :] for b in range(4)],
                    [xn[:, b % 2, 512 * (b // 2):512 * (b // 2) + 512] for b in range(4)])
            square_root(1, 2)
            residual_squares(1, 2)
            square_root(2, 2)
            hT_part(1)
            split_hi(SPLIT0 + 2)
            for f in range(2):
                act.wait_ge(unit_done, DONE("gu", f))
                A(sg[:, f, :], ps[:, f, 0:T], ACT.Silu).then_inc(silu_done, 1)
                split_hi(SPLIT0 + 3 + f)
            with act.Fori(1, PAIRS) as i:
                for f in range(2):
                    act.wait_ge(unit_done, 3 * i + (AT["gu", 2 + f] - 3 + 1))
                    act.wait_ge(hid_ready, 2 * i + (f - 1))
                    A(sg[:, f, :], ps[:, f, 0:T], ACT.Silu).then_inc(silu_done, 1)
                    if f == 0:
                        split_hi(SPLIT0 + 5 - 3, i)
                        split_hi(SPLIT0 + 6 - 3, i)
                    else:
                        split_hi(SPLIT0 + 7 - 3, i)
            act.wait_ge(unit_done, DONE("dn", PAIRS - 1))
            squares(3, [ps[:, B3 + b, :] for b in range(4)],
                    [xn[:, b % 2, 512 * (b // 2):512 * (b // 2) + 512] for b in range(4)])
            row_copy(1, gate_row)
            square_root(3, 2)
            residual_squares(2, 4)
            square_root(4, 2)
            split_hi(AT["qk2", 2])
            hT_part(2)
            for j in range(4):
                copy_out("qk2", j, qk2[:, 2 * j:2 * j + 2, :], bank=j % 2)
                split_hi(AT["qk2", 3] + j)
            split_hi(AT["u2", 1])

            def token_major(kind, dst, bank):
                act.wait_ge(unit_done, DONE(kind, 1))
                for t in range(NT):
                    A(dst[:, t, :], ps[:, bank + t, :], ACT.Identity).then_inc(evac, 1)

            token_major("v2", v2, B3)

            def att_exp(b):
                act.wait_ge(at_max, b + 1)
                for n in range(4):
                    for t, (lo, hi) in enumerate(((0, P), (P, 384))):
                        A(pnrm[:, n, lo:hi], pexp[:, n, lo:hi], ACT.Exp, scale=0.125,
                          bias=stat[:, 4 * t + n:4 * t + n + 1]).then_inc(at_exp, 1)

            def pT_copy(b):
                act.wait_ge(at_T, b + 1)
                if b:
                    act.wait_ge(at_pv, b)
                A(pT, flat_ps[:, 0:1536].rearrange("p (a b) -> p a b", a=4), ACT.Identity).then_inc(at_pT, 1)

            def o_copy(b):
                act.wait_ge(at_pv, b + 1)
                A(mT[:, 2 * b:2 * b + 2, :], ps[:, BX, :].rearrange("p (b t) -> p b t", b=2), ACT.Identity)\
                    .then_inc(at_o, 1)

            flat_ps = ps[:, :, :].rearrange("p b n -> p (b n)")
            row_copy(2, gate_row)
            att_exp(0)
            token_major("u2", u2, 0)
            pT_copy(0)
            att_exp(1)
            o_copy(0)
            act.wait_ge(pool_mm, 1)
            A(pooled, flat_ps[:, 0:1024].rearrange("p (a b) -> p a b", a=4), ACT.Identity).then_inc(pool_ev, 1)
            act.wait_ge(pool_out, 1)
            for g in range(4):
                A(mT[:, 4 + g, :], flat_ps[:, g * T:(g + 1) * T], ACT.Identity,
                  scale=c_("pool_scale", g, g + 1)).then_inc(act_step if g < 3 else pool_y, 1)
            step.n += 3
            pT_copy(1)
            row_copy(3, scale_row)
            o_copy(1)
            row_copy(4, shift_row)
            residual_squares(3, 5)
            square_root(5, 2)
            hT_part(3)

            def gate_exp(h):
                act.wait_ge(top_v, h + 1)
                A(gate_h, gate_h, ACT.Exp).then_inc(top_exp, 1)

            def gelu(h):
                act.wait_ge(row_used, ROWS * (2 * NT * h + NT + 1))
                A(now, now, ACT.Gelu).then_inc(gelu_done, 1)

            for h in range(HEADS + 1):
                if h < HEADS:
                    act.wait_ge(unit_done, DONE("wq", h))
                    if h >= 2:
                        act.wait_ge(s_mm, h - 1)
                    A(qh[:, h % 2, :], ps[:, h % 2, :], ACT.Identity).then_inc(evac, 1)
                if h != 1:
                    head = max(h - 1, 0)
                    act.wait_ge(s_mm, head + 1)
                    if head:
                        act.wait_ge(top_done, head)
                    A(score, ps[:, B3 + head % 4, :], ACT.Identity).then_inc(s_ready, 1)
                if h == 0:
                    row_copy(5, gate_row)
                if h == 1:
                    gate_exp(0)
                if h == 2:
                    gelu(0)
                if h >= 3:
                    gate_exp(h - 2)
                    gelu(h - 2)
            gate_exp(HEADS - 1)
            gelu(HEADS - 1)
            for t in range(NT):
                act.wait_ge(res_done, NT * 3 + t + 1)
                A(xn[:, t, :], x_sb[:, t, :], ACT.Square, accum_out=stat[:, 16 + t:17 + t]).then_inc(sq_sum, 1)
                act.wait_ge(mean_sq, 7 + t)
                A(stat[:, 44 + t:45 + t], stat[:, 60 + t:61 + t], ACT.Sqrt).then_inc(root, 1)

        @block.gpsimd
        def _(pool):
            def load_mods(m0, m1):
                with pool.Fori(m0 // 2, m1 // 2) as i:
                    for n in range(2):
                        pool.wait_ge(mod_summed, 2 * i + (n - 1))
                        pool.sem_inc(pool_go, 1)
                        pool.dma_start(cut(mod_ring, n * UNIT, UNIT),
                                       mod_w[bass.ds(2 * i + n, 1)].rearrange("o p n -> p (o n)"))\
                            .then_inc(mod_in[n], 16)

            load_mods(MOD_EARLY, 24)
            def load_mod(m, i=0):
                pool.wait_ge(mod_summed, i * 2 + (m - 1))
                pool.sem_inc(pool_go, 1)
                pool.dma_start(cut(mod_ring, (m % 2) * UNIT, UNIT),
                               mod_w[bass.ds(i * 2 + m, 1)].rearrange("o p n -> p (o n)")).then_inc(mod_in[m % 2], 16)

            def split_lo(u, i=0):
                s = u % RING
                pool.wait_ge(hi_ready, i * RING + (u - SPLIT0 + 1))
                nc.gpsimd.tensor_tensor(w_lo[s][:, HALF:], slot[s][:, HALF:], w_hi[s][:, HALF:].bitcast(F32),
                                        ALU.subtract).then_inc(lo_pool, 1)

            def hT_split(n):
                for m, k in enumerate((0, 1, 4, 5)):
                    pool.wait_ge(hTh_act, 4 * (n - 1) + m + 1)
                    nc.gpsimd.tensor_tensor(hT_l[:, k, :], hT[:, k, :], hT_h[:, k, :].bitcast(F32),
                                            ALU.subtract).then_inc(hT_lo, 1)

            load_mod(24)
            load_mod(25)
            split_lo(SPLIT0)
            split_lo(SPLIT0 + 1)
            hT_split(1)
            split_lo(SPLIT0 + 2)
            load_mod(26)
            load_mod(27)
            split_lo(SPLIT0 + 3)
            split_lo(SPLIT0 + 4)
            load_mod(28)
            load_mod(29)
            with pool.Fori(1, PAIRS - 1) as i:
                split_lo(SPLIT0 + 5 - 3, i)
                load_mod(28, i)
                load_mod(29, i)
                split_lo(SPLIT0 + 6 - 3, i)
                split_lo(SPLIT0 + 7 - 3, i)
            pool.dma_start(cut(areaA, 4096, 2048), band).then_inc(band_in, 16)
            for u in range(AT["dn", PAIRS - 1], AT["qk2", 2]):
                split_lo(u)
            hT_split(2)
            for u in range(AT["qk2", 2], SPLIT0 + SPLITS):
                split_lo(u)
            pool.wait_ge(row_mm, 12)
            pool.dma_start(final_row[:, :], final_g).then_inc(final_in, 16)

            with pool.Fori(0, HEADS) as i:
                for g in range(2 * NT):
                    if g < NT:
                        pool.wait_ge(idx_ready, i * NT + (g + 1))
                        pool.sem_inc(pool_go, 1)
                    for part in range(ROWS // FEW):
                        r0 = part * FEW
                        pool.wait_ge(row_used, i * (2 * NT * ROWS) + (ROWS * g + r0 + FEW))
                        pool.sem_inc(pool_go, 1)
                        nc.gpsimd.tensor_copy(idx_now[:, r0:r0 + FEW],
                                              idx[:, bass.ds(i * (NT * TOPK) + ((g % NT) * TOPK + r0), FEW)])\
                            .then_inc(idx_copied, 1)
                        pool.wait_ge(idx_copied, i * (2 * NT * ROWS // FEW) + (g * ROWS // FEW + part + 1))
                        pool.sem_inc(pool_go, 1)
                        for r in range(r0, r0 + FEW):
                            pool.indirect_dma_start(row[r], None, (expert_u, expert_v)[g // NT],
                                                    bass.IndirectOffsetOnAxis(ap=idx_now[:, r:r + 1], axis=0))\
                                .then_inc(row_in[r], 16)

        @block.vector
        def _(dve):
            V = nc.vector
            step = Steps(dve, dve_step)

            def rstd(n, pieces):
                need = {0: 2, 1: 6, 2: 8, 3: 12, 4: 14, 5: 16, 6: 18}[n]
                dve.wait_ge(sq_sum, need)
                src = stat[:, 8 * (n % 4):8 * (n % 4) + 2]
                if pieces == 2:
                    step(V.tensor_tensor(stat[:, 8 * (n % 4) + 4:8 * (n % 4) + 6], src,
                                         stat[:, 8 * (n % 4) + 2:8 * (n % 4) + 4], ALU.add))
                    step.wait()
                    src = stat[:, 8 * (n % 4) + 4:8 * (n % 4) + 6]
                V.tensor_scalar(stat[:, 48 + 2 * (n % 8):50 + 2 * (n % 8)], src, 1.0 / D, EPS, ALU.mult, ALU.add)\
                    .then_inc(mean_sq, 1)
                dve.wait_ge(root, n + 1)
                r = stat[:, 32 + 2 * (n % 8):34 + 2 * (n % 8)]
                step(V.reciprocal(r, r))
                step.wait()
                return r

            def normalise(n, r):
                for t in range(NT):
                    V.tensor_scalar(xn[:, t, :], x_sb[:, t, :], r[:, t:t + 1], None, ALU.mult).then_inc(xn_ready, 1)

            def hT_part(n):
                dve.wait_ge(col_ready, (1, 3, 4, 8)[n])
                for k in (2, 3, 6, 7):
                    dve.wait_ge(x_T, KC // 2 * n + k // 2 + 1)
                    src = ps[:, B3 + k // 2, (k % 2) * T:(k % 2) * T + T]
                    scale, bias = (cols[:, c + k:c + k + 1] for c in (16 * n, 16 * n + 8))
                    ins = V.tensor_scalar(hT[:, k, :], src, scale, bias, ALU.mult, ALU.add)
                    if n in (1, 2):
                        step(ins)
                        step(V.tensor_scalar(hT_h[:, k, :], src, scale, bias, ALU.mult, ALU.add))
                        step.wait()
                        ins = V.tensor_tensor(hT_l[:, k, :], hT[:, k, :], hT_h[:, k, :].bitcast(F32), ALU.subtract)
                    ins.then_inc(hT_dve, 1)

            def mod_products(places, first, vec, wait_for):
                o = [mod_sum[:, n * T:(n + 1) * T] for n in (first, first + 1)]
                for k in range(KC):
                    for n in range(2):
                        w = places[n].rearrange("p (k c) -> p k c", k=KC)[:, k, :]
                        if k == 0:
                            ins = V.tensor_scalar(o[n], w, vec[:, k:k + 1], None, ALU.mult)
                        else:
                            wait_for(1 if k < KC - 1 or n == 0 else 0)
                            ins = V.scalar_tensor_tensor(out=o[n], in0=w, scalar=vec[:, k:k + 1], in1=o[n],
                                                         op0=ALU.mult, op1=ALU.add)
                        if k < KC - 1:
                            yield ins
                        else:
                            ins.then_inc(mod_summed, 1)

            def split_lo(u, i=0):
                s = u % RING
                dve.wait_ge(hi_ready, i * RING + (u - SPLIT0 + 1))
                V.tensor_tensor(w_lo[s][:, 0:HALF], slot[s][:, 0:HALF], w_hi[s][:, 0:HALF].bitcast(F32),
                                ALU.subtract).then_inc(lo_dve, 1)

            def mod_units(m0, m1):
                for m in range(m0, m1, 2):
                    if m == 0:
                        dve.wait_ge(c_silu, 1)
                    elif m >= 4:
                        dve.wait_ge(mod_used, m - 2 if m < 24 else m)
                    for n in range(2):
                        dve.wait_ge(*mod_arrived(m + n))
                    vec = cols[:, 48 + 8 * (m // 24):56 + 8 * (m // 24)]
                    for ins in mod_products([mod_place(m), mod_place(m + 1)], sum_place(m), vec, step.wait):
                        step(ins)

            def modulation(m0, m1):
                dve.wait_ge(mod_used, m1)
                V.tensor_tensor(modT[:, 2 * m0:2 * m1], ps[:, BM, 2 * m0:2 * m1], c_("mod_b", 2 * m0, 2 * m1),
                                ALU.add).then_inc(mod_read, 1)
                dve.wait_ge(mod_read, MOD_READS.index(m1) + 1)

            ident8 = c_("ident").unsqueeze(1).to_broadcast([P, 8, P])
            diag3 = diag[:, :].rearrange("p (k n) -> p k n", k=8)

            def spread(n, vec):
                if n:
                    dve.wait_ge(row_mm, 2 * n)
                V.tensor_tensor(diag3, ident8, vec.unsqueeze(2).to_broadcast([P, 8, P]), ALU.mult)\
                    .then_inc(diag_ready, 1)

            def residual(n, r, rows):
                dve.wait_ge(row_ready, rows)
                for t in range(NT):
                    for b in (t, NT + t):
                        lo = 512 * (b // 2)
                        src = ps[:, B3 + b, :]
                        if r is None:
                            step(V.tensor_tensor(xn[:, t, lo:lo + 512], src, gate_row[:, lo:lo + 512], ALU.mult))
                        else:
                            step(V.scalar_tensor_tensor(out=xn[:, t, lo:lo + 512], in0=src, scalar=r[:, t:t + 1],
                                                        in1=gate_row[:, lo:lo + 512], op0=ALU.mult, op1=ALU.mult))
                    step.wait()
                    V.tensor_tensor(x_sb[:, t, :], x_sb[:, t, :], xn[:, t, :], ALU.add).then_inc(res_done, 1)

            step(V.memset(xbc_raw[:, :, 0:3], 0.0))
            step(V.memset(cx[:, :, 0:2], 0.0))
            mod_units(0, 2)
            normalise(0, rstd(0, 1))
            mod_units(2, 8)
            dve.wait_ge(small_in, 16)
            modulation(0, 8)
            step(V.scalar_tensor_tensor(out=cols[:, 0:8], in0=modT[:, 8:16], scalar=1.0, in1=c_("g_pre_mix"),
                                        op0=ALU.add, op1=ALU.mult))
            step.wait()
            V.tensor_copy(cols[:, 8:16], modT[:, 0:8]).then_inc(col_ready, 1)
            dve.wait_ge(col_ready, 1)
            hT_part(0)

            for k in range(4):
                for b in range(6):
                    w = c_("ssm_w", 4 * b + k, 4 * b + k + 1)
                    if k == 0:
                        if b % 2 == 0:
                            dve.wait_ge(evac, b // 2 + 1)
                        step(V.tensor_scalar(xbc[:, b, :], xbc_raw[:, b, 0:T], w, None, ALU.mult))
                    else:
                        step.wait(5)
                        ins = V.scalar_tensor_tensor(out=xbc[:, b, :], in0=xbc_raw[:, b, k:k + T], scalar=w,
                                                     in1=xbc[:, b, :], op0=ALU.mult, op1=ALU.add)
                        if k < 3:
                            step(ins)
                        else:
                            ins.then_inc(conv_done, 1)
                if k == 2:
                    step.wait()
            dt, a, ea = dtb[:, 0:16], dtb[:, 16:32], dtb[:, 32:40]
            mag, e, u, l, lin = dtb[:, 48:64], dtb[:, 64:80], dtb[:, 80:96], dtb[:, 96:112], dtb[:, 112:128]
            dve.wait_ge(dt_mm, 1)
            step(V.tensor_tensor(lin.rearrange("p (t h) -> p t h", t=NT),
                                 ps[:, BX, 0:16].rearrange("p (t h) -> p t h", t=NT),
                                 c_("dt_b").unsqueeze(1).to_broadcast([P, NT, 8]), ALU.add))
            step.wait()
            V.scalar_tensor_tensor(out=mag, in0=lin, scalar=-1.0, in1=lin, op0=ALU.mult, op1=ALU.max)\
                .then_inc(dt_lin, 1)
            V.tensor_scalar(lin, lin, 0.0, None, ALU.max).then_inc(dt_lin, 1)
            dve.wait_ge(dt_exp, 1)
            V.tensor_scalar(u, e, 1.0, None, ALU.add).then_inc(dt_one, 1)
            dve.wait_ge(dt_one, 1)
            step(V.scalar_tensor_tensor(out=dtb[:, 128:144], in0=u, scalar=-1.0, in1=e, op0=ALU.add,
                                        op1=ALU.subtract))
            step(V.reciprocal(dtb[:, 144:160], u))
            step.wait()
            step(V.scalar_tensor_tensor(out=dtb[:, 160:176], in0=dtb[:, 128:144], scalar=-1.0, in1=dtb[:, 144:160],
                                        op0=ALU.mult, op1=ALU.mult))
            dve.wait_ge(dt_log, 1)
            dve.wait_ge(dt_lin, 2)
            step(V.tensor_tensor(lin, lin, l, ALU.add))
            step.wait()
            step(V.tensor_tensor(dt, lin, dtb[:, 160:176], ALU.add))
            step.wait()
            dve.wait_ge(a_exp, 1)
            V.scalar_tensor_tensor(out=a.rearrange("p (t h) -> p t h", t=NT),
                                   in0=dt.rearrange("p (t h) -> p t h", t=NT), scalar=-1.0,
                                   in1=ea.unsqueeze(1).to_broadcast([P, NT, 8]), op0=ALU.mult, op1=ALU.mult)\
                .then_inc(a_ready, 1)
            dve.wait_ge(a_ready, 1)
            V.tensor_copy(a_rep, a.unsqueeze(2).to_broadcast([P, 16, P])).then_inc(a_ready, 1)
            dve.wait_ge(evac, 6)
            step(V.tensor_tensor(cx[:, :, 2:], sc[:, 2:4, :], sc[:, 4:6, :], ALU.mult))
            step.wait()
            for k in range(3):
                for b in range(2):
                    w = c_("sc_w", 3 * b + k, 3 * b + k + 1)
                    if k == 0:
                        step(V.tensor_scalar(ya[:, b, :], cx[:, b, 0:T], w, None, ALU.mult))
                    else:
                        step.wait(1)
                        step(V.scalar_tensor_tensor(out=ya[:, b, :], in0=cx[:, b, k:k + T], scalar=w,
                                                    in1=ya[:, b, :], op0=ALU.mult, op1=ALU.add))
            step.wait()
            V.tensor_tensor(ya, ya, sc[:, 0:2, :], ALU.mult).then_inc(ya_ready, 1)
            mod_units(8, 12)
            z4 = ps[:, B3:B3 + 4, 0:384]
            dve.wait_ge(sb_log, 1)
            for h in range(4):
                step(V.scalar_tensor_tensor(out=sbl[:, h, :], in0=ps[:, B3 + h, 0:384], scalar=0.0,
                                            in1=sbl[:, h, :], op0=ALU.max, op1=ALU.add))
            step.wait()
            dve.wait_ge(late_in, 16)
            V.tensor_tensor(sbl, sbl, c_("sb_keep").unsqueeze(1).to_broadcast([P, 4, 384]), ALU.mult)\
                .then_inc(sb_lk, 1)
            mod_units(12, 14)
            dve.wait_ge(sb_sum, 1)
            V.tensor_tensor(sba, z4, c_("sb_bias").unsqueeze(1).to_broadcast([P, 4, 384]), ALU.add)\
                .then_inc(sb_arg, 1)
            dve.wait_ge(acs_col_mm, 1)
            V.tensor_copy(dtb[:, 176:192], ps[:, BX, 0:16]).then_inc(acs_read, 1)
            mod_units(14, 16)
            dve.wait_ge(acs_mm, 1)
            dve.wait_ge(acs_read, 1)
            for h in range(8):
                col = ps[:, B3 + h // 2, (h % 2) * T:(h % 2) * T + T]
                V.scalar_tensor_tensor(out=decay[:, h, 0:T], in0=col, scalar=dtb[:, 176 + h:177 + h],
                                       in1=c_("ssm_bias", 0, T), op0=ALU.subtract, op1=ALU.add).then_inc(dec_arg, 1)
                V.scalar_tensor_tensor(out=decay[:, h, T:384], in0=col[:, P:T], scalar=dtb[:, 184 + h:185 + h],
                                       in1=c_("ssm_bias", T, 384), op0=ALU.subtract, op1=ALU.add)\
                    .then_inc(dec_arg, 1)
            dve.wait_ge(bc_mm, 1)
            for h in range(8):
                if h % 4 == 0:
                    dve.wait_ge(dec_exp, h // 4 + 1)
                for t, (lo, hi) in enumerate(((0, T), (T, 384))):
                    V.scalar_tensor_tensor(out=decay[:, h, lo:hi], in0=decay[:, h, lo:hi],
                                           scalar=dt[:, 8 * t + h:8 * t + h + 1], in1=ps[:, B3 + h // 4, lo:hi],
                                           op0=ALU.mult, op1=ALU.mult).then_inc(w_ready, 1)
            mod_units(16, 18)
            dve.wait_ge(y_mm, 1)
            for b in range(4):
                step(V.scalar_tensor_tensor(out=yc[:, b, :], in0=xbc[:, b, :], scalar=c_("ssm_d", b, b + 1),
                                            in1=ps[:, B3 + 2 + b // 2, (b % 2) * T:(b % 2) * T + T],
                                            op0=ALU.mult, op1=ALU.add))
            step.wait()
            step(V.tensor_tensor(yc, yc, zg, ALU.mult))
            step.wait()
            V.tensor_tensor(ysq, yc, yc, ALU.mult).then_inc(ysq_ready, 1)
            mod_units(18, 20)
            dve.wait_ge(ysum_mm, 1)
            V.tensor_scalar(ysq[:, 0:2, :], ps[:, BX, :].rearrange("p (b t) -> p b t", b=2), 1.0 / (2 * P), EPS, ALU.mult,
                            ALU.add).then_inc(yms, 1)
            dve.wait_ge(yroot, 1)
            step(V.reciprocal(ysq[:, 0:2, :], ysq[:, 0:2, :]))
            step.wait()
            for b in range(4):
                ins = V.scalar_tensor_tensor(out=yc[:, b, :], in0=yc[:, b, :], scalar=c_("ssm_norm", b, b + 1),
                                             in1=ysq[:, b // 2, :], op0=ALU.mult, op1=ALU.mult)
                if b < 3:
                    step(ins)
            step.wait()
            ins.then_inc(yc_ready, 1)
            modulation(8, 20)
            step(V.tensor_tensor(modT[:, 16:24], modT[:, 16:24], c_("g_post_mix"), ALU.mult))
            step.wait()
            spread(0, modT[:, 16:24])
            step(V.scalar_tensor_tensor(out=cols[:, 16:24], in0=modT[:, 32:40], scalar=1.0, in1=c_("g_pre_ffn"),
                                        op0=ALU.add, op1=ALU.mult))
            V.tensor_copy(cols[:, 24:32], modT[:, 24:32]).then_inc(col_ready, 2)
            for j in range(4):
                dve.wait_ge(unit_done, DONE("br", j))
                if j == 0:
                    dve.wait_ge(evac, 23)
                banks = (3, 4, 5) if j % 2 == 0 else (6, 7, 0)
                pr = prod[3 * (j % 2):3 * (j % 2) + 3]
                for n in range(3):
                    step(V.tensor_tensor(pr[n], ps[:, banks[n], :].rearrange("p (b t) -> p b t", b=2),
                                         gates[:, 8 * n + 2 * j:8 * n + 2 * j + 2, :], ALU.mult))
                step.wait()
                step(V.tensor_tensor(pr[0], pr[0], pr[1], ALU.add))
                step.wait()
                V.tensor_tensor(mT[:, 2 * j:2 * j + 2, :], pr[0], pr[2], ALU.add).then_inc(merged, 1)
            mod_units(20, 24)
            split_lo(SPLIT0)
            split_lo(SPLIT0 + 1)
            residual(0, rstd(1, 2), 2)
            dve.wait_ge(res_done, 2)
            normalise(1, rstd(2, 1))
            hT_part(1)

            def hidden(f, i=0):
                dve.wait_ge(silu_done, i * 2 + (f + 1))
                up = ps[:, f, T:2 * T]
                V.tensor_tensor(hid[:, f, :], sg[:, f, :], up, ALU.mult).then_inc(hid_step, 1)
                V.tensor_tensor(hid_h[:, f, :], sg[:, f, :], up, ALU.mult).then_inc(hid_step, 1)
                dve.wait_ge(hid_step, i * 4 + (2 * f + 2))
                V.tensor_tensor(hid_l[:, f, :], hid[:, f, :], hid_h[:, f, :].bitcast(F32), ALU.subtract)\
                    .then_inc(hid_ready, 1)

            split_lo(SPLIT0 + 2)
            hidden(0)
            mod_units(24, 26)
            hidden(1)
            split_lo(SPLIT0 + 3)
            split_lo(SPLIT0 + 4)
            mod_units(26, 28)
            with dve.Fori(1, PAIRS) as i:
                split_lo(SPLIT0 + 5 - 3, i)
                dve.wait_ge(unit_done, 3 * i + (AT["dn", 0] - 3 + 1))
                hidden(0, i)
                dve.wait_ge(mod_used, 2 * i + 26)
                for n in range(2):
                    dve.wait_ge(mod_in[n], 16 * i + (mod_arrived(26)[1]))
                own = [0]
                for ins in mod_products([mod_place(26), mod_place(27)], sum_place(26), cols[:, 56:64],
                                        lambda n: dve.wait_ge(mod_step, 14 * i + (own[0] - n - 14))):
                    ins.then_inc(mod_step, 1)
                    own[0] += 1
                hidden(1, i)
                split_lo(SPLIT0 + 6 - 3, i)
                split_lo(SPLIT0 + 7 - 3, i)
            modulation(20, 48)
            step(V.tensor_tensor(modT[:, 40:48], modT[:, 40:48], c_("g_post_ffn"), ALU.mult))
            step(V.scalar_tensor_tensor(out=cols[:, 32:40], in0=modT[:, 56:64], scalar=1.0, in1=c_("norm1"),
                                        op0=ALU.add, op1=ALU.mult))
            step.wait()
            V.tensor_copy(cols[:, 40:48], modT[:, 48:56]).then_inc(col_ready, 1)
            spread(1, modT[:, 40:48])
            residual(1, rstd(3, 2), 4)
            dve.wait_ge(res_done, 4)
            normalise(2, rstd(4, 1))
            spread(2, modT[:, 64:72])
            hT_part(2)
            for u in range(AT["qk2", 2], SPLIT0 + SPLITS):
                split_lo(u)
            V.scalar_tensor_tensor(out=modT[:, 80:88], in0=modT[:, 80:88], scalar=1.0, in1=c_("norm2"),
                                   op0=ALU.add, op1=ALU.mult).then_inc(col_ready, 2)
            dve.wait_ge(col_ready, 6)
            V.tensor_copy(cols[:, 48:56], modT[:, 80:88]).then_inc(col_ready, 1)
            V.tensor_copy(cols[:, 56:64], modT[:, 72:80]).then_inc(col_ready, 1)

            for b in range(2):
                dve.wait_ge(at_s, b + 1)
                if b:
                    dve.wait_ge(at_exp, 8)
                for n in range(4):
                    slope = 2.0 ** (-(4 * b + n + 1))
                    ins = V.scalar_tensor_tensor(out=pexp[:, n, :], in0=c_("dist"), scalar=-8.0 * slope,
                                                 in1=ps[:, B3 + n, 0:384], op0=ALU.mult, op1=ALU.add)
                    if n < 3:
                        step(ins)
                ins.then_inc(at_read, 1)
                step.wait()
                dve.wait_ge(at_read, b + 1)
                mx = stat[:, 0:8]
                step(V.tensor_reduce(stat[:, 8:12], pexp[:, :, 0:P], X, ALU.max))
                step(V.tensor_reduce(stat[:, 12:16], pexp[:, :, P:384], X, ALU.max))
                step.wait()
                V.tensor_scalar(mx, stat[:, 8:16], -0.125, None, ALU.mult).then_inc(at_max, 1)
                dve.wait_ge(at_exp, 8 * b + 8)
                if b:
                    dve.wait_ge(at_T, b)
                step(V.tensor_tensor(pnrm, pnrm, c_("count").unsqueeze(1).to_broadcast([P, 4, 384]), ALU.mult))
                step.wait()
                for t, (lo, hi) in enumerate(((0, P), (P, 384))):
                    step(V.tensor_reduce(stat[:, 16 + 4 * t:20 + 4 * t], pnrm[:, :, lo:hi], X, ALU.add))
                step.wait()
                step(V.reciprocal(stat[:, 16:24], stat[:, 16:24]))
                step.wait()
                for t, (lo, hi) in enumerate(((0, P), (P, 384))):
                    ins = V.tensor_tensor(pnrm[:, :, lo:hi], pnrm[:, :, lo:hi],
                                          stat[:, 16 + 4 * t:20 + 4 * t].unsqueeze(2).to_broadcast([P, 4, hi - lo]),
                                          ALU.mult)
                    if t == 0:
                        step(ins)
                step.wait()
                ins.then_inc(at_p, 1)
            dve.wait_ge(col_ready, 6)
            spread(3, modT[:, 80:88])
            spread(4, modT[:, 72:80])
            dve.wait_ge(unit_done, DONE("wo2", 2))
            residual(2, None, 6)
            dve.wait_ge(res_done, 6)
            spread(5, modT[:, 88:96])
            normalise(3, rstd(5, 1))
            hT_part(3)

            n_step = [0]

            def own(ins):
                ins.then_inc(route_step, 1)
                n_step[0] += 1

            def top16(h, values, spare, out_v, out_i):
                lists = range(len(values))
                for q in lists:
                    own(V.max(out_v[q][:, 0:8], values[q]))
                settled(h)
                carry()
                for q in lists:
                    own(V.max_index(out_i[q][:, 0:8], out_v[q][:, 0:8], values[q]))
                for q in lists:
                    own(V.match_replace(spare[q], out_v[q][:, 0:8], values[q], -3e38))
                settled(h)
                carry()
                for q in lists:
                    own(V.max(out_v[q][:, 8:16], spare[q]))
                settled(h)
                carry()
                for q in lists:
                    own(V.max_index(out_i[q][:, 8:16], out_v[q][:, 8:16], spare[q]))
                settled(h)

            def settled(h):
                if isinstance(h, int):
                    dve.wait_ge(route_step, n_step[0])
                else:
                    dve.wait_ge(route_step, (h - 1) * ROUTE_STEPS + (ROUTE_STEPS_0 + n_step[0]))

            def carry():
                dve.sem_inc(dve_go, 1)

            def route_keys(h, t0=0, t1=NT):
                if t0 == 0:
                    n_step[0] = 0
                    dve.wait_ge(s_ready, h + 1)
                carry()
                sc4 = score.rearrange("p (q n) -> p q n", q=4)
                lists = range(2 * t0, 2 * t1)
                top16(h, [sc4[:, q, :] for q in lists], [rest[:, q, :] for q in lists],
                      [sv[:, q, :] for q in lists], [si[:, q, :] for q in lists])
                ins = V.tensor_copy(sif[:, 2 * t0:2 * t1, :], si[:, 2 * t0:2 * t1, :])
                if t1 == NT:
                    ins.then_inc(top_done, 1)
                else:
                    own(ins)
                sv4 = sv.rearrange("p (t s) k -> p t s k", s=2)[:, t0:t1]
                own(V.tensor_tensor(cand[:, t0:t1, :].rearrange("p t (i j) -> p t i j", i=TOPK),
                                    sv4[:, :, 0, :].unsqueeze(3).to_broadcast([P, t1 - t0, TOPK, TOPK]),
                                    sv4[:, :, 1, :].unsqueeze(2).to_broadcast([P, t1 - t0, TOPK, TOPK]), ALU.add))
                settled(h)

            def route_pairs(h, t0=0, t1=NT):
                tiles, n, part = range(t0, t1), (t1 - t0) * TOPK, slice(TOPK * t0, TOPK * t1)
                carry()
                top16(h, [cand[:, t, :] for t in tiles], [cand_rest[:, t, :] for t in tiles],
                      [tv[:, t, :] for t in tiles], [ti[:, TOPK * t:TOPK * (t + 1)] for t in tiles])
                halves = ((ALU.logical_shift_right, 4), (ALU.bitwise_and, 15))
                for p, (op, by) in enumerate(halves):
                    own(V.tensor_scalar(tr[p][:, part], ti[:, part], by, None, op))
                settled(h)
                for p in range(2):
                    own(V.tensor_copy(pos_f[p][:, part], tr[p][:, part]))
                settled(h)
                for p in range(2):
                    own(V.tensor_tensor(onehot[p][:, part, :],
                                        pos_f[p][:, part].unsqueeze(2).to_broadcast([P, n, TOPK]),
                                        c_("iota").unsqueeze(1).to_broadcast([P, n, TOPK]), ALU.is_equal))
                settled(h)
                for p in range(2):
                    oh4 = onehot[p][:, part, :].rearrange("p (t k) j -> p t k j", t=t1 - t0)
                    keys = sif.rearrange("p (t s) k -> p t s k", s=2)[:, t0:t1, p, :]
                    own(V.tensor_tensor(oh4, oh4, keys.unsqueeze(2).to_broadcast([P, t1 - t0, TOPK, TOPK]), ALU.mult))
                settled(h)
                for p in range(2):
                    own(V.tensor_reduce(pick[p][:, part], onehot[p][:, part, :], X, ALU.add))
                settled(h)
                at = bass.ds(NT * TOPK * h + TOPK * t0, n) if t0 == 0 else slice(TOPK * t0, TOPK * t1)
                V.scalar_tensor_tensor(out=idx[:, at], in0=pick[0][:, part], scalar=float(P), in1=pick[1][:, part],
                                       op0=ALU.mult, op1=ALU.add).then_inc(idx_ready, t1 - t0)
                dve.wait_ge(idx_ready, h * NT + t1)

            def less_maximum(h):
                V.tensor_tensor(gate_h, tv, tv[:, :, 0:1].to_broadcast([P, NT, TOPK]), ALU.subtract)\
                    .then_inc(top_v, 1)
                dve.wait_ge(top_v, h + 1)

            def dot_products(h):
                for t in range(NT):
                    for r in range(ROWS):
                        dve.wait_ge(row_in[r], h * (16 * 2 * NT) + 16 * (t + 1))
                        V.tensor_tensor_reduce(row[r], row[r], xn[:, t, :], 1.0, 0.0, ALU.mult, ALU.add,
                                               now[:, t, r:r + 1]).then_inc(row_used, 1)

            def weights(h):
                z = stat[:, 0:NT]
                dve.wait_ge(top_exp, h + 1)
                V.tensor_reduce(z, gate_h, X, ALU.add).then_inc(weigh_step, 1)
                dve.wait_ge(weigh_step, h * 3 + 1)
                V.reciprocal(z, z).then_inc(weigh_step, 1)
                dve.wait_ge(weigh_step, h * 3 + 2)
                V.tensor_tensor(gate_h, gate_h, z.unsqueeze(2).to_broadcast([P, NT, TOPK]), ALU.mult)\
                    .then_inc(weigh_step, 1)
                dve.wait_ge(weigh_step, h * 3 + 3)
                dve.wait_ge(gelu_done, h + 1)
                V.tensor_tensor(weight, gate_h, now, ALU.mult).then_inc(weight_ready, 1)
                dve.wait_ge(weight_ready, h + 1)

            def weighted_sums(h, between):
                for t in range(NT):
                    if t:
                        between()
                    for r in range(ROWS):
                        dve.wait_ge(row_in[r], h * (16 * 2 * NT) + 16 * (NT + t + 1))
                        dve.wait_ge(row_used, h * (2 * NT * ROWS) + (ROWS * (NT + t + 1) + r - 1))
                        y = (y_acc, y_alt)[r % 2][t]
                        V.scalar_tensor_tensor(out=y, in0=row[r], scalar=weight[:, t, r:r + 1], in1=y,
                                               op0=ALU.mult, op1=ALU.add).then_inc(row_used, 1)
                dve.wait_ge(row_used, h * (2 * NT * ROWS) + ROWS * (2 * NT + 1))

            for y in y_acc + y_alt:
                step(V.memset(y, 0.0))
            step.wait()
            dve.sem_inc(row_used, ROWS)
            for t in range(NT):
                route_keys(0, t, t + 1)
                route_pairs(0, t, t + 1)
            less_maximum(0)
            dve.wait_ge(row_ready, 10)
            dve.wait_ge(x_T, 4 * KC // 2)
            for y, op in ((scale_row, ALU.mult), (shift_row, ALU.add)):
                for t in range(NT):
                    step(V.tensor_tensor(xn[:, t, :], xn[:, t, :], y, op))
                step.wait()
            with dve.Fori(0, HEADS - 1) as i:
                dot_products(i)
                route_keys(i + 1)
                weights(i)
                weighted_sums(i, lambda: route_pairs(i + 1))
                less_maximum(i + 1)
            dot_products(HEADS - 1)
            weights(HEADS - 1)

            def last_residual(t):
                if t == 0:
                    dve.wait_ge(row_ready, 12)
                    dve.wait_ge(row_used, ROWS * (2 * NT * HEADS))
                step(V.tensor_tensor(y_acc[t], y_acc[t], y_alt[t], ALU.add))
                step.wait()
                step(V.tensor_tensor(y_acc[t], y_acc[t], gate_row[:, :], ALU.mult))
                step.wait()
                V.tensor_tensor(x_sb[:, t, :], x_sb[:, t, :], y_acc[t], ALU.add).then_inc(res_done, 1)

            def last_norm(t):
                dve.wait_ge(sq_sum, 17 + t)
                dve.wait_ge(res_done, 7 + t)
                V.tensor_scalar(stat[:, 60 + t:61 + t], stat[:, 16 + t:17 + t], 1.0 / D, EPS, ALU.mult, ALU.add)\
                    .then_inc(mean_sq, 1)
                dve.wait_ge(root, 7 + t)
                r = stat[:, 44 + t:45 + t]
                step(V.reciprocal(r, r))
                step.wait()
                V.scalar_tensor_tensor(out=xn[:, t, :], in0=x_sb[:, t, :], scalar=r, in1=final_row,
                                       op0=ALU.mult, op1=ALU.mult).then_inc(out_ready, 1)

            weighted_sums(HEADS - 1, lambda: last_residual(0))
            last_residual(1)
            dve.wait_ge(final_in, 16)
            for t in range(NT):
                last_norm(t)


def _cols(v):
    return np.asarray(v).reshape(-1, P).T


def _t_units(w):
    w = w.reshape(KC, P, -1, 2, P).transpose(2, 1, 3, 0, 4)
    return w.reshape(w.shape[0], P, UNIT)


def _m_units(w):
    n = w.shape[1] // 512
    return w.reshape(2, 4, P, n, 512).transpose(3, 0, 2, 1, 4).reshape(2 * n, P, UNIT)


def _pair_blocks(w):
    k = w.shape[0] // P
    return w.reshape(k, P, KC // 2, 2, P).transpose(2, 1, 3, 0, 4).reshape(KC // 2, P, -1)


def _mod_units(w):
    return w.reshape(KC, P, -1, T).transpose(2, 1, 0, 3).reshape(-1, P, UNIT)


def _constants():
    p, c = np.arange(P)[:, None], np.arange(P)[None, :]
    key, wide = np.arange(P)[:, None], np.arange(T)[None, :]
    strict = np.concatenate([key < wide, key < np.arange(P)[None, :]], 1)
    loose = np.concatenate([key <= wide, key <= np.arange(P)[None, :]], 1)
    dist = np.concatenate([p - c, P + p - wide], 1)
    count = np.zeros(dist.shape)
    for w, d in ((128, 1), (512, 4), (2048, 16)):
        count += (dist >= 0) & (dist <= w) & (dist % d == 0)
    band = np.zeros((P, NT, 4, T))
    t = np.arange(T)
    for g, w in enumerate((2, 4, 8, 16)):
        for n in range(NT):
            s = n * P + np.arange(P)[:, None]
            band[:, n, g, :] = ((s <= t) & (s > t - w)) / np.minimum(t + 1.0, w) - (s == t)
    return {
        "ident": p == c, "tri": p <= c, "ones": np.ones((P, P)), "suffix": p >= c,
        "sb_keep": np.where(strict, -1.0, 0.0), "sb_bias": np.where(strict, 0.0, NEG),
        "ssm_bias": np.where(loose, 0.0, NEG), "dist": np.where(dist >= 0, dist, -NEG), "count": count,
        "iota": np.broadcast_to(np.arange(TOPK), (P, TOPK)),
    }, band.reshape(P, -1)


def kernel(**inputs):
    import concourse.bacc as bacc
    from concourse.bass_utils import run_bass_kernel_spmd

    f = {k: np.asarray(v) for k, v in inputs.items()}
    for name in ("mod_w", "mod_b", "g_pre_mix", "g_post_mix", "g_pre_ffn", "g_post_ffn", "w_in", "sc_conv_w",
                 "ssm_conv_w", "ssm_conv_b", "ssm_dt_bias", "ssm_a_log", "ssm_d", "ssm_norm_w", "w_sc_out",
                 "w_sb_out", "w_ssm_out", "w_o", "w_ffn_in", "w_ffn_out", "w_ada_2", "b_ada_2", "norm1_g_2",
                 "w_in_2", "pool_w_2", "pool_scale_2", "w_out_2", "norm2_g_2", "peer_wq_2", "peer_subkeys_2",
                 "peer_u_2", "peer_v_2"):
        f[name] = f[name][0]
    w_in = f["w_in"]
    at = np.cumsum([0, 768, 256, 256, 256, 512, 768, 8, 3072])
    part = {n: w_in[:, at[i]:at[i + 1]] for i, n in enumerate(("sc", "q", "k", "v", "z", "xbc", "dt", "gl"))}
    hidden = FB * P
    gu = f["w_ffn_in"].reshape(KC, P, 2, FB, P).transpose(3, 1, 2, 0, 4).reshape(FB, P, UNIT)
    w2 = f["w_in_2"]
    kinds = {
        "xbc": _t_units(part["xbc"]), "sc": _t_units(part["sc"]),
        "qk": np.concatenate([_t_units(part["q"]), _t_units(part["k"])]),
        "v": part["v"].reshape(KC, P, T).transpose(1, 0, 2).reshape(1, P, UNIT),
        "z": _t_units(part["z"]), "gl": _t_units(part["gl"]),
        "br": np.concatenate([_pair_blocks(f[n]) for n in ("w_sc_out", "w_sb_out", "w_ssm_out")], 2),
        "wo": _m_units(f["w_o"]), "gu": gu,
        "dn": f["w_ffn_out"].reshape(PAIRS, 2, P, D).transpose(0, 2, 1, 3).reshape(PAIRS, P, UNIT),
        "qk2": _t_units(w2[:, 0:1024]), "v2": _m_units(w2[:, 1024:1536]), "u2": _m_units(w2[:, 1536:2048]),
        "wo2": _m_units(f["w_out_2"]), "wq": _t_units(f["peer_wq_2"]),
    }
    assert hidden == f["w_ffn_out"].shape[0]
    stream = np.stack([kinds[kind][j] for kind, j in ORDER])
    consts, band = _constants()
    pieces = {
        "c": _cols(f["c"]), "c2": _cols(f["c_2"]),
        "mod_b": np.concatenate([_cols(f["mod_b"]), _cols(f["b_ada_2"])], 1),
        "g_pre_mix": _cols(f["g_pre_mix"]), "g_pre_ffn": _cols(f["g_pre_ffn"]),
        "g_post_mix": _cols(f["g_post_mix"]), "g_post_ffn": _cols(f["g_post_ffn"]),
        "norm1": _cols(f["norm1_g_2"]), "norm2": _cols(f["norm2_g_2"]), "ssm_b": _cols(f["ssm_conv_b"]),
        "ssm_w": f["ssm_conv_w"].reshape(4, 6, P).transpose(2, 1, 0).reshape(P, 24),
        "sc_w": f["sc_conv_w"].reshape(3, 2, P).transpose(2, 1, 0).reshape(P, 6),
        "ssm_norm": _cols(f["ssm_norm_w"]), "pool_scale": _cols(f["pool_scale_2"]),
        "ssm_d": _cols(np.repeat(f["ssm_d"], 64)),
        "dt_b": np.broadcast_to(f["ssm_dt_bias"], (P, 8)), "a_log": np.broadcast_to(f["ssm_a_log"], (P, 8)),
        "w_dt": part["dt"].reshape(KC, P, 8).transpose(1, 0, 2).reshape(P, 64),
        "pool_w": f["pool_w_2"].transpose(1, 0, 2).reshape(P, 512),
        "keys": f["peer_subkeys_2"].transpose(2, 0, 1).reshape(P, 256),
        **consts,
    }
    small = np.concatenate([np.asarray(pieces[n], dtype=np.float32) for n in SMALL], 1)
    arrays = {
        "stream": stream, "mod_w": np.concatenate([_mod_units(f["mod_w"]), _mod_units(f["w_ada_2"])]),
        "small": small,
        "x": np.ascontiguousarray(f["x"].reshape(NT, P, D).transpose(1, 0, 2)),
        "band": band.astype(np.float32), "final_g": np.ascontiguousarray(np.broadcast_to(f["final_g_2"], (P, D))),
        "expert_u": f["peer_u_2"], "expert_v": f["peer_v_2"],
    }
    nc = bacc.Bacc("TRN2", target_bir_lowering=False, num_devices=1)
    args = [nc.dram_tensor(f"in_{n}", a.shape, mybir.dt.from_np(a.dtype), kind="ExternalInput").ap()
            for n, a in arrays.items()]
    out = nc.dram_tensor("out", (T, D), F32, kind="ExternalOutput").ap()
    build(nc, *args, out)
    r = run_bass_kernel_spmd(nc, [{f"in_{n}": a for n, a in arrays.items()}], core_ids=[0])
    return r.results[0]["out"].reshape(1, T, D)
```
